# Optimizing a Trainium2 kernel written in Bass

```python
import math
import jax, jax.numpy as jnp
from jax import lax
import numpy as np

D_MODEL = 1024
BATCH = 1
SEQ = 512
DEPTH = 2
DEC_BATCH = 8
DEC_SEQ = 8
PAST_LEN = 4096
PAGE_SIZE = 128

CONV_WIDTH = 512
CONV_K = 3
RET_HEADS = 4
RET_DK = 128
RET_DV = 256
RET_QK_WIDTH = RET_HEADS * RET_DK
RET_V_WIDTH = RET_HEADS * RET_DV
RET_CHUNK = 128
MEM_LEN = 256
MEM_HEADS = 4
MEM_HEAD_DIM = 128
MEM_WIDTH = MEM_HEADS * MEM_HEAD_DIM
N_BRANCH = 3
D_FF = 4 * D_MODEL
ROPE_BASE = 10000.0
LN_EPS = 1e-5
GN_EPS = 1e-6
DEEPNORM_ALPHA = (2 * DEPTH) ** 0.25
DEEPNORM_BETA = (8 * DEPTH) ** -0.25
SPLITS = (CONV_WIDTH, CONV_WIDTH, CONV_WIDTH, RET_QK_WIDTH, RET_QK_WIDTH,
          RET_V_WIDTH, RET_V_WIDTH, MEM_WIDTH, N_BRANCH * D_MODEL)
IN_WIDTH = sum(SPLITS)

kernel_name = "hybrid_conv_retention_memory_deepnorm_step"

def layer_norm(x, g, b):
    xf = x.astype(jnp.float32)
    mu = xf.mean(-1, keepdims=True)
    var = jnp.square(xf - mu).mean(-1, keepdims=True)
    y = (xf - mu) * lax.rsqrt(var + LN_EPS) * g.astype(jnp.float32) + b.astype(jnp.float32)
    return y.astype(x.dtype)

def rotary(x, pos):
    half = x.shape[-1] // 2
    inv = ROPE_BASE ** (-jnp.arange(half, dtype=jnp.float32) / half)
    ang = pos.astype(jnp.float32)[:, None] * inv[None, :]
    cos = jnp.cos(ang)[None, :, None, :]
    sin = jnp.sin(ang)[None, :, None, :]
    xf = x.astype(jnp.float32)
    x1, x2 = xf[..., :half], xf[..., half:]
    return jnp.concatenate([x1 * cos - x2 * sin, x1 * sin + x2 * cos], axis=-1)

def short_conv(u, buf, w):
    t = u.shape[1]
    full = jnp.concatenate([buf.astype(u.dtype), u], axis=1)
    y = full[:, 0:t] * w[0]
    for j in range(1, CONV_K):
        y = y + full[:, j:j + t] * w[j]
    return y, full[:, -(CONV_K - 1):]

def retention(q, k, v, s0):
    b, t, h, _ = q.shape
    c = RET_CHUNK if t % RET_CHUNK == 0 else t
    n = t // c
    log_g = jnp.log1p(-jnp.exp2(-5.0 - jnp.arange(h, dtype=jnp.float32)))
    idx = jnp.arange(c, dtype=jnp.float32)
    rel = idx[:, None] - idx[None, :]
    causal = rel >= 0
    dmask = jnp.where(causal[None], jnp.exp(jnp.where(causal, rel, 0.0)[None] * log_g[:, None, None]), 0.0)
    q_decay = jnp.exp((idx + 1.0)[None, :] * log_g[:, None])
    k_decay = jnp.exp((c - 1.0 - idx)[None, :] * log_g[:, None])
    chunk_decay = jnp.exp(c * log_g)

    def to_chunks(a):
        return a.reshape(b, n, c, h, a.shape[-1]).transpose(1, 0, 3, 2, 4)

    def step(s, inp):
        qi, ki, vi = inp
        scores = jnp.einsum('bhid,bhjd->bhij', qi, ki) * dmask[None]
        o = (jnp.einsum('bhij,bhje->bhie', scores, vi)
             + jnp.einsum('bhid,bhde->bhie', qi, s) * q_decay[None, :, :, None])
        s = (s * chunk_decay[None, :, None, None]
             + jnp.einsum('bhjd,bhje->bhde', ki * k_decay[None, :, :, None], vi))
        return s, o

    s_final, o = lax.scan(step, s0, (to_chunks(q), to_chunks(k), to_chunks(v)))
    o = o.transpose(1, 0, 3, 2, 4).reshape(b, t, h, v.shape[-1])
    return o, s_final

def mem_kv(mem, w_mem_kv_l):
    b, m, _ = mem.shape
    kv = mem @ w_mem_kv_l
    k, v = jnp.split(kv, 2, axis=-1)
    return (k.reshape(b, m, MEM_HEADS, MEM_HEAD_DIM), v.reshape(b, m, MEM_HEADS, MEM_HEAD_DIM))

def mem_attention(q, mk, mv):
    s = jnp.einsum('bthd,bmhd->bhtm', q, mk).astype(jnp.float32) * (MEM_HEAD_DIM ** -0.5)
    p = jax.nn.softmax(s, axis=-1).astype(mv.dtype)
    return jnp.einsum('bhtm,bmhd->bthd', p, mv)

def trunk_layer(x, pos, conv_buf, ret_state, mk, mv, w_in, b_gate, conv_w, ret_gn_g,
                w_conv_out, w_ret_out, w_mem_out, w_out, ln1_g, ln1_b, w_up, w_down, ln2_g, ln2_b):
    b, t, _ = x.shape
    split_idx = np.cumsum(np.array(SPLITS))[:-1].tolist()
    proj = x @ w_in
    cb, cc, ch, rq, rk, rv, rg, mq, gl = jnp.split(proj, split_idx, axis=-1)
    conv_y, new_buf = short_conv(cc * ch, conv_buf, conv_w)
    a_out = (cb * conv_y) @ w_conv_out
    q = rotary(rq.reshape(b, t, RET_HEADS, RET_DK), pos)
    k = rotary(rk.reshape(b, t, RET_HEADS, RET_DK), pos) * (RET_DK ** -0.5)
    v = rv.reshape(b, t, RET_HEADS, RET_DV).astype(jnp.float32)
    o, new_state = retention(q, k, v, ret_state.astype(jnp.float32))
    mu = o.mean(-1, keepdims=True)
    var = jnp.square(o - mu).mean(-1, keepdims=True)
    o = ((o - mu) * lax.rsqrt(var + GN_EPS)).reshape(b, t, RET_V_WIDTH) * ret_gn_g.astype(jnp.float32)
    b_out = (jax.nn.silu(rg.astype(jnp.float32)) * o).astype(x.dtype) @ w_ret_out
    m_out = mem_attention(mq.reshape(b, t, MEM_HEADS, MEM_HEAD_DIM), mk, mv).reshape(b, t, MEM_WIDTH) @ w_mem_out
    g = jax.nn.sigmoid((gl + b_gate).astype(jnp.float32)).astype(x.dtype).reshape(b, t, N_BRANCH, D_MODEL)
    merged = g[:, :, 0] * a_out + g[:, :, 1] * b_out + g[:, :, 2] * m_out
    x = layer_norm(DEEPNORM_ALPHA * x + merged @ w_out, ln1_g, ln1_b)
    hdn = jnp.square(jax.nn.relu(x @ w_up))
    x = layer_norm(DEEPNORM_ALPHA * x + hdn @ w_down, ln2_g, ln2_b)
    return x, new_buf, new_state.astype(ret_state.dtype)

def setup_inputs(seed: int = 0) -> dict:
    key = jax.random.key(seed)
    ks = jax.random.split(key, 24)
    f32 = jnp.float32
    nrm = lambda k, shape, scale: jax.random.normal(k, shape, f32) * scale
    return {
        "x_prompt": nrm(ks[0], (BATCH, SEQ, D_MODEL), 1.0),
        "x_sample": nrm(ks[1], (DEC_BATCH, DEC_SEQ, D_MODEL), 1.0),
        "cache_mem_k": nrm(ks[2], (DEPTH, DEC_BATCH, MEM_LEN, MEM_HEADS, MEM_HEAD_DIM), 1.0),
        "cache_mem_v": nrm(ks[3], (DEPTH, DEC_BATCH, MEM_LEN, MEM_HEADS, MEM_HEAD_DIM), 1.0),
        "state_conv": nrm(ks[4], (DEPTH, DEC_BATCH, CONV_K - 1, CONV_WIDTH), 1.0),
        "state_ret": nrm(ks[5], (DEPTH, DEC_BATCH, RET_HEADS, RET_DK, RET_DV), RET_DK ** -0.5),
        "mem_prompt": nrm(ks[6], (BATCH, MEM_LEN, D_MODEL), 1.0),
        "w_in": nrm(ks[7], (DEPTH, D_MODEL, IN_WIDTH), D_MODEL ** -0.5),
        "b_gate": nrm(ks[8], (DEPTH, N_BRANCH * D_MODEL), 0.02),
        "conv_w": nrm(ks[9], (DEPTH, CONV_K, CONV_WIDTH), CONV_K ** -0.5),
        "ret_gn_g": 1.0 + nrm(ks[10], (DEPTH, RET_V_WIDTH), 0.02),
        "w_conv_out": nrm(ks[11], (DEPTH, CONV_WIDTH, D_MODEL), CONV_WIDTH ** -0.5),
        "w_ret_out": nrm(ks[12], (DEPTH, RET_V_WIDTH, D_MODEL), RET_V_WIDTH ** -0.5),
        "w_mem_out": nrm(ks[13], (DEPTH, MEM_WIDTH, D_MODEL), MEM_WIDTH ** -0.5),
        "w_out": nrm(ks[14], (DEPTH, D_MODEL, D_MODEL), DEEPNORM_BETA * D_MODEL ** -0.5),
        "w_mem_kv": nrm(ks[15], (DEPTH, D_MODEL, 2 * MEM_WIDTH), D_MODEL ** -0.5),
        "ln1_g": 1.0 + nrm(ks[16], (DEPTH, D_MODEL), 0.02),
        "ln1_b": nrm(ks[17], (DEPTH, D_MODEL), 0.02),
        "w_up": nrm(ks[18], (DEPTH, D_MODEL, D_FF), D_MODEL ** -0.5),
        "w_down": nrm(ks[19], (DEPTH, D_FF, D_MODEL), DEEPNORM_BETA * D_FF ** -0.5),
        "ln2_g": 1.0 + nrm(ks[20], (DEPTH, D_MODEL), 0.02),
        "ln2_b": nrm(ks[21], (DEPTH, D_MODEL), 0.02),
    }

def reference(x_prompt, x_sample, cache_mem_k, cache_mem_v, state_conv, state_ret, mem_prompt,
              w_in, b_gate, conv_w, ret_gn_g, w_conv_out, w_ret_out, w_mem_out, w_out, w_mem_kv,
              ln1_g, ln1_b, w_up, w_down, ln2_g, ln2_b):
    pos_p = jnp.arange(x_prompt.shape[1], dtype=jnp.int32)
    pos_s = PAST_LEN + jnp.arange(x_sample.shape[1], dtype=jnp.int32)
    bp = x_prompt.shape[0]
    xp, xs = x_prompt, x_sample
    mk_list, mv_list, cp_list, rp_list, cs_list, rs_list = [], [], [], [], [], []
    for l in range(DEPTH):
        lw = (w_in[l], b_gate[l], conv_w[l], ret_gn_g[l], w_conv_out[l], w_ret_out[l], w_mem_out[l],
              w_out[l], ln1_g[l], ln1_b[l], w_up[l], w_down[l], ln2_g[l], ln2_b[l])
        mk_p, mv_p = mem_kv(mem_prompt, w_mem_kv[l])
        conv0 = jnp.zeros((bp, CONV_K - 1, CONV_WIDTH), xp.dtype)
        ret0 = jnp.zeros((bp, RET_HEADS, RET_DK, RET_DV), state_ret.dtype)
        xp, cbuf_p, rst_p = trunk_layer(xp, pos_p, conv0, ret0, mk_p, mv_p, *lw)
        xs, cbuf_s, rst_s = trunk_layer(xs, pos_s, state_conv[l], state_ret[l],
                                        cache_mem_k[l], cache_mem_v[l], *lw)
        mk_list.append(mk_p)
        mv_list.append(mv_p)
        cp_list.append(cbuf_p)
        rp_list.append(rst_p)
        cs_list.append(cbuf_s)
        rs_list.append(rst_s)
    return (xp, xs, jnp.stack(mk_list), jnp.stack(mv_list), jnp.stack(cp_list),
            jnp.stack(rp_list), jnp.stack(cs_list), jnp.stack(rs_list))


_drawn_inputs = setup_inputs


def setup_inputs(seed=0):
    import zlib

    import numpy as np

    out = dict(_drawn_inputs(seed))
    spreads = {}
    factors = {'b_gate': 8.0, 'ret_gn_g': 8.0}
    for name, (base, spread) in spreads.items():
        noise = np.random.default_rng([zlib.crc32(name.encode()), seed]).standard_normal(out[name].shape)
        drawn = base * np.exp(spread * noise) if base else spread * noise
        out[name] = __import__('jax').numpy.asarray(drawn.astype(out[name].dtype))
    for name, factor in factors.items():
        out[name] = (out[name] * factor).astype(out[name].dtype)
    return out
```

```python
import numpy as np
import concourse.bass as bass
from concourse import mybir

F32 = mybir.dt.float32
F32R = mybir.dt.float32r
ALU = mybir.AluOpType
ACT = mybir.ActivationFunctionType
AX = mybir.AxisListType

DEPTH = 2
D = 1024
SEQ, NB, TS = 512, 8, 8
NS = NB * TS
N = NS + SEQ
HALF = N // 2
P = 128
KT = D // P
CW, H, DK, DV, ML = 512, 4, 128, 256, 256
CHUNK = 128
NCH = SEQ // CHUNK
ALPHA = (2 * DEPTH) ** 0.25
LN_EPS, GN_EPS = 1e-5, 1e-6
ATT_SCALE = P ** -0.5
RET_SCALE = DK ** -0.5
LOG_G = [float(np.log1p(-np.exp2(-5.0 - h))) for h in range(H)]
G_CHUNK = [float(np.exp(CHUNK * g)) for g in LOG_G]
G_TS = [float(np.exp(TS * g)) for g in LOG_G]
PAD = NB * (TS + 2) + SEQ + 2

C_CB, C_CC, C_CH, C_RQ, C_MQ, C_GATE = 0, 512, 1024, 1536, 4608, 5120

T_RQK, T_RV, T_RG, T_RO, T_KV, T_MQ, T_CC, T_CH, T_CB = 0, 8, 16, 24, 40, 48, 52, 56, 60
T_AM, T_WO, T_FF, TILES = 64, 96, 104, 168
RING = 4
PIECE = KT * P

K_COS = 0
K_SIN = K_COS + N
K_DMP = K_SIN + N
K_DMS = K_DMP + H * P
K_QDP = K_DMS + H * NS
K_QDS = K_QDP + H * P
K_KDP = K_QDS + H * NS
K_KDS = K_KDP + H
K_ID = K_KDS + H * NB
K_ONE = K_ID + P
K_ALL = K_ONE + 1

V_BG, V_GN, V_CONV, V_LG1, V_LB1, V_LG2, V_LB2 = 0, 24, 32, 44, 52, 60, 68
V_ALL = 76

SIDE = [[], [], [], []]
for _c in range(NCH):
    SIDE[0] += [("sc", _c), ("kv", _c)]
    SIDE[1] += [("kt", _c), ("kv", _c)]
    SIDE[2] += [("o", _c), ("ot", _c)]
    SIDE[3] += [("o", _c), ("ot", _c)]
SIDE[0] += [("sc", "s")] + [("kvs", _b) for _b in range(NB)]
SIDE[1] += [("kt", "s")] + [("kvs", _b) for _b in range(NB)]
SIDE[2] += [("oT", "s"), ("o", "s"), ("ot", "s")]
SIDE[3] += [("o", "s")]
for _h in range(H):
    for _b in (0, 1):
        SIDE[2 * (_h % 2) + _b] += [("qk", _h), ("pt", _h)] + [("pv", _h)] * (_b == 0)
SIDE[0] += [("qk", "s"), ("pt", "s")]
SIDE[1] += [("pv", "s")]
SIDE[2] += [("sn", "s")]
SIDE[3] += [("sn", "s")]
for _x in range(2):
    SIDE[0] += [("sum", _x)]
    SIDE[1] += [("mean", _x), ("rstd", _x)]
    SIDE[2] += [("mean", _x), ("rstd", _x)]
    SIDE[3] += [("sq", _x)]


def use(l, bank, tag):
    return l * len(SIDE[bank]) + SIDE[bank].index(tag) + 1


def layers(nc, xT, memT, kT_cache, v_cache, conv_state, ret_state, w_in, w_conv_out, w_ret_out,
           w_mem_out, w_out, w_mem_kv, w_up, w_down, vectors, table,
           yT, kT_new, v_new, conv_new, ret_prompt, ret_sample):
    at = [(nc.sbuf_base + 31) // 32 * 32]

    def place(name, shape, dt, offset=None):
        size = 4 * int(np.prod(shape[1:]))
        if offset is None:
            offset, at[0] = at[0], at[0] + (size + 31) // 32 * 32
        return nc.alloc_sbuf_tensor_at(name, shape, dt, offset=offset)

    def here():
        return at[0]

    stage = place("stage", [P, RING, PIECE], F32)
    w_hi = place("w_hi", [P, RING, PIECE], F32R)
    w_lo = place("w_lo", [P, RING, PIECE], F32R)
    x_hi = place("x_hi", [P, KT, N], F32R)
    x_lo = place("x_lo", [P, KT, N], F32R)
    a_bhi = here()
    b_hi = place("b_hi", [P, KT, N], F32R)
    a_blo = here()
    b_lo = place("b_lo", [P, KT, N], F32R)
    rot = place("rot", [P, 2, 2, N], F32, a_bhi)
    sil = place("sil", [P, KT, N], F32, a_blo)
    a_r = here()
    r = place("r", [P, KT, N], F32)
    kn = place("kn", [P, H * P], F32, a_r)
    qd = place("qd", [P, H, P], F32, a_r + 2048)
    sc = place("sc", [P, H, P], F32, a_r + 4096)
    kb1 = place("kb1", [P, H * P], F32, a_r + 6144)
    S = place("S", [P, H, DV], F32, a_r + 8192)
    on = place("on", [P, H, DV], F32, a_r + 12288)
    prod = place("prod", [P, 512], F32, a_r + 16384)
    a_g = here()
    gate = place("gate", [P, 4, N], F32)
    place("gate_rest", [P, 4096 - 4 * N], F32)
    s_in = place("s_in", [P, 4, H, DV], F32, a_g)
    up = place("up", [P, 2, PAD], F32, a_g)
    a_c = here()
    place("C", [P, 11776], F32)

    def c_at(name, shape, dt, first):
        return place(name, shape, dt, a_c + 4 * first)

    qT = c_at("qT", [P, H, N], F32, 0)
    kT = c_at("kT", [P, H, N], F32, 2304)
    v = c_at("v", [P, 5, H * DV], F32, 4608)
    km = c_at("km", [P, H, ML], F32, 9728)
    vm = c_at("vm", [P, 2, CW], F32, 10752)
    mt_hi = c_at("mt_hi", [P, KT, ML], F32R, 0)
    mt_lo = c_at("mt_lo", [P, KT, ML], F32R, 2304)
    mt_raw = c_at("mt_raw", [P, KT, ML], F32, 4608)
    mq = c_at("mq", [P, H, N], F32, 0)
    cc = c_at("cc", [P, H, N], F32, 2304)
    pr = c_at("pr", [P, 2, 4, ML], F32, 4608)
    sT = c_at("sT", [P, 2, H, NS], F32, 4608)
    pT_s = c_at("pT_s", [P, 2, H, NS], F32, 5120)
    pr_s = c_at("pr_s", [P, H, ML], F32, 5632)
    pT = c_at("pT", [P, 2, SEQ], F32, 6656)
    kv_c = c_at("kv_c", [P, 2, 1024], F32, 7680)
    kv_g = place("kv_g", [P, 4, 1024], F32, a_g)
    m_hi = c_at("m_hi", [P, KT, N], F32R, 0)
    m_lo = c_at("m_lo", [P, KT, N], F32R, 4608)
    sq = c_at("sq", [P, KT, N], F32, 0)
    relu = c_at("relu", [P, 2, N], F32, 0)
    racc = c_at("racc", [P, N], F32, 9728)
    row = c_at("row", [P, N], F32, 10304)
    table_sb = place("table_sb", [P, K_ALL], F32)
    vec = place("vec", [P, V_ALL], F32)
    tmp = place("tmp", [P, 2, N], F32)
    hist = place("hist", [P, H, NB, 2], F32)
    tail = place("tail", [P, H, 2 * (NB + 1)], F32)
    mx = place("mx", [P, 2, H], F32)
    nb = place("nb", [P, 2, H], F32)
    rs = place("rs", [P, 2, H], F32)
    ri = place("ri", [P, 2, H], F32)
    bst = place("bst", [P, H, 6], F32)
    mv = place("mv", [P, H, 2], F32)
    ve = place("ve", [P, H], F32)
    sd = place("sd", [P, H], F32)
    rstd = place("rstd", [P, H], F32)
    st = place("st", [P, 4, 5], F32)
    assert at[0] <= nc.sbuf_usable_end, (at[0], nc.sbuf_usable_end)

    ident = table_sb[:, K_ID:K_ID + P]
    ones = table_sb[:, K_ONE:K_ONE + 1]

    def const3(first, a, b, p=P):
        return table_sb[0:p, first:first + a * b].rearrange("p (a b) -> p a b", a=a)

    def vcol(i):
        return vec[:, i:i + 1]

    def kv_slot(i):
        i %= 6
        return kv_c[:, i, :] if i < 2 else kv_g[:, i - 2, :]

    gp = nc.alloc_psum_tensor("gp", [P, 4, 512], F32)
    qb = nc.alloc_psum_tensor("qb", [P, 4, 512], F32)

    def pair(par):
        return gp[:, 2 * par:2 * par + 2, 0:HALF]

    def halves(ap):
        return ap.rearrange("p (a b) -> p a b", a=2)

    sem = nc.alloc_semaphore
    split_done = sem("split_done")
    tile_done = sem("tile_done")
    pair_free = [sem(f"pair_free{i}") for i in range(2)]
    stage_full = [sem(f"stage_full{i}") for i in range(RING)]
    hi_done = sem("hi_done")
    split_begun = sem("split_begun")
    side_full = [sem(f"side_full{i}") for i in range(4)]
    side_free = [sem(f"side_free{i}") for i in range(4)]
    dve_step = sem("dve_step")
    act_step = sem("act_step")
    table_in, x_in, vec_in, hist_in, mem_in = (sem(n) for n in ("table_in", "x_in", "vec_in", "hist_in", "mem_in"))
    s_in_full = [sem(f"s_in_full{i}") for i in range(4)]
    s_out_done = [sem(f"s_out_done{i}") for i in range(4)]
    kv_full = [sem(f"kv_full{i}") for i in range(6)]
    kv_used = sem("kv_used")
    x_ready = sem("x_ready")
    mem_split = sem("mem_split")
    km_ready = sem("km_ready")
    rot_in = sem("rot_in")
    rot_done = sem("rot_done")
    v_ready = sem("v_ready")
    sig_in = sem("sig_in")
    gate_in = sem("gate_in")
    mq_ready = sem("mq_ready")
    cc_in = sem("cc_in")
    z_ready = sem("z_ready")
    knb_ready = sem("knb_ready")
    s_ready = sem("s_ready")
    var_in = sem("var_in")
    std_in = sem("std_in")
    b_ready = sem("b_ready")
    nb_ready = sem("nb_ready")
    p_ready = sem("p_ready")
    m_ready = sem("m_ready")
    sum_ready = sem("sum_ready")
    d_ready = sem("d_ready")
    sq_ready = sem("sq_ready")
    lvar_in, lstd_in, lrs_ready = sem("lvar_in"), sem("lstd_in"), sem("lrs_ready")
    y1_ready = sem("y1_ready")
    xh_in = sem("xh_in")
    r_ready = sem("r_ready")
    relu_in = sem("relu_in")
    hid_ready = sem("hid_ready")
    km_out, st_out, tail_out, y_out = sem("km_out"), sem("st_out"), sem("tail_out"), sem("y_out")

    def filled(eng, l, bank, tag):
        eng.wait_ge(side_full[bank], use(l, bank, tag))

    def drained(eng, l, bank, tag):
        eng.wait_ge(side_free[bank], use(l, bank, tag) + 1)

    def tile_is_done(eng, l, t):
        eng.wait_ge(tile_done, l * TILES + t + 1 + RING)

    block_cm = nc.Block()
    block = block_cm.__enter__()

    @block.sync
    def _(sp):
        def load(l, t, slot, src):
            sp.wait_ge(split_done, l * TILES + t + 1)
            rows = src.shape[0] * src.shape[1] // P
            sp.dma_start(stage[:, slot, 0:rows * P].rearrange("p (k c) -> p k c", k=rows),
                         src.rearrange("l (k p) c -> p (l k) c", p=P)).then_inc(stage_full[slot], 16)

        def four(l, t, w, col, rows=slice(0, D)):
            for i in range(4):
                load(l, t + i, i, w[bass.ds(l, 1), rows, bass.ds(col + i * P, P)])

        with sp.Fori(0, DEPTH) as l:
            with sp.Fori(0, 6) as j:
                four(l, j * 4 + T_RQK, w_in, j * 512 + C_RQ)
            with sp.Fori(0, 2) as j:
                four(l, j * 8 + T_RO, w_in, j * 512 + C_GATE + D)
                four(l, j * 8 + T_RO + 4, w_ret_out, j * 512)
            with sp.Fori(0, 2) as j:
                four(l, j * 4 + T_KV, w_mem_kv, j * 512)
            four(l, T_MQ, w_in, C_MQ)
            four(l, T_CC, w_in, C_CC)
            with sp.Fori(0, 2) as j:
                four(l, j * 4 + T_CH, w_in, j * (C_CB - C_CH) + C_CH)
            for br, w in ((0, w_conv_out), (1, w_mem_out)):
                with sp.Fori(0, 2) as j:
                    four(l, j * 8 + T_AM + 16 * br, w_in, j * 512 + C_GATE + 2 * D * br)
                    four(l, j * 8 + T_AM + 16 * br + 4, w, j * 512, slice(0, CW))
            with sp.Fori(0, 2) as j:
                four(l, j * 4 + T_WO, w_out, j * 512)
            with sp.Fori(0, 4) as g:
                with sp.Fori(0, 2) as j:
                    four(l, g * 16 + j * 4 + T_FF, w_up, g * D + j * 512)
                with sp.Fori(0, 2) as j:
                    four(l, g * 16 + j * 4 + T_FF + 8, w_down, j * 512, bass.ds(g * D, D))
        sp.wait_ge(r_ready, DEPTH * 16)
        sp.dma_start(yT.rearrange("(k p) n -> p k n", p=P), r[:, :, :]).then_inc(y_out, 16)
        sp.wait_ge(y_out, 16)
        sp.wait_ge(km_out, 32 * DEPTH)
        sp.wait_ge(st_out, 16 * DEPTH)
        sp.wait_ge(tail_out, 16 * DEPTH)
        for i in range(4):
            sp.wait_ge(s_out_done[i], 32 * DEPTH)

    @block.gpsimd
    def _(pool):
        pool.sem_inc(split_done, RING)
        with pool.Fori(0, DEPTH * TILES // RING) as it:
            for s in range(RING):
                pool.wait_ge(tile_done, it * RING + s + 1)
                pool.wait_ge(stage_full[s], it * 16 + 16)
                pool.sem_inc(split_begun, 1)
                nc.gpsimd.tensor_scalar(w_hi[:, s, :], stage[:, s, :], 1.0, 1.0, ALU.mult, ALU.mult).then_inc(hi_done, 1)
                pool.wait_ge(hi_done, it * RING + s + 1)
                nc.gpsimd.tensor_tensor(w_lo[:, s, :], stage[:, s, :], w_hi[:, s, :].bitcast(F32),
                                        ALU.subtract).then_inc(split_done, 1)

    @block.tensor
    def _(pe):
        mm = nc.tensor.matmul
        pe.sem_inc(tile_done, RING)

        def product(l, t, half_t, i, hi, lo, nk=KT, wait_k=None):
            pe.wait_ge(split_done, l * TILES + t + 1 + RING)
            pe.wait_ge(pair_free[i % 2], l * (TILES // 2) + half_t + 1)
            n, last = 0, None
            for k in range(nk):
                if wait_k is not None:
                    wait_k(k)
                for w, x in ((w_hi, hi), (w_hi, lo), (w_lo, hi)):
                    for half in range(2):
                        last = mm(gp[:, 2 * (i % 2) + half, 0:HALF], w[:, i % 4, k * P:(k + 1) * P],
                                  x(k, half), start=(n == 0), stop=(n == 3 * nk - 1))
                    n += 1
            last.then_inc(tile_done, 1)

        def tiles_of(buf, first=None):
            def get(k, half):
                if first is None:
                    return buf[:, k, half * HALF:(half + 1) * HALF]
                return buf[:, bass.ds(first + k, 1), half * HALF:(half + 1) * HALF].rearrange("p a b -> p (a b)")
            return get

        X = (tiles_of(x_hi), tiles_of(x_lo))
        B = (tiles_of(b_hi), tiles_of(b_lo))
        M = (tiles_of(m_hi), tiles_of(m_lo))

        def take(l, bank, tag):
            pe.wait_ge(side_free[bank], use(l, bank, tag))

        def f32(out, lhsT, rhs, start=True, stop=True, shared=False):
            return mm(out, lhsT, rhs, start=start, stop=stop, **({"skip_group_check": True} if shared else {}))

        def transpose(out, in_, p=P):
            return nc.tensor.transpose(out, in_, ident[0:p, 0:p])

        def flip(out, in_, p=P):
            return f32(out, in_, ident[0:p, 0:p])

        pe.wait_ge(table_in, 16)
        with pe.Fori(0, DEPTH) as l:
            for i in range(8):
                product(l, T_RQK + i, (T_RQK + i) // 2, i, *X,
                        wait_k=(lambda k: pe.wait_ge(x_ready, l * 16 + k + 1)) if i == 0 else None)
            with pe.Fori(0, 2) as j:
                for i in range(4):
                    pe.wait_ge(split_done, l * TILES + j * 4 + T_RV + i + 1 + RING)
                    pe.wait_ge(pair_free[i % 2], l * (TILES // 2) + j * 2 + (T_RV + i) // 2 + 1)
                    for t in range(5):
                        first = 0 if t == 0 else NS + (t - 1) * P
                        out = gp[:, 2 * (i % 2) + t // 4, (t % 4) * P:(t % 4 + 1) * P]
                        n = 0
                        for k in range(KT):
                            for x, w in ((x_hi, w_hi), (x_hi, w_lo), (x_lo, w_hi)):
                                last = mm(out, x[:, k, first:first + P], w[:, i, k * P:(k + 1) * P],
                                          start=(n == 0), stop=(n == 3 * KT - 1))
                                n += 1
                    last.then_inc(tile_done, 1)
            with pe.Fori(0, 2) as j:
                for i in range(4):
                    product(l, j * 4 + T_RG + i, j * 2 + (T_RG + i) // 2, i, *X)

            pe.wait_ge(rot_done, l * 8 + 8 + 2)
            pe.wait_ge(v_ready, l * 8 + 8)
            for c in range(NCH):
                cols = slice(NS + c * P, NS + (c + 1) * P)
                take(l, 0, ("sc", c))
                for h in range(H):
                    last = f32(qb[:, 0, h * P:(h + 1) * P], kT[:, h, cols], qT[:, h, cols])
                last.then_inc(side_full[0], 1)
                take(l, 1, ("kt", c))
                for h in range(H):
                    last = transpose(qb[:, 1, h * P:(h + 1) * P], kT[:, h, cols])
                last.then_inc(side_full[1], 1)
                drained(pe, l, 0, ("sc", c))
                for bank in (2, 3):
                    take(l, bank, ("o", c))
                    for h in (2 * bank - 4, 2 * bank - 3):
                        out = qb[:, bank, (h % 2) * DV:(h % 2 + 1) * DV]
                        last = f32(out, sc[:, h, :], v[:, c + 1, h * DV:(h + 1) * DV], stop=(c == 0))
                        if c > 0:
                            last = f32(out, qd[:, h, :], S[:, h, :], start=False)
                    last.then_inc(side_full[bank], 1)
                drained(pe, l, 1, ("kt", c))
                for bank in (0, 1):
                    take(l, bank, ("kv", c))
                    for h in (2 * bank, 2 * bank + 1):
                        last = f32(qb[:, bank, (h % 2) * DV:(h % 2 + 1) * DV], kn[:, h * P:(h + 1) * P],
                                   v[:, c + 1, h * DV:(h + 1) * DV])
                    last.then_inc(side_full[bank], 1)
                for bank in (2, 3):
                    take(l, bank, ("ot", c))
                    for i in range(4):
                        n = 4 * (bank - 2) + i
                        last = transpose(qb[:, bank, i * P:(i + 1) * P], on[:, n // 2, (n % 2) * P:(n % 2 + 1) * P])
                    last.then_inc(side_full[bank], 1)

            take(l, 0, ("sc", "s"))
            for h in range(H):
                last = f32(qb[0:NS, 0, h * NS:(h + 1) * NS], kT[:, h, 0:NS], qT[:, h, 0:NS])
            last.then_inc(side_full[0], 1)
            take(l, 1, ("kt", "s"))
            for h in range(H):
                last = flip(qb[0:NS, 1, h * P:(h + 1) * P], kT[:, h, 0:NS])
            last.then_inc(side_full[1], 1)
            drained(pe, l, 0, ("sc", "s"))
            take(l, 2, ("oT", "s"))
            for n in range(2 * H):
                f32(qb[:, 2, n * NS:(n + 1) * NS], v[0:NS, 0, n * P:(n + 1) * P], sc[0:NS, n // 2, 0:NS],
                    start=(n == 0), stop=False, shared=True)
            for b in range(NB):
                pe.wait_ge(s_in_full[b % 4], l * 32 + (b // 4) * 16 + 16)
                for n in range(2 * H):
                    last = f32(qb[:, 2, n * NS + b * TS:n * NS + (b + 1) * TS],
                               s_in[:, b % 4, n // 2, (n % 2) * P:(n % 2 + 1) * P],
                               qd[:, n // 2, b * TS:(b + 1) * TS], start=False,
                               stop=(b == NB - 1 and n == 2 * H - 1), shared=True)
                if b == NB - 1:
                    last.then_inc(side_full[2], 1)
                pe.wait_ge(knb_ready, l * NB + b + 1)
                keys = (kn, kb1)[b % 2]
                for bank in (0, 1):
                    take(l, bank, ("kvs", b))
                    for h in (2 * bank, 2 * bank + 1):
                        last = f32(qb[:, bank, (h % 2) * DV:(h % 2 + 1) * DV], keys[0:NS, h * P:(h + 1) * P],
                                   v[0:NS, 0, h * DV:(h + 1) * DV])
                    last.then_inc(side_full[bank], 1)
            drained(pe, l, 2, ("oT", "s"))
            for bank in (2, 3):
                take(l, bank, ("o", "s"))
                for i in range(4):
                    n = 4 * (bank - 2) + i
                    last = flip(qb[0:NS, bank, i * P:(i + 1) * P],
                                     sc[:, :, :].rearrange("p a b -> p (a b)")[:, n * NS:(n + 1) * NS])
                last.then_inc(side_full[bank], 1)
            drained(pe, l, 3, ("o", "s"))
            take(l, 2, ("ot", "s"))
            for n in range(8):
                last = flip(qb[:, 2, n * NS:(n + 1) * NS], on[0:NS, n // 2, (n % 2) * P:(n % 2 + 1) * P], NS)
            last.then_inc(side_full[2], 1)

            with pe.Fori(0, 2) as j:
                for i in range(4):
                    product(l, j * 8 + T_RO + i, j * 4 + (T_RO + i) // 2, i, *X)
                for i in range(4):
                    if i == 0:
                        pe.wait_ge(b_ready, l * 9 + 9)
                    product(l, j * 8 + T_RO + 4 + i, j * 4 + (T_RO + 4 + i) // 2, i, *B)

            pe.wait_ge(mem_split, l + 1)
            for i in range(8):
                t = T_KV + i
                pe.wait_ge(split_done, l * TILES + t + 1 + RING)
                pe.wait_ge(pair_free[i % 2], l * (TILES // 2) + t // 2 + 1)
                if i < 4:
                    n = 0
                    for k in range(KT):
                        for w, x in ((w_hi, mt_hi), (w_hi, mt_lo), (w_lo, mt_hi)):
                            last = mm(gp[:, 2 * (i % 2), 0:ML], w[:, i, k * P:(k + 1) * P], x[:, k, :],
                                      start=(n == 0), stop=(n == 3 * KT - 1))
                            n += 1
                else:
                    for m in range(2):
                        n = 0
                        for k in range(KT):
                            for x, w in ((mt_hi, w_hi), (mt_hi, w_lo), (mt_lo, w_hi)):
                                last = mm(gp[:, 2 * (i % 2) + m, 0:P], x[:, k, m * P:(m + 1) * P],
                                          w[:, i - 4, k * P:(k + 1) * P], start=(n == 0), stop=(n == 3 * KT - 1))
                                n += 1
                last.then_inc(tile_done, 1)

            with pe.Fori(0, 4) as j:
                for i in range(4):
                    product(l, j * 4 + T_MQ + i, j * 2 + (T_MQ + i) // 2, i, *X)

            pe.wait_ge(mq_ready, l * 4 + 4)
            pe.wait_ge(km_ready, l * 8 + 8)

            def qk(h):
                b0 = 2 * (h % 2)
                for bank in (0, 1):
                    take(l, b0 + bank, ("qk", h))
                    for t in (2 * bank, 2 * bank + 1):
                        last = f32(qb[:, b0 + bank, (t % 2) * ML:(t % 2 + 1) * ML],
                                   mq[:, h, NS + t * P:NS + (t + 1) * P], km[:, h, :])
                    last.then_inc(side_full[b0 + bank], 1)

            def pv(h):
                b0 = 2 * (h % 2)
                pe.wait_ge(p_ready, l * 5 + h + 1)
                for m in (0, 1):
                    take(l, b0 + m, ("pt", h))
                    for t in range(4):
                        last = transpose(qb[:, b0 + m, t * P:(t + 1) * P], pr[:, h % 2, t, m * P:(m + 1) * P])
                    last.then_inc(side_full[b0 + m], 1)
                drained(pe, l, b0, ("pt", h))
                drained(pe, l, b0 + 1, ("pt", h))
                for m in (0, 1):
                    last = f32(qb[:, b0, :], vm[:, m, h * P:(h + 1) * P], pT[:, m, :], start=(m == 0), stop=(m == 1))
                last.then_inc(side_full[b0], 1)

            qk(0)
            qk(1)
            for h in range(H):
                pv(h)
                if h + 2 < H:
                    qk(h + 2)

            take(l, 0, ("qk", "s"))
            for b in range(NB):
                pe.wait_ge(kv_full[b % 6], l * 16 * kv_loads(b % 6) + (b // 6) * 16 + 16)
                for h in range(H):
                    for m in range(2):
                        n = m * H + h
                        last = f32(qb[:, 0, n * NS + b * TS:n * NS + (b + 1) * TS],
                                   kv_slot(b)[:, h * ML + m * P:h * ML + (m + 1) * P], mq[:, h, b * TS:(b + 1) * TS])
                last.then_inc(side_full[0] if b == NB - 1 else kv_used, 1)
            drained(pe, l, 0, ("qk", "s"))
            for bank in (2, 3):
                take(l, bank, ("sn", "s"))
                for h in (2 * bank - 4, 2 * bank - 3):
                    for m in range(2):
                        last = flip(qb[0:NS, bank, (h % 2) * ML + m * P:(h % 2) * ML + (m + 1) * P], sT[:, m, h, :])
                last.then_inc(side_full[bank], 1)
            pe.wait_ge(p_ready, l * 5 + 5)
            take(l, 0, ("pt", "s"))
            for n in range(2 * H):
                m, h = n // H, n % H
                last = flip(qb[:, 0, n * NS:(n + 1) * NS], pr_s[0:NS, h, m * P:(m + 1) * P], NS)
            last.then_inc(side_full[0], 1)
            drained(pe, l, 0, ("pt", "s"))
            take(l, 1, ("pv", "s"))
            for b in range(NB):
                i = NB + b
                pe.wait_ge(kv_full[i % 6], l * 16 * kv_loads(i % 6) + (i // 6) * 16 + 16)
                for h in range(H):
                    for m in range(2):
                        last = f32(qb[:, 1, h * NS + b * TS:h * NS + (b + 1) * TS],
                                   kv_slot(i)[:, m * CW + h * P:m * CW + (h + 1) * P],
                                   pT_s[:, m, h, b * TS:(b + 1) * TS], start=(m == 0), stop=(m == 1))
                last.then_inc(side_full[1] if b == NB - 1 else kv_used, 1)

            with pe.Fori(0, 2) as br:
                Z = (tiles_of(b_hi, br * 4), tiles_of(b_lo, br * 4))
                for j in range(2):
                    for i in range(4):
                        product(l, br * 16 + T_AM + 8 * j + i, br * 8 + (T_AM + 8 * j + i) // 2, i, *X)
                    if j == 0:
                        drained(pe, l, 1, ("pv", "s"))
                    for i in range(4):
                        product(l, br * 16 + T_AM + 8 * j + 4 + i, br * 8 + (T_AM + 8 * j + 4 + i) // 2, i, *Z, nk=4)

            for i in range(8):
                product(l, T_WO + i, (T_WO + i) // 2, i, *M,
                        wait_k=(lambda k: pe.wait_ge(m_ready, l * 8 + k + 1)) if i == 0 else None)

            def norm_stats(x):
                first = [0, 128, 256, 384, 448]
                pe.wait_ge(sum_ready, l * 2 + x + 1)
                take(l, 0, ("sum", x))
                for t in range(5):
                    last = f32(qb[:, 0, t:t + 1], racc[:, first[t]:first[t] + P], ones)
                last.then_inc(side_full[0], 1)

                def spread(tag, col):
                    take(l, 1, tag)
                    for t in range(4):
                        last = f32(qb[:, 1, t * P:(t + 1) * P], st[:, col, t:t + 1].to_broadcast([P, P]), ident)
                    last.then_inc(side_full[1], 1)
                    take(l, 2, tag)
                    f32(qb[:, 2, 0:NS], st[:, col, 4:5].to_broadcast([P, P]),
                        ident[:, P - NS:P]).then_inc(side_full[2], 1)

                drained(pe, l, 0, ("sum", x))
                spread(("mean", x), 0)
                take(l, 3, ("sq", x))
                for k in range(KT):
                    pe.wait_ge(sq_ready, l * 16 + 8 * x + k + 1)
                    for t in range(5):
                        last = f32(qb[:, 3, t:t + 1], sq[:, k, first[t]:first[t] + P], ones,
                                   start=(k == 0 and t == 0), stop=(k == KT - 1 and t == 4), shared=True)
                last.then_inc(side_full[3], 1)
                pe.wait_ge(lrs_ready, l * 2 + x + 1)
                spread(("rstd", x), 3)

            norm_stats(0)

            with pe.Fori(0, 4) as g:
                for i in range(8):
                    product(l, g * 16 + T_FF + i, g * 8 + (T_FF + i) // 2, i, *X,
                            wait_k=(lambda k: pe.wait_ge(x_ready, l * 16 + 8 + k + 1)) if i == 0 else None)
                for i in range(8):
                    product(l, g * 16 + T_FF + 8 + i, g * 8 + (T_FF + 8 + i) // 2, i, *B,
                            wait_k=(lambda k: pe.wait_ge(hid_ready, l * 32 + g * 8 + k + 1 + 2)) if i == 0 else None)
            norm_stats(1)

    @block.scalar
    def _(act):
        act_fn = nc.scalar.activation
        act.dma_start(table_sb[:, :], table).then_inc(table_in, 16)
        act.dma_start(r[:, :, :], xT.rearrange("(k p) n -> p k n", p=P)).then_inc(x_in, 16)

        def free_pair(ins, i):
            ins.then_inc(pair_free[i % 2], 1)

        def gate_tile(l, t, i, br, tile):
            tile_is_done(act, l, t)
            ins = act_fn(halves(gate[:, i, :]), pair(i % 2), ACT.Sigmoid, bias=vcol(V_BG + br * KT + tile))
            free_pair(ins, i)

        act.wait_ge(table_in, 16)
        with act.Fori(0, DEPTH) as l:
            act.wait_ge(x_ready, l * 16 + 8)
            act.dma_start(vec[:, :], vectors[bass.ds(l, 1), :, :].rearrange("l p c -> (l p) c")).then_inc(vec_in, 16)
            act.dma_start(hist[:, :, :, :].rearrange("p a b c -> p (a b c)"),
                          conv_state[bass.ds(l, 1), :, :].rearrange("l p c -> (l p) c")).then_inc(hist_in, 16)
            for i in range(8):
                tile_is_done(act, l, T_RQK + i)
                act.wait_ge(rot_done, l * 8 + i + 1)
                act_fn(halves(rot[:, i % 2, 0, :]), pair(i % 2), ACT.Copy)
                act_fn(halves(rot[0:64, i % 2, 1, :]), gp[64:128, 2 * (i % 2):2 * (i % 2) + 2, 0:HALF], ACT.Copy)
                act_fn(halves(rot[64:128, i % 2, 1, :]), gp[0:64, 2 * (i % 2):2 * (i % 2) + 2, 0:HALF],
                       ACT.Copy).then_inc(rot_in, 1)
                act.wait_ge(rot_in, l * 8 + i + 1)
                act.sem_inc(pair_free[i % 2], 1)
            for i in range(8):
                tile_is_done(act, l, T_RV + i)
                b0 = 2 * (i % 2)
                act_fn(v[:, 0:4, i * P:(i + 1) * P], gp[:, b0, :].rearrange("p (t c) -> p t c", t=4), ACT.Copy)
                act_fn(v[:, 4, i * P:(i + 1) * P], gp[:, b0 + 1, 0:P], ACT.Copy).then_inc(v_ready, 1)
                act.wait_ge(v_ready, l * 8 + i + 1)
                act.sem_inc(pair_free[i % 2], 1)
            act.wait_ge(rot_done, l * 8 + 8 + 2)
            for i in range(8):
                tile_is_done(act, l, T_RG + i)
                act_fn(halves(rot[:, i % 2, 0, :]), pair(i % 2), ACT.Sigmoid).then_inc(sig_in, 1)
            def state_in(b):
                act.dma_start(s_in[:, b % 4, :, :], ret_state[bass.ds(l, 1), b, :, :, :].rearrange("l h d e -> d (l h) e")
                              ).then_inc(s_in_full[b % 4], 16)

            for b in range(4):
                state_in(b)

            for c in range(NCH + 1):
                p = P if c < NCH else NS
                if c == NCH:
                    drained(act, l, 0, ("kv", NCH - 1))
                    drained(act, l, 1, ("kv", NCH - 1))
                    act.dma_start(ret_prompt[bass.ds(l, 1), :, :, :].rearrange("l h d e -> d (l h) e"),
                                  S[:, :, :]).then_inc(st_out, 16)
                    for b in range(NB):
                        drained(act, l, 0, ("kvs", b))
                        drained(act, l, 1, ("kvs", b))
                        act.dma_start(ret_sample[bass.ds(l, 1), b, :, :, :].rearrange("l h d e -> d (l h) e"),
                                      s_in[:, b % 4, :, :]).then_inc(s_out_done[b % 4], 16)
                        if b >= 1 and b + 3 < NB:
                            act.wait_ge(s_out_done[(b - 1) % 4], l * 32 + ((b - 1) // 4) * 16 + 16)
                            state_in(b + 3)
                act.wait_ge(var_in, l * 5 + c + 1)
                act_fn(sd[0:p, :], ve[0:p, :], ACT.Sqrt).then_inc(std_in, 1)
            drained(act, l, 1, ("kvs", NB - 1))
            drained(act, l, 2, ("oT", "s"))
            act.wait_ge(st_out, l * 16 + 16)
            act.dma_start(mt_raw[:, :, :], memT.rearrange("(k p) m -> p k m", p=P)).then_inc(mem_in, 16)
            for b in range(4, NB):
                act.wait_ge(s_out_done[b % 4], l * 32 + 32)
            act.wait_ge(vec_in, l * 16 + 16)
            for j in range(2):
                for i in range(4):
                    gate_tile(l, T_RO + 8 * j + i, i, 1, 4 * j + i)
            for i in range(8):
                tile_is_done(act, l, T_KV + i)
                b0 = 2 * (i % 2)
                if i < 4:
                    ins = act_fn(km[:, i, :], gp[:, b0, 0:ML], ACT.Copy)
                else:
                    ins = act_fn(vm[:, :, (i - 4) * P:(i - 3) * P], gp[:, b0:b0 + 2, 0:P], ACT.Copy)
                ins.then_inc(km_ready, 1)
                act.wait_ge(km_ready, l * 8 + i + 1)
                act.sem_inc(pair_free[i % 2], 1)
            act.dma_start(kT_new[bass.ds(l, 1), :, :, :].rearrange("l p h m -> (l p) h m"), km[:, :, :]).then_inc(km_out, 16)
            act.dma_start(v_new[bass.ds(l, 1), :, :].rearrange("l (m p) c -> p (l m) c", p=P), vm[:, :, :]).then_inc(km_out, 16)
            for t0, buf, s in ((T_MQ, mq, mq_ready), (T_CC, cc, cc_in)):
                for i in range(4):
                    tile_is_done(act, l, t0 + i)
                    act_fn(halves(buf[:, i, :]), pair(i % 2), ACT.Copy).then_inc(s, 1)
                    act.wait_ge(s, l * 4 + i + 1)
                    act.sem_inc(pair_free[i % 2], 1)
            act.wait_ge(z_ready, l * 4 + 4)
            act.dma_start(conv_new[bass.ds(l, 1), :, :].rearrange("l p c -> (l p) c"),
                          tail[:, :, :].rearrange("p a b -> p (a b)")).then_inc(tail_out, 16)

            def cache_in(i):
                src = (kT_cache[bass.ds(l, 1), i, :, :].rearrange("l p c -> (l p) c") if i < NB else
                       v_cache[bass.ds(l, 1), i - NB, :, :].rearrange("l (m p) c -> p (l m) c", p=P))
                dst = kv_slot(i) if i < NB else kv_slot(i).rearrange("p (m c) -> p m c", m=2)
                act.dma_start(dst, src).then_inc(kv_full[i % 6], 16)

            def cache_slot_free(i):
                if i == NB - 1:
                    filled(act, l, 0, ("qk", "s"))
                else:
                    act.wait_ge(kv_used, l * 14 + i + 1 - (i >= NB))

            for i in range(6):
                cache_in(i)

            def exps(n, banks, width, p, out):
                act.wait_ge(nb_ready, l * 5 + n + 1)
                for t in range(4):
                    ins = act_fn(out[0:p, t, :], qb[0:p, banks[t // 2], (t % 2) * ML:(t % 2 + 1) * ML], ACT.Exp,
                                 bias=nb[0:p, n % 2, t:t + 1], scale=ATT_SCALE, accum_out=rs[0:p, n % 2, t:t + 1])
                    if t % 2:
                        ins.then_inc(side_free[banks[t // 2]], 1)

            def transposed(h):
                b0 = 2 * (h % 2)
                for m in range(2):
                    filled(act, l, b0 + m, ("pt", h))
                    if m == 0 and h > 0:
                        filled(act, l, 2 - b0, ("pv", h - 1))
                    act_fn(pT[:, m, :], qb[:, b0 + m, :], ACT.Copy).then_inc(side_free[b0 + m], 1)

            exps(0, (0, 1), ML, P, pr[:, 0, :, :])
            exps(1, (2, 3), ML, P, pr[:, 1, :, :])
            for h in range(H):
                transposed(h)
                if h + 2 < H:
                    b0 = 2 * (h % 2)
                    exps(h + 2, (b0, b0 + 1), ML, P, pr[:, h % 2, :, :])
            for i in range(6, 2 * NB):
                if i == 14:
                    exps(4, (2, 3), ML, NS, pr_s)
                    filled(act, l, 0, ("pt", "s"))
                    act_fn(pT_s[:, :, :, :].rearrange("p a b c -> p (a b c)"), qb[:, 0, :], ACT.Copy).then_inc(side_free[0], 1)
                cache_slot_free(i - 6)
                cache_in(i)
            act.wait_ge(km_out, l * 32 + 32)
            act.wait_ge(tail_out, l * 16 + 16)
            for br, sel in ((0, 0), (1, 2)):
                for j in range(2):
                    for i in range(4):
                        gate_tile(l, T_AM + 16 * br + 8 * j + i, i, sel, 4 * j + i)

            def norm(x):
                def spread(tag):
                    filled(act, l, 1, tag)
                    act_fn(row[:, 0:SEQ], qb[:, 1, :], ACT.Copy).then_inc(side_free[1], 1)
                    filled(act, l, 2, tag)
                    act_fn(row[:, SEQ:N], qb[:, 2, 0:NS], ACT.Copy).then_inc(side_free[2], 1)

                spread(("mean", x))
                for k in range(KT):
                    act.wait_ge(d_ready, l * 16 + 8 * x + k + 1)
                    act_fn(sq[:, k, :], r[:, k, :], ACT.Square).then_inc(sq_ready, 1)
                act.wait_ge(lvar_in, l * 2 + x + 1)
                act_fn(st[:, 2, :], st[:, 1, :], ACT.Sqrt).then_inc(lstd_in, 1)
                spread(("rstd", x))
                b = (V_LB1, V_LB2)[x]
                for k in range(KT):
                    act.wait_ge(y1_ready, l * 16 + 8 * x + k + 1)
                    act_fn(x_hi[:, k, :], r[:, k, :], ACT.Identity, bias=vcol(b + k)).then_inc(xh_in, 1)
                for k in range(KT):
                    act.wait_ge(x_ready, l * 16 + 8 * x + 8 + k + 1)
                    ins = act_fn(r[:, k, :], r[:, k, :], ACT.Identity, bias=vcol(b + k))
                    if x == 0:
                        ins.then_inc(act_step, 1)
                        act.wait_ge(act_step, k + 1)
                        ins = act_fn(r[:, k, :], r[:, k, :], ACT.Copy, scale=ALPHA)
                    ins.then_inc(r_ready, 1)

            act.sem_clear(act_step)
            norm(0)
            with act.Fori(0, 4) as g:
                for i in range(8):
                    tile_is_done(act, l, g * 16 + T_FF + i)
                    act.wait_ge(hid_ready, l * 32 + g * 8 + i + 1)
                    act_fn(halves(relu[:, i % 2, :]), pair(i % 2), ACT.Relu).then_inc(relu_in, 1)
                    act.wait_ge(relu_in, l * 32 + g * 8 + i + 1)
                    act.sem_inc(pair_free[i % 2], 1)
            norm(1)
            act.wait_ge(r_ready, l * 16 + 16)

    @block.vector
    def _(dve):
        vec_ = nc.vector
        steps = [0]

        def link(ins):
            steps[0] += 1
            ins.then_inc(dve_step, 1)
            dve.wait_ge(dve_step, steps[0])

        def split(hi, lo, x):
            link(vec_.tensor_copy(hi, x))
            return vec_.tensor_tensor(lo, x, hi.bitcast(F32), ALU.subtract)

        for i in range(2):
            dve.sem_inc(pair_free[i], 1)
        for i in range(4):
            dve.sem_inc(side_free[i], 1)
        dve.sem_inc(rot_done, 2)
        dve.sem_inc(hid_ready, 2)
        dve.wait_ge(x_in, 16)
        for k in range(KT):
            split(x_hi[:, k, :], x_lo[:, k, :], r[:, k, :]).then_inc(x_ready, 1)
        dve.wait_ge(table_in, 16)
        dve.wait_ge(x_ready, 8)
        with dve.Fori(0, DEPTH) as l:
            dve.sem_clear(dve_step)
            steps[0] = 0
            for i in range(8):
                dst = (qT if i < 4 else kT)[:, i % 4, :]
                dve.wait_ge(rot_in, l * 8 + i + 1)
                link(vec_.tensor_tensor(rot[:, i % 2, 0, :], rot[:, i % 2, 0, :], table_sb[:, K_COS:K_COS + N], ALU.mult))
                link(vec_.tensor_tensor(rot[:, i % 2, 1, :], rot[:, i % 2, 1, :], table_sb[:, K_SIN:K_SIN + N], ALU.mult))
                vec_.tensor_tensor(dst, rot[:, i % 2, 0, :], rot[:, i % 2, 1, :], ALU.add).then_inc(rot_done, 1)
            dve.wait_ge(vec_in, l * 16 + 16)
            for i in range(8):
                dve.wait_ge(sig_in, l * 8 + i + 1)
                vec_.scalar_tensor_tensor(halves(sil[:, i, :]), pair(i % 2), vcol(V_GN + i), halves(rot[:, i % 2, 0, :]),
                                          ALU.mult, ALU.mult).then_inc(pair_free[i % 2], 1)
            dve.wait_ge(pair_free[1], l * (TILES // 2) + (T_RG + 7) // 2 + 2)

            def group_norm(c, p):
                for h in range(H):
                    if h % 2 == 0:
                        filled(dve, l, 2 + h // 2, ("o", c))
                    ins = vec_.bn_stats(bst[0:p, h, :], qb[0:p, 2 + h // 2, (h % 2) * DV:(h % 2 + 1) * DV])
                link(ins)
                for h in range(H):
                    ins = vec_.bn_aggr(mv[0:p, h, :], bst[0:p, h, :])
                link(ins)
                vec_.tensor_scalar(ve[0:p, :], mv[0:p, :, 1], GN_EPS, None, ALU.add).then_inc(var_in, 1)
                n = c if c != "s" else NCH
                dve.wait_ge(std_in, l * 5 + n + 1)
                link(vec_.reciprocal(rstd[0:p, :], sd[0:p, :]))
                for h in range(H):
                    ins = vec_.tensor_scalar(on[0:p, h, :], qb[0:p, 2 + h // 2, (h % 2) * DV:(h % 2 + 1) * DV],
                                             mv[0:p, h, 0:1], rstd[0:p, h:h + 1], ALU.subtract, ALU.mult)
                    if h % 2:
                        ins.then_inc(side_free[2 + h // 2], 1)

            link(vec_.memset(S[:, :, :], 0.0))
            for c in range(NCH):
                cols = slice(NS + c * P, NS + (c + 1) * P)
                dve.wait_ge(rot_done, l * 8 + 8 + 2)
                link(vec_.tensor_tensor(qd[:, :, :], qT[:, :, cols], const3(K_QDP, H, P), ALU.mult))
                filled(dve, l, 0, ("sc", c))
                vec_.tensor_tensor(sc[:, :, :], qb[:, 0, :].rearrange("p (a b) -> p a b", a=H),
                                   const3(K_DMP, H, P), ALU.mult).then_inc(side_free[0], 1)
                filled(dve, l, 1, ("kt", c))
                vec_.tensor_tensor(kn[:, :].rearrange("p (a b) -> p a b", a=H), qb[:, 1, :].rearrange("p (a b) -> p a b", a=H),
                                   const3(K_KDP, H, 1).to_broadcast([P, H, P]), ALU.mult).then_inc(side_free[1], 1)
                group_norm(c, P)
                for bank in (0, 1):
                    filled(dve, l, bank, ("kv", c))
                    for h in (2 * bank, 2 * bank + 1):
                        ins = vec_.scalar_tensor_tensor(S[:, h, :], S[:, h, :], G_CHUNK[h],
                                                        qb[:, bank, (h % 2) * DV:(h % 2 + 1) * DV], ALU.mult, ALU.add)
                    ins.then_inc(side_free[bank], 1)
                for bank in (2, 3):
                    tiles = slice(4 * (bank - 2), 4 * (bank - 1))
                    filled(dve, l, bank, ("ot", c))
                    p3 = prod[:, :].rearrange("p (a b) -> p a b", a=4)
                    vec_.tensor_tensor(p3, qb[:, bank, :].rearrange("p (a b) -> p a b", a=4),
                                       sil[:, tiles, cols], ALU.mult).then_inc(side_free[bank], 1)
                    drained(dve, l, bank, ("ot", c))
                    split(b_hi[:, tiles, cols], b_lo[:, tiles, cols], p3).then_inc(b_ready, 1)
                    dve.wait_ge(b_ready, l * 9 + 2 * c + bank - 1)
                drained(dve, l, 1, ("kv", c))

            link(vec_.tensor_tensor(qd[:, :, 0:NS], qT[:, :, 0:NS], const3(K_QDS, H, NS), ALU.mult))
            filled(dve, l, 0, ("sc", "s"))
            vec_.tensor_tensor(sc[0:NS, :, 0:NS], qb[0:NS, 0, 0:H * NS].rearrange("p (a b) -> p a b", a=H),
                               const3(K_DMS, H, NS, NS), ALU.mult).then_inc(side_free[0], 1)
            filled(dve, l, 1, ("kt", "s"))
            keys = prod[0:NS, :]
            vec_.tensor_copy(keys, qb[0:NS, 1, :]).then_inc(side_free[1], 1)
            drained(dve, l, 1, ("kt", "s"))
            for b in range(NB):
                dst = (kn, kb1)[b % 2]
                if b >= 2:
                    filled(dve, l, 1, ("kvs", b - 2))
                vec_.tensor_tensor(dst[0:NS, :].rearrange("p (a b) -> p a b", a=H), keys.rearrange("p (a b) -> p a b", a=H),
                                   const3(K_KDS + b * H, H, 1, NS).to_broadcast([NS, H, P]), ALU.mult).then_inc(knb_ready, 1)
                if b >= 1:
                    state_of = b - 1
                    for bank in (0, 1):
                        filled(dve, l, bank, ("kvs", state_of))
                        for h in (2 * bank, 2 * bank + 1):
                            s = s_in[:, state_of % 4, h, :]
                            ins = vec_.scalar_tensor_tensor(s, s, G_TS[h], qb[:, bank, (h % 2) * DV:(h % 2 + 1) * DV],
                                                            ALU.mult, ALU.add)
                        ins.then_inc(side_free[bank], 1)
            for bank in (0, 1):
                filled(dve, l, bank, ("kvs", NB - 1))
                for h in (2 * bank, 2 * bank + 1):
                    s = s_in[:, (NB - 1) % 4, h, :]
                    ins = vec_.scalar_tensor_tensor(s, s, G_TS[h], qb[:, bank, (h % 2) * DV:(h % 2 + 1) * DV],
                                                    ALU.mult, ALU.add)
                ins.then_inc(side_free[bank], 1)
            filled(dve, l, 2, ("oT", "s"))
            vec_.tensor_copy(sc[:, :, :].rearrange("p a b -> p (a b)"), qb[:, 2, :]).then_inc(side_free[2], 1)
            group_norm("s", NS)
            filled(dve, l, 2, ("ot", "s"))
            p8 = prod[:, :].rearrange("p (a b) -> p a b", a=KT)
            vec_.tensor_tensor(p8, qb[:, 2, :].rearrange("p (a b) -> p a b", a=KT), sil[:, :, 0:NS],
                               ALU.mult).then_inc(side_free[2], 1)
            drained(dve, l, 2, ("ot", "s"))
            split(b_hi[:, :, 0:NS], b_lo[:, :, 0:NS], p8).then_inc(b_ready, 1)

            dve.wait_ge(mem_in, l * 16 + 16)
            split(mt_hi[:, :, :], mt_lo[:, :, :], mt_raw[:, :, :]).then_inc(mem_split, 1)
            dve.wait_ge(st_out, l * 16 + 16)
            dve.wait_ge(b_ready, l * 9 + 9)
            for j in range(2):
                for i in range(4):
                    tile_is_done(dve, l, T_RO + 8 * j + 4 + i)
                    vec_.tensor_tensor(halves(r[:, 4 * j + i, :]), pair(i % 2), halves(gate[:, i, :]),
                                       ALU.mult).then_inc(pair_free[i % 2], 1)

            dve.wait_ge(hist_in, l * 16 + 16)
            for i in range(4):
                u = up[:, i % 2, :]
                us = u[:, 0:NB * (TS + 2)].rearrange("p (b t) -> p b t", b=NB)
                upr = u[:, NB * (TS + 2):PAD]
                tile_is_done(dve, l, T_CH + i)
                dve.wait_ge(cc_in, l * 4 + i + 1)
                link(vec_.tensor_copy(us[:, :, 0:2], hist[:, i, :, :]))
                link(vec_.memset(upr[:, 0:2], 0.0))
                b0 = 2 * (i % 2)
                c3 = cc[:, i, :]
                link(vec_.tensor_tensor(us[:, :, 2:TS + 2], gp[:, b0, 0:NS].rearrange("p (b t) -> p b t", b=NB),
                                        c3[:, 0:NS].rearrange("p (b t) -> p b t", b=NB), ALU.mult))
                link(vec_.tensor_tensor(upr[:, 2:2 + HALF - NS], gp[:, b0, NS:HALF], c3[:, NS:HALF], ALU.mult))
                vec_.tensor_tensor(upr[:, 2 + HALF - NS:2 + SEQ], gp[:, b0 + 1, 0:HALF], c3[:, HALF:N],
                                   ALU.mult).then_inc(pair_free[i % 2], 1)
                dve.wait_ge(pair_free[i % 2], l * (TILES // 2) + (T_CH + i) // 2 + 2)
                link(vec_.tensor_copy(tail[:, i, 0:2 * NB].rearrange("p (b t) -> p b t", b=NB), us[:, :, TS:TS + 2]))
                link(vec_.tensor_copy(tail[:, i, 2 * NB:2 * NB + 2], upr[:, SEQ:SEQ + 2]))
                for w in range(3):
                    wc = vcol(V_CONV + 4 * w + i)
                    for dst, src in ((c3[:, 0:NS].rearrange("p (b t) -> p b t", b=NB), us[:, :, w:w + TS]),
                                     (c3[:, NS:N], upr[:, w:w + SEQ])):
                        if w == 0:
                            ins = vec_.tensor_scalar(dst, src, wc, None, ALU.mult)
                        else:
                            ins = vec_.scalar_tensor_tensor(dst, src, wc, dst, ALU.mult, ALU.add)
                    link(ins)
            for i in range(4):
                tile_is_done(dve, l, T_CB + i)
                vec_.tensor_tensor(halves(cc[:, i, :]), pair(i % 2), halves(cc[:, i, :]), ALU.mult).then_inc(pair_free[i % 2], 1)
                dve.wait_ge(pair_free[i % 2], l * (TILES // 2) + (T_CB + i) // 2 + 2)
                split(b_hi[:, i, :], b_lo[:, i, :], cc[:, i, :]).then_inc(z_ready, 1)

            def maxima(n, view, p):
                link(vec_.reduce_max(mx[0:p, n % 2, :], view, axis=AX.X))
                vec_.tensor_scalar(nb[0:p, n % 2, :], mx[0:p, n % 2, :], -ATT_SCALE, None, ALU.mult).then_inc(nb_ready, 1)

            def scores(b0, p):
                return qb[0:p, b0:b0 + 2, :].rearrange("p a (b c) -> p (a b) c", b=2)

            def normalise(n, buf, p):
                link(vec_.reciprocal(ri[0:p, n % 2, :], rs[0:p, n % 2, :]))
                for t in range(4):
                    ins = vec_.tensor_scalar(buf[0:p, t, :], buf[0:p, t, :], ri[0:p, n % 2, t:t + 1], None, ALU.mult)
                ins.then_inc(p_ready, 1)

            def head_max(h):
                for bank in (0, 1):
                    filled(dve, l, 2 * (h % 2) + bank, ("qk", h))
                maxima(h, scores(2 * (h % 2), P), P)

            def head_norm(h):
                for bank in (0, 1):
                    drained(dve, l, 2 * (h % 2) + bank, ("qk", h))
                normalise(h, pr[:, h % 2, :, :], P)

            def head_out(h):
                b0 = 2 * (h % 2)
                filled(dve, l, b0, ("pv", h))
                link(vec_.tensor_copy(b_hi[:, 4 + h, NS:N], qb[:, b0, :]))
                vec_.tensor_tensor(b_lo[:, 4 + h, NS:N], qb[:, b0, :], b_hi[:, 4 + h, NS:N].bitcast(F32),
                                   ALU.subtract).then_inc(side_free[b0], 1)

            head_max(0)
            head_max(1)
            for h in range(H):
                head_norm(h)
                head_out(h)
                if h + 2 < H:
                    head_max(h + 2)
            filled(dve, l, 0, ("qk", "s"))
            vec_.tensor_copy(sT[:, :, :, :].rearrange("p a b c -> p (a b c)"), qb[:, 0, :]).then_inc(side_free[0], 1)
            filled(dve, l, 2, ("sn", "s"))
            filled(dve, l, 3, ("sn", "s"))
            maxima(4, scores(2, NS), NS)
            drained(dve, l, 2, ("sn", "s"))
            drained(dve, l, 3, ("sn", "s"))
            normalise(4, pr_s, NS)
            filled(dve, l, 1, ("pv", "s"))
            o4 = qb[:, 1, 0:H * NS].rearrange("p (a b) -> p a b", a=H)
            link(vec_.tensor_copy(b_hi[:, 4:8, 0:NS], o4))
            vec_.tensor_tensor(b_lo[:, 4:8, 0:NS], o4, b_hi[:, 4:8, 0:NS].bitcast(F32), ALU.subtract).then_inc(side_free[1], 1)

            for br in range(2):
                for j in range(2):
                    for i in range(4):
                        t, m = T_AM + 16 * br + 8 * j + 4 + i, 4 * j + i
                        tile_is_done(dve, l, t)
                        vec_.tensor_tensor(halves(tmp[:, i % 2, :]), pair(i % 2), halves(gate[:, i, :]),
                                           ALU.mult).then_inc(pair_free[i % 2], 1)
                        dve.wait_ge(pair_free[i % 2], l * (TILES // 2) + t // 2 + 2)
                        link(vec_.tensor_tensor(r[:, m, :], r[:, m, :], tmp[:, i % 2, :], ALU.add))
                        if br == 1:
                            split(m_hi[:, m, :], m_lo[:, m, :], r[:, m, :]).then_inc(m_ready, 1)
            dve.wait_ge(km_out, l * 32 + 32)
            dve.wait_ge(m_ready, l * 8 + 8)
            for m in range(KT):
                t = T_WO + m
                tile_is_done(dve, l, t)
                vec_.scalar_tensor_tensor(halves(r[:, m, :]), halves(x_hi[:, m, :].bitcast(F32)), ALPHA, pair(m % 2),
                                          ALU.mult, ALU.add).then_inc(pair_free[m % 2], 1)
                dve.wait_ge(pair_free[m % 2], l * (TILES // 2) + t // 2 + 2)
                link(vec_.scalar_tensor_tensor(r[:, m, :], x_lo[:, m, :].bitcast(F32), ALPHA, r[:, m, :], ALU.mult, ALU.add))
                if m == 0:
                    link(vec_.tensor_copy(racc[:, :], r[:, 0, :]))
                elif m < KT - 1:
                    link(vec_.tensor_tensor(racc[:, :], racc[:, :], r[:, m, :], ALU.add))
                else:
                    vec_.tensor_tensor(racc[:, :], racc[:, :], r[:, m, :], ALU.add).then_inc(sum_ready, 1)

            def norm(x):
                filled(dve, l, 0, ("sum", x))
                vec_.tensor_scalar(st[:, 0, :], qb[:, 0, 0:5], -1.0 / D, None, ALU.mult).then_inc(side_free[0], 1)
                drained(dve, l, 1, ("mean", x))
                drained(dve, l, 2, ("mean", x))
                for k in range(KT):
                    vec_.tensor_tensor(r[:, k, :], r[:, k, :], row[:, :], ALU.add).then_inc(d_ready, 1)
                filled(dve, l, 3, ("sq", x))
                link(vec_.tensor_scalar(st[:, 1, :], qb[:, 3, 0:5], 1.0 / D, LN_EPS, ALU.mult, ALU.add))
                dve.sem_inc(side_free[3], 1)
                dve.sem_inc(lvar_in, 1)
                dve.wait_ge(lstd_in, l * 2 + x + 1)
                vec_.reciprocal(st[:, 3, :], st[:, 2, :]).then_inc(lrs_ready, 1)
                drained(dve, l, 1, ("rstd", x))
                drained(dve, l, 2, ("rstd", x))
                g, b = ((V_LG1, V_LB1), (V_LG2, V_LB2))[x]

                def low(k):
                    dve.wait_ge(xh_in, l * 16 + 8 * x + k + 1)
                    vec_.scalar_tensor_tensor(x_lo[:, k, :], r[:, k, :], vcol(b + k), x_hi[:, k, :].bitcast(F32),
                                              ALU.add, ALU.subtract).then_inc(x_ready, 1)

                for k in range(KT):
                    vec_.scalar_tensor_tensor(r[:, k, :], r[:, k, :], vcol(g + k), row[:, :], ALU.mult,
                                              ALU.mult).then_inc(y1_ready, 1)
                    if k:
                        low(k - 1)
                low(KT - 1)

            norm(0)

            base = steps[0]

            def group(g, first_step, last):
                n = [0]

                def glink(ins):
                    n[0] += 1
                    ins.then_inc(dve_step, 1)
                    dve.wait_ge(dve_step, first_step + n[0])

                for i in range(8):
                    dve.wait_ge(relu_in, l * 32 + g * 8 + i + 1)
                    t = relu[:, i % 2, :]
                    glink(vec_.tensor_tensor(t, t, t, ALU.mult))
                    glink(vec_.tensor_copy(b_hi[:, i, :], t))
                    vec_.tensor_tensor(b_lo[:, i, :], t, b_hi[:, i, :].bitcast(F32), ALU.subtract).then_inc(hid_ready, 1)
                dve.wait_ge(r_ready, l * 16 + 8)
                for m in range(KT):
                    tile_is_done(dve, l, g * 16 + T_FF + 8 + m)
                    vec_.tensor_tensor(halves(r[:, m, :]), halves(r[:, m, :]), pair(m % 2), ALU.add).then_inc(pair_free[m % 2], 1)
                    if last:
                        dve.wait_ge(pair_free[m % 2], l * (TILES // 2) + g * 8 + (T_FF + 8 + m) // 2 + 2)
                        if m == 0:
                            glink(vec_.tensor_copy(racc[:, :], r[:, 0, :]))
                        elif m < KT - 1:
                            glink(vec_.tensor_tensor(racc[:, :], racc[:, :], r[:, m, :], ALU.add))
                        else:
                            vec_.tensor_tensor(racc[:, :], racc[:, :], r[:, m, :], ALU.add).then_inc(sum_ready, 1)
                return n[0]

            with dve.Fori(0, 3) as g:
                per = group(g, g * 16 + base, False)
                assert per == 16
            group(3, base + 3 * per, True)
            steps[0] = base + 3 * per + per + KT - 1
            norm(1)
            dve.wait_ge(x_ready, l * 16 + 24)

    block_cm.__exit__(None, None, None)


def kv_loads(slot):
    return len(range(slot, 2 * NB, 6))


def shape_table():
    t = np.zeros((P, K_ALL), np.float32)
    pos = np.concatenate([np.tile(4096 + np.arange(TS), NB), np.arange(SEQ)]).astype(np.float32)
    inv = (10000.0 ** (-np.arange(64, dtype=np.float64) / 64)).astype(np.float32)
    ang = (pos[None, :] * inv[:, None]).astype(np.float32).astype(np.float64)
    t[:, K_COS:K_COS + N] = np.concatenate([np.cos(ang)] * 2)
    t[:, K_SIN:K_SIN + N] = np.concatenate([-np.sin(ang), np.sin(ang)])
    g = np.array(LOG_G)
    j, i = np.arange(P)[:, None, None], np.arange(P)[None, None, :]
    keep = np.where(i >= j, np.exp(np.maximum(i - j, 0) * g[None, :, None]), 0.0) * RET_SCALE
    t[:, K_DMP:K_DMP + H * P] = keep.reshape(P, -1)
    js, is_ = j[:NS], i[:, :, :NS]
    same = (js // TS == is_ // TS)
    t[:NS, K_DMS:K_DMS + H * NS] = (keep[:NS, :, :NS] * same).reshape(NS, -1)
    t[:, K_QDP:K_QDP + H * P] = np.exp((np.arange(P)[None] + 1.0) * g[:, None]).reshape(1, -1)
    t[:, K_QDS:K_QDS + H * NS] = np.exp((np.arange(NS)[None] % TS + 1.0) * g[:, None]).reshape(1, -1)
    t[:, K_KDP:K_KDP + H] = np.exp((CHUNK - 1.0 - np.arange(P))[:, None] * g[None]) * RET_SCALE
    kd = np.exp((TS - 1.0 - np.arange(NS) % TS)[:, None, None] * g[None, None]) * RET_SCALE
    own = (np.arange(NS)[:, None] // TS == np.arange(NB)[None])[:, :, None]
    t[:NS, K_KDS:K_KDS + H * NB] = (kd * own).reshape(NS, -1)
    t[:, K_ID:K_ID + P] = np.eye(P)
    t[:, K_ONE] = 1.0
    return t


def kernel(**inputs):
    import concourse.bacc as bacc
    from concourse.bass_utils import run_bass_kernel_spmd

    a = {k: np.asarray(x) for k, x in inputs.items()}
    c = np.ascontiguousarray

    def columns(x):
        return x.reshape(DEPTH, -1, P).transpose(0, 2, 1)

    ins = {
        "xT": c(np.concatenate([a["x_sample"].reshape(NS, D), a["x_prompt"].reshape(SEQ, D)]).T),
        "memT": c(a["mem_prompt"].reshape(ML, D).T),
        "kT_cache": c(a["cache_mem_k"].transpose(0, 1, 4, 3, 2).reshape(DEPTH, NB, P, H * ML)),
        "v_cache": c(a["cache_mem_v"].reshape(DEPTH, NB, ML, CW)),
        "conv_state": c(a["state_conv"].reshape(DEPTH, NB, 2, 4, P).transpose(0, 4, 3, 1, 2).reshape(DEPTH, P, 64)),
        "ret_state": c(a["state_ret"]),
    }
    for w in ("w_in", "w_conv_out", "w_ret_out", "w_mem_out", "w_out", "w_mem_kv", "w_up", "w_down"):
        ins[w] = c(a[w])
    ins["vectors"] = c(np.concatenate(
        [columns(a["b_gate"]), columns(a["ret_gn_g"]), columns(a["conv_w"].reshape(DEPTH, -1)), columns(a["ln1_g"]),
         columns(a["ln1_b"]), columns(a["ln2_g"]), columns(a["ln2_b"])], axis=2))
    ins["table"] = shape_table()
    outs = {"yT": (D, N), "kT_new": (DEPTH, P, H, ML), "v_new": (DEPTH, ML, CW), "conv_new": (DEPTH, P, 72),
            "ret_prompt": (DEPTH, H, DK, DV), "ret_sample": (DEPTH, NB, H, DK, DV)}

    nc = bacc.Bacc("TRN2", target_bir_lowering=False, num_devices=1, dynamic_dma_scratch_size=1024)
    args = [nc.dram_tensor(f"in_{n}", x.shape, F32, kind="ExternalInput").ap() for n, x in ins.items()]
    args += [nc.dram_tensor(f"out_{n}", s, F32, kind="ExternalOutput").ap() for n, s in outs.items()]
    layers(nc, *args)
    res = run_bass_kernel_spmd(nc, [{f"in_{n}": x for n, x in ins.items()}], core_ids=[0]).results[0]
    o = {n: res[f"out_{n}"] for n in outs}
    y = o["yT"].T
    conv = o["conv_new"].reshape(DEPTH, P, 4, NB + 1, 2).transpose(0, 3, 4, 2, 1).reshape(DEPTH, NB + 1, 2, CW)
    return (c(y[NS:]).reshape(1, SEQ, D), c(y[:NS]).reshape(NB, TS, D),
            c(o["kT_new"].transpose(0, 3, 2, 1)).reshape(DEPTH, 1, ML, H, P),
            o["v_new"].reshape(DEPTH, 1, ML, H, P),
            c(conv[:, NB:]), o["ret_prompt"].reshape(DEPTH, 1, H, DK, DV),
            c(conv[:, :NB]), o["ret_sample"])
```

```python
import numpy as np
import concourse.bass as bass
from concourse import mybir

F32 = mybir.dt.float32
F32R = mybir.dt.float32r
ALU = mybir.AluOpType
ACT = mybir.ActivationFunctionType
AX = mybir.AxisListType

DEPTH = 2
D = 1024
SEQ, NB, TS = 512, 8, 8
NS = NB * TS
N = NS + SEQ
HALF = N // 2
P = 128
KT = D // P
CW, H, DK, DV, ML = 512, 4, 128, 256, 256
CHUNK = 128
NCH = SEQ // CHUNK
ALPHA = (2 * DEPTH) ** 0.25
LN_EPS, GN_EPS = 1e-5, 1e-6
ATT_SCALE = P ** -0.5
RET_SCALE = DK ** -0.5
LOG_G = [float(np.log1p(-np.exp2(-5.0 - h))) for h in range(H)]
G_CHUNK = [float(np.exp(CHUNK * g)) for g in LOG_G]
G_TS = [float(np.exp(TS * g)) for g in LOG_G]
PAD = NB * (TS + 2) + SEQ + 2

C_CB, C_CC, C_CH, C_RQ, C_MQ, C_GATE = 0, 512, 1024, 1536, 4608, 5120

T_RQK, T_RV, T_RG, T_RO, T_KV, T_MQ, T_CC, T_CH, T_CB = 0, 8, 16, 24, 40, 48, 52, 56, 60
T_AM, T_WO, T_FF, TILES = 64, 96, 104, 168
KV_RING = 5
RING = 4
PIECE = KT * P

K_COS = 0
K_SIN = K_COS + N
K_DMP = K_SIN + N
K_DMS = K_DMP + H * P
K_QDP = K_DMS + H * NS
K_QDS = K_QDP + H * P
K_KDP = K_QDS + H * NS
K_KDS = K_KDP + H
K_ID = K_KDS + H * NB
K_ONE = K_ID + P
K_ALL = K_ONE + 1

V_BG, V_GN, V_CONV, V_LG1, V_LB1, V_LG2, V_LB2 = 0, 24, 32, 44, 52, 60, 68
V_ALL = 76

SIDE = [[], [], [], []]
for _c in range(NCH):
    SIDE[0] += [("sc", _c), ("kv", _c)]
    SIDE[1] += [("kt", _c), ("kv", _c)]
    SIDE[2] += [("o", _c), ("ot", _c)]
    SIDE[3] += [("o", _c), ("ot", _c)]
SIDE[0] += [("sc", "s")] + [("kvs", _b) for _b in range(NB)]
SIDE[1] += [("kt", "s")] + [("kvs", _b) for _b in range(NB)]
SIDE[2] += [("oT", "s"), ("o", "s"), ("ot", "s")]
SIDE[3] += [("o", "s")]
for _h in range(H):
    for _b in (0, 1):
        SIDE[2 * (_h % 2) + _b] += [("qk", _h), ("pt", _h)] + [("pv", _h)] * (_b == 0)
SIDE[0] += [("qk", "s"), ("pt", "s")]
SIDE[1] += [("pv", "s")]
SIDE[2] += [("sn", "s")]
SIDE[3] += [("sn", "s")]
for _x in range(2):
    SIDE[0] += [("sum", _x)]
    SIDE[1] += [("mean", _x), ("rstd", _x)]
    SIDE[2] += [("mean", _x), ("rstd", _x)]
    SIDE[3] += [("sq", _x)]


def use(l, bank, tag):
    return l * len(SIDE[bank]) + SIDE[bank].index(tag) + 1


def layers(nc, xT, memT, kT_cache, v_cache, conv_state, ret_state, w_in, w_conv_out, w_ret_out,
           w_mem_out, w_out, w_mem_kv, w_up, w_down, vectors, table,
           yT, kT_new, v_new, conv_new, ret_prompt, ret_sample):
    at = [(nc.sbuf_base + 31) // 32 * 32]

    def place(name, shape, dt, offset=None):
        size = 4 * int(np.prod(shape[1:]))
        if offset is None:
            offset, at[0] = at[0], at[0] + (size + 31) // 32 * 32
        return nc.alloc_sbuf_tensor_at(name, shape, dt, offset=offset)

    def here():
        return at[0]

    stage = place("stage", [P, RING, PIECE], F32)
    w_hi = place("w_hi", [P, RING, PIECE], F32R)
    w_lo = place("w_lo", [P, RING, PIECE], F32R)
    x_hi = place("x_hi", [P, KT, N], F32R)
    x_lo = place("x_lo", [P, KT, N], F32R)
    a_bhi = here()
    b_hi = place("b_hi", [P, KT, N], F32R)
    a_blo = here()
    b_lo = place("b_lo", [P, KT, N], F32R)
    rot = place("rot", [P, 2, 2, N], F32, a_bhi)
    oT = place("oT", [P, KT, N], F32, a_bhi)
    sil = place("sil", [P, KT, N], F32, a_blo)
    a_r = here()
    r = place("r", [P, KT, N], F32)
    kn = place("kn", [P, H * P], F32, a_r)
    qd = place("qd", [P, H, P], F32, a_r + 2048)
    sc = place("sc", [P, H, P], F32, a_r + 4096)
    kb1 = place("kb1", [P, H * P], F32, a_r + 6144)
    S = place("S", [P, H, DV], F32, a_r + 8192)
    on = place("on", [P, H, DV], F32, a_r + 12288)
    prod = place("prod", [P, 512], F32, a_r + 16384)
    a_g = here()
    gate = place("gate", [P, 4, N], F32)
    place("gate_rest", [P, 4096 - 4 * N], F32)
    s_in_g = place("s_in_g", [P, H, DV], F32, a_g + 16 * N)
    up = place("up", [P, 2, PAD], F32, a_g)
    a_c = here()
    place("C", [P, 11776], F32)

    def c_at(name, shape, dt, first):
        return place(name, shape, dt, a_c + 4 * first)

    qT = c_at("qT", [P, H, N], F32, 0)
    kT = c_at("kT", [P, H, N], F32, 2304)
    v = c_at("v", [P, 5, H * DV], F32, 4608)
    km = c_at("km", [P, H, ML], F32, 9728)
    vm = c_at("vm", [P, 2, CW], F32, 10752)
    s_in_c = c_at("s_in_c", [P, 2, H, DV], F32, 9728)
    mt_hi = c_at("mt_hi", [P, KT, ML], F32R, 0)
    mt_lo = c_at("mt_lo", [P, KT, ML], F32R, 2304)
    mt_raw = c_at("mt_raw", [P, KT, ML], F32, 4608)
    mq = c_at("mq", [P, H, N], F32, 0)
    cc = c_at("cc", [P, H, N], F32, 2304)
    pr = c_at("pr", [P, 2, 4, ML], F32, 4608)
    sT = c_at("sT", [P, 2, H, NS], F32, 4608)
    pT_s = c_at("pT_s", [P, 2, H, NS], F32, 5120)
    pr_s = c_at("pr_s", [P, H, ML], F32, 5632)
    pT = c_at("pT", [P, 2, SEQ], F32, 6656)
    kv_c = c_at("kv_c", [P, 2, 1024], F32, 7680)
    kv_z = c_at("kv_z", [P, 2, 1024], F32, 2304)
    kv_g = place("kv_g", [P, 1024], F32, a_g + 16 * N)
    m_hi = c_at("m_hi", [P, KT, N], F32R, 0)
    m_lo = c_at("m_lo", [P, KT, N], F32R, 4608)
    sq = c_at("sq", [P, KT, N], F32, 0)
    relu = c_at("relu", [P, 2, N], F32, 0)
    racc = c_at("racc", [P, N], F32, 9728)
    row = c_at("row", [P, N], F32, 10304)
    table_sb = place("table_sb", [P, K_ALL], F32)
    vec = place("vec", [P, V_ALL], F32)
    tmp = place("tmp", [P, 2, N], F32)
    hist = place("hist", [P, H, NB, 2], F32)
    tail = place("tail", [P, H, 2 * (NB + 1)], F32)
    mx = place("mx", [P, 2, H], F32)
    nb = place("nb", [P, 2, H], F32)
    rs = place("rs", [P, 2, H], F32)
    ri = place("ri", [P, 2, H], F32)
    bst = place("bst", [P, H, 6], F32)
    mv = place("mv", [P, H, 2], F32)
    ve = place("ve", [P, H], F32)
    sd = place("sd", [P, H], F32)
    rstd = place("rstd", [P, H], F32)
    st = place("st", [P, 4, 5], F32)
    assert at[0] <= nc.sbuf_usable_end, (at[0], nc.sbuf_usable_end)

    ident = table_sb[:, K_ID:K_ID + P]
    ones = table_sb[:, K_ONE:K_ONE + 1]

    def const3(first, a, b, p=P):
        return table_sb[0:p, first:first + a * b].rearrange("p (a b) -> p a b", a=a)

    def vcol(i):
        return vec[:, i:i + 1]

    def s_in(b):
        return s_in_g[:, :, :] if b % 3 == 2 else s_in_c[:, b % 3, :, :]

    def kv_slot(i):
        i %= KV_RING
        return kv_c[:, i, :] if i < 2 else kv_z[:, i - 2, :] if i < 4 else kv_g[:, :]

    gp = nc.alloc_psum_tensor("gp", [P, 4, 512], F32)
    qb = nc.alloc_psum_tensor("qb", [P, 4, 512], F32)

    def pair(par):
        return gp[:, 2 * par:2 * par + 2, 0:HALF]

    def halves(ap):
        return ap.rearrange("p (a b) -> p a b", a=2)

    sem = nc.alloc_semaphore
    split_done = sem("split_done")
    tile_done = sem("tile_done")
    pair_free = [sem(f"pair_free{i}") for i in range(2)]
    stage_full = [sem(f"stage_full{i}") for i in range(RING)]
    hi_done = sem("hi_done")
    split_begun = sem("split_begun")
    side_full = [sem(f"side_full{i}") for i in range(4)]
    side_free = [sem(f"side_free{i}") for i in range(4)]
    dve_step = sem("dve_step")
    act_step = sem("act_step")
    table_in, x_in, vec_in, hist_in, mem_in = (sem(n) for n in ("table_in", "x_in", "vec_in", "hist_in", "mem_in"))
    s_in_full = [sem(f"s_in_full{i}") for i in range(3)]
    s_out_done = [sem(f"s_out_done{i}") for i in range(3)]
    values_done = sem("values_done")
    oT_ready = sem("oT_ready")
    kv_full = [sem(f"kv_full{i}") for i in range(KV_RING)]
    kv_used = sem("kv_used")
    x_ready = sem("x_ready")
    mem_split = sem("mem_split")
    km_ready = sem("km_ready")
    rot_in = sem("rot_in")
    rot_done = sem("rot_done")
    v_ready = sem("v_ready")
    sig_in = sem("sig_in")
    gate_in = sem("gate_in")
    mq_ready = sem("mq_ready")
    cc_in = sem("cc_in")
    z_ready = sem("z_ready")
    knb_ready = sem("knb_ready")
    s_ready = sem("s_ready")
    var_in = sem("var_in")
    std_in = sem("std_in")
    b_ready = sem("b_ready")
    nb_ready = sem("nb_ready")
    p_ready = sem("p_ready")
    m_ready = sem("m_ready")
    sum_ready = sem("sum_ready")
    d_ready = sem("d_ready")
    sq_ready = sem("sq_ready")
    lvar_in, lstd_in, lrs_ready = sem("lvar_in"), sem("lstd_in"), sem("lrs_ready")
    y1_ready = sem("y1_ready")
    xh_in = sem("xh_in")
    r_ready = sem("r_ready")
    relu_in = sem("relu_in")
    hid_ready = sem("hid_ready")
    km_out, st_out, tail_out, y_out = sem("km_out"), sem("st_out"), sem("tail_out"), sem("y_out")

    def filled(eng, l, bank, tag):
        eng.wait_ge(side_full[bank], use(l, bank, tag))

    def drained(eng, l, bank, tag):
        eng.wait_ge(side_free[bank], use(l, bank, tag) + 1)

    def tile_is_done(eng, l, t):
        eng.wait_ge(tile_done, l * TILES + t + 1 + RING)

    block_cm = nc.Block()
    block = block_cm.__enter__()

    @block.sync
    def _(sp):
        def load(l, t, slot, src):
            sp.wait_ge(split_done, l * TILES + t + 1)
            rows = src.shape[0] * src.shape[1] // P
            sp.dma_start(stage[:, slot, 0:rows * P].rearrange("p (k c) -> p k c", k=rows),
                         src.rearrange("l (k p) c -> p (l k) c", p=P)).then_inc(stage_full[slot], 16)

        def four(l, t, w, col, rows=slice(0, D)):
            for i in range(4):
                load(l, t + i, i, w[bass.ds(l, 1), rows, bass.ds(col + i * P, P)])

        with sp.Fori(0, DEPTH) as l:
            with sp.Fori(0, 6) as j:
                four(l, j * 4 + T_RQK, w_in, j * 512 + C_RQ)
            with sp.Fori(0, 2) as j:
                four(l, j * 8 + T_RO, w_in, j * 512 + C_GATE + D)
                four(l, j * 8 + T_RO + 4, w_ret_out, j * 512)
            with sp.Fori(0, 2) as j:
                four(l, j * 4 + T_KV, w_mem_kv, j * 512)
            four(l, T_MQ, w_in, C_MQ)
            four(l, T_CC, w_in, C_CC)
            with sp.Fori(0, 2) as j:
                four(l, j * 4 + T_CH, w_in, j * (C_CB - C_CH) + C_CH)
            for br, w in ((0, w_conv_out), (1, w_mem_out)):
                with sp.Fori(0, 2) as j:
                    four(l, j * 8 + T_AM + 16 * br, w_in, j * 512 + C_GATE + 2 * D * br)
                    four(l, j * 8 + T_AM + 16 * br + 4, w, j * 512, slice(0, CW))
            with sp.Fori(0, 2) as j:
                four(l, j * 4 + T_WO, w_out, j * 512)
            with sp.Fori(0, 4) as g:
                with sp.Fori(0, 2) as j:
                    four(l, g * 16 + j * 4 + T_FF, w_up, g * D + j * 512)
                with sp.Fori(0, 2) as j:
                    four(l, g * 16 + j * 4 + T_FF + 8, w_down, j * 512, bass.ds(g * D, D))
        sp.wait_ge(r_ready, DEPTH * 16)
        sp.dma_start(yT.rearrange("(k p) n -> p k n", p=P), r[:, :, :]).then_inc(y_out, 16)
        sp.wait_ge(y_out, 16)
        sp.wait_ge(km_out, 32 * DEPTH)
        sp.wait_ge(st_out, 16 * DEPTH)
        sp.wait_ge(tail_out, 16 * DEPTH)
        for i in range(3):
            sp.wait_ge(s_out_done[i], 16 * state_loads(i) * DEPTH)

    @block.gpsimd
    def _(pool):
        pool.sem_inc(split_done, RING)
        with pool.Fori(0, DEPTH * TILES // RING) as it:
            for s in range(RING):
                pool.wait_ge(tile_done, it * RING + s + 1)
                pool.wait_ge(stage_full[s], it * 16 + 16)
                pool.sem_inc(split_begun, 1)
                nc.gpsimd.tensor_scalar(w_hi[:, s, :], stage[:, s, :], 1.0, 1.0, ALU.mult, ALU.mult).then_inc(hi_done, 1)
                pool.wait_ge(hi_done, it * RING + s + 1)
                nc.gpsimd.tensor_tensor(w_lo[:, s, :], stage[:, s, :], w_hi[:, s, :].bitcast(F32),
                                        ALU.subtract).then_inc(split_done, 1)

    @block.tensor
    def _(pe):
        mm = nc.tensor.matmul
        pe.sem_inc(tile_done, RING)

        def product(l, t, half_t, i, hi, lo, nk=KT, wait_k=None):
            pe.wait_ge(split_done, l * TILES + t + 1 + RING)
            pe.wait_ge(pair_free[i % 2], l * (TILES // 2) + half_t + 1)
            n, last = 0, None
            for k in range(nk):
                if wait_k is not None:
                    wait_k(k)
                for w, x in ((w_hi, hi), (w_hi, lo), (w_lo, hi)):
                    for half in range(2):
                        last = mm(gp[:, 2 * (i % 2) + half, 0:HALF], w[:, i % 4, k * P:(k + 1) * P],
                                  x(k, half), start=(n == 0), stop=(n == 3 * nk - 1))
                    n += 1
            last.then_inc(tile_done, 1)

        def tiles_of(buf, first=None):
            def get(k, half):
                if first is None:
                    return buf[:, k, half * HALF:(half + 1) * HALF]
                return buf[:, bass.ds(first + k, 1), half * HALF:(half + 1) * HALF].rearrange("p a b -> p (a b)")
            return get

        X = (tiles_of(x_hi), tiles_of(x_lo))
        B = (tiles_of(b_hi), tiles_of(b_lo))
        M = (tiles_of(m_hi), tiles_of(m_lo))

        def take(l, bank, tag):
            pe.wait_ge(side_free[bank], use(l, bank, tag))

        def f32(out, lhsT, rhs, start=True, stop=True, shared=False):
            return mm(out, lhsT, rhs, start=start, stop=stop, **({"skip_group_check": True} if shared else {}))

        def transpose(out, in_, p=P):
            return nc.tensor.transpose(out, in_, ident[0:p, 0:p])

        def flip(out, in_, p=P):
            return f32(out, in_, ident[0:p, 0:p])

        pe.wait_ge(table_in, 16)
        with pe.Fori(0, DEPTH) as l:
            for i in range(8):
                product(l, T_RQK + i, (T_RQK + i) // 2, i, *X,
                        wait_k=(lambda k: pe.wait_ge(x_ready, l * 16 + k + 1)) if i == 0 else None)
            with pe.Fori(0, 2) as j:
                for i in (0, 2):
                    pe.wait_ge(split_done, l * TILES + j * 4 + T_RV + i + 2 + RING)
                    for t in (1, 2, 3, 4, 0):
                        first = 0 if t == 0 else NS + (t - 1) * P
                        if t == 1:
                            pe.wait_ge(pair_free[0], l * (TILES // 2) + j * 2 + (T_RV + i) // 2 + 1)
                        elif t == 0:
                            pe.wait_ge(pair_free[1], l * (TILES // 2) + j * 2 + (T_RV + i) // 2 + 1)
                        out = gp[:, 2, 0:2 * P] if t == 0 else gp[:, (t - 1) // 2, (t - 1) % 2 * 2 * P:((t - 1) % 2 + 1) * 2 * P]
                        n = 0
                        for k in range(KT):
                            for x, w in ((x_hi, w_hi), (x_hi, w_lo), (x_lo, w_hi)):
                                last = mm(out, x[:, k, first:first + P], w[:, i:i + 2, k * P:(k + 1) * P],
                                          start=(n == 0), stop=(n == 3 * KT - 1))
                                n += 1
                        if t == 4:
                            last.then_inc(values_done, 1)
                    last.then_inc(tile_done, 2)
            def swish(i):
                product(l, T_RG + i, (T_RG + i) // 2, i, *X)

            pe.wait_ge(rot_done, l * 8 + 8 + 2)
            pe.wait_ge(v_ready, l * 8 + 8)
            for c in range(NCH):
                cols = slice(NS + c * P, NS + (c + 1) * P)
                take(l, 0, ("sc", c))
                for h in range(H):
                    last = f32(qb[:, 0, h * P:(h + 1) * P], kT[:, h, cols], qT[:, h, cols])
                last.then_inc(side_full[0], 1)
                take(l, 1, ("kt", c))
                for h in range(H):
                    last = transpose(qb[:, 1, h * P:(h + 1) * P], kT[:, h, cols])
                last.then_inc(side_full[1], 1)
                swish(2 * c)
                drained(pe, l, 0, ("sc", c))
                for bank in (2, 3):
                    take(l, bank, ("o", c))
                    for h in (2 * bank - 4, 2 * bank - 3):
                        out = qb[:, bank, (h % 2) * DV:(h % 2 + 1) * DV]
                        last = f32(out, sc[:, h, :], v[:, c + 1, h * DV:(h + 1) * DV], stop=(c == 0))
                        if c > 0:
                            last = f32(out, qd[:, h, :], S[:, h, :], start=False)
                    last.then_inc(side_full[bank], 1)
                drained(pe, l, 1, ("kt", c))
                for bank in (0, 1):
                    take(l, bank, ("kv", c))
                    for h in (2 * bank, 2 * bank + 1):
                        last = f32(qb[:, bank, (h % 2) * DV:(h % 2 + 1) * DV], kn[:, h * P:(h + 1) * P],
                                   v[:, c + 1, h * DV:(h + 1) * DV])
                    last.then_inc(side_full[bank], 1)
                swish(2 * c + 1)
                for bank in (2, 3):
                    take(l, bank, ("ot", c))
                    for i in range(4):
                        n = 4 * (bank - 2) + i
                        last = transpose(qb[:, bank, i * P:(i + 1) * P], on[:, n // 2, (n % 2) * P:(n % 2 + 1) * P])
                    last.then_inc(side_full[bank], 1)

            def ret_gate(i):
                product(l, T_RO + i, (T_RO + i) // 2, i, *X)

            take(l, 0, ("sc", "s"))
            for h in range(H):
                last = f32(qb[0:NS, 0, h * NS:(h + 1) * NS], kT[:, h, 0:NS], qT[:, h, 0:NS])
            last.then_inc(side_full[0], 1)
            take(l, 1, ("kt", "s"))
            for h in range(H):
                last = flip(qb[0:NS, 1, h * P:(h + 1) * P], kT[:, h, 0:NS])
            last.then_inc(side_full[1], 1)
            ret_gate(0)
            drained(pe, l, 0, ("sc", "s"))
            take(l, 2, ("oT", "s"))
            for n in range(2 * H):
                f32(qb[:, 2, n * NS:(n + 1) * NS], v[0:NS, 0, n * P:(n + 1) * P], sc[0:NS, n // 2, 0:NS],
                    start=(n == 0), stop=False, shared=True)
            for b in range(NB):
                if b == 4:
                    ret_gate(1)
                pe.wait_ge(s_in_full[b % 3], l * 16 * state_loads(b % 3) + (b // 3) * 16 + 16)
                for n in range(2 * H):
                    last = f32(qb[:, 2, n * NS + b * TS:n * NS + (b + 1) * TS],
                               s_in(b)[:, n // 2, (n % 2) * P:(n % 2 + 1) * P],
                               qd[:, n // 2, b * TS:(b + 1) * TS], start=False,
                               stop=(b == NB - 1 and n == 2 * H - 1), shared=True)
                if b == NB - 1:
                    last.then_inc(side_full[2], 1)
                pe.wait_ge(knb_ready, l * NB + b + 1)
                keys = (kn, kb1)[b % 2]
                for bank in (0, 1):
                    take(l, bank, ("kvs", b))
                    for h in (2 * bank, 2 * bank + 1):
                        last = f32(qb[:, bank, (h % 2) * DV:(h % 2 + 1) * DV], keys[0:NS, h * P:(h + 1) * P],
                                   v[0:NS, 0, h * DV:(h + 1) * DV])
                    last.then_inc(side_full[bank], 1)
            drained(pe, l, 2, ("oT", "s"))
            for bank in (2, 3):
                take(l, bank, ("o", "s"))
                for i in range(4):
                    n = 4 * (bank - 2) + i
                    last = flip(qb[0:NS, bank, i * P:(i + 1) * P],
                                     sc[:, :, :].rearrange("p a b -> p (a b)")[:, n * NS:(n + 1) * NS])
                last.then_inc(side_full[bank], 1)
            ret_gate(2)
            drained(pe, l, 3, ("o", "s"))
            take(l, 2, ("ot", "s"))
            for n in range(8):
                last = flip(qb[:, 2, n * NS:(n + 1) * NS], on[0:NS, n // 2, (n % 2) * P:(n % 2 + 1) * P], NS)
            last.then_inc(side_full[2], 1)

            ret_gate(3)

            pe.wait_ge(b_ready, l * 9 + 9)
            for i in range(4):
                product(l, T_RO + 4 + i, (T_RO + 4 + i) // 2, i, *B)
            for i in range(4):
                product(l, T_RO + 8 + i, (T_RO + 8 + i) // 2, i, *X)
            for i in range(4):
                product(l, T_RO + 12 + i, (T_RO + 12 + i) // 2, i, *B)

            pe.wait_ge(mem_split, l + 1)
            for i in range(4):
                t = T_KV + i
                pe.wait_ge(split_done, l * TILES + t + 1 + RING)
                pe.wait_ge(pair_free[i % 2], l * (TILES // 2) + t // 2 + 1)
                n = 0
                for k in range(KT):
                    for w, x in ((w_hi, mt_hi), (w_hi, mt_lo), (w_lo, mt_hi)):
                        last = mm(gp[:, 2 * (i % 2), 0:ML], w[:, i, k * P:(k + 1) * P], x[:, k, :],
                                  start=(n == 0), stop=(n == 3 * KT - 1))
                        n += 1
                last.then_inc(tile_done, 1)
            for i in (0, 2):
                t = T_KV + 4 + i
                pe.wait_ge(split_done, l * TILES + t + 2 + RING)
                for m in range(2):
                    pe.wait_ge(pair_free[m], l * (TILES // 2) + t // 2 + 1)
                    n = 0
                    for k in range(KT):
                        for x, w in ((mt_hi, w_hi), (mt_hi, w_lo), (mt_lo, w_hi)):
                            last = mm(gp[:, 2 * m, 0:2 * P], x[:, k, m * P:(m + 1) * P],
                                      w[:, i:i + 2, k * P:(k + 1) * P], start=(n == 0), stop=(n == 3 * KT - 1))
                            n += 1
                last.then_inc(tile_done, 2)

            with pe.Fori(0, 4) as j:
                for i in range(4):
                    product(l, j * 4 + T_MQ + i, j * 2 + (T_MQ + i) // 2, i, *X)

            Z = (tiles_of(b_hi, 0), tiles_of(b_lo, 0))
            Y = (tiles_of(b_hi, 4), tiles_of(b_lo, 4))

            def conv(*tiles):
                for n in tiles:
                    product(l, T_AM + n, (T_AM + n) // 2, n, *(Z if n // 4 % 2 else X), nk=4 if n // 4 % 2 else KT)

            pe.wait_ge(mq_ready, l * 4 + 4)
            pe.wait_ge(km_ready, l * 8 + 8)

            def qk(h):
                b0 = 2 * (h % 2)
                for bank in (0, 1):
                    take(l, b0 + bank, ("qk", h))
                    for t in (2 * bank, 2 * bank + 1):
                        last = f32(qb[:, b0 + bank, (t % 2) * ML:(t % 2 + 1) * ML],
                                   mq[:, h, NS + t * P:NS + (t + 1) * P], km[:, h, :])
                    last.then_inc(side_full[b0 + bank], 1)

            def pt(h):
                b0 = 2 * (h % 2)
                pe.wait_ge(p_ready, l * 5 + h + 1)
                for m in (0, 1):
                    take(l, b0 + m, ("pt", h))
                    for t in range(4):
                        last = transpose(qb[:, b0 + m, t * P:(t + 1) * P], pr[:, h % 2, t, m * P:(m + 1) * P])
                    last.then_inc(side_full[b0 + m], 1)

            def pv(h):
                b0 = 2 * (h % 2)
                drained(pe, l, b0, ("pt", h))
                drained(pe, l, b0 + 1, ("pt", h))
                for m in (0, 1):
                    last = f32(qb[:, b0, :], vm[:, m, h * P:(h + 1) * P], pT[:, m, :], start=(m == 0), stop=(m == 1))
                last.then_inc(side_full[b0], 1)

            qk(0)
            qk(1)
            conv(0, 1)
            pt(0)
            conv(2)
            pv(0)
            pt(1)
            conv(3)
            qk(2)
            pv(1)
            pe.wait_ge(z_ready, l * 4 + 4)
            conv(4, 5)
            qk(3)
            pt(2)
            conv(6)
            pv(2)
            conv(7)
            pt(3)
            conv(8)
            pv(3)

            take(l, 0, ("qk", "s"))
            for b in range(NB):
                if b == 4:
                    conv(9)
                pe.wait_ge(kv_full[b % KV_RING], l * 16 * kv_loads(b % KV_RING) + (b // KV_RING) * 16 + 16)
                for h in range(H):
                    for m in range(2):
                        n = m * H + h
                        last = f32(qb[:, 0, n * NS + b * TS:n * NS + (b + 1) * TS],
                                   kv_slot(b)[:, h * ML + m * P:h * ML + (m + 1) * P], mq[:, h, b * TS:(b + 1) * TS])
                last.then_inc(side_full[0] if b == NB - 1 else kv_used, 1)
            conv(10)
            drained(pe, l, 0, ("qk", "s"))
            for bank in (2, 3):
                take(l, bank, ("sn", "s"))
                for h in (2 * bank - 4, 2 * bank - 3):
                    for m in range(2):
                        last = flip(qb[0:NS, bank, (h % 2) * ML + m * P:(h % 2) * ML + (m + 1) * P], sT[:, m, h, :])
                last.then_inc(side_full[bank], 1)
            conv(11)
            pe.wait_ge(p_ready, l * 5 + 5)
            take(l, 0, ("pt", "s"))
            for n in range(2 * H):
                m, h = n // H, n % H
                last = flip(qb[:, 0, n * NS:(n + 1) * NS], pr_s[0:NS, h, m * P:(m + 1) * P], NS)
            last.then_inc(side_full[0], 1)
            conv(12)
            drained(pe, l, 0, ("pt", "s"))
            take(l, 1, ("pv", "s"))
            for b in range(NB):
                i = NB + b
                if b == 4:
                    conv(13)
                pe.wait_ge(kv_full[i % KV_RING], l * 16 * kv_loads(i % KV_RING) + (i // KV_RING) * 16 + 16)
                for h in range(H):
                    for m in range(2):
                        last = f32(qb[:, 1, h * NS + b * TS:h * NS + (b + 1) * TS],
                                   kv_slot(i)[:, m * CW + h * P:m * CW + (h + 1) * P],
                                   pT_s[:, m, h, b * TS:(b + 1) * TS], start=(m == 0), stop=(m == 1))
                last.then_inc(side_full[1] if b == NB - 1 else kv_used, 1)

            conv(14, 15)

            with pe.Fori(0, 2) as j:
                for i in range(4):
                    product(l, j * 8 + T_AM + 16 + i, j * 4 + (T_AM + 16 + i) // 2, i, *X)
                drained(pe, l, 1, ("pv", "s"))
                for i in range(4):
                    product(l, j * 8 + T_AM + 20 + i, j * 4 + (T_AM + 20 + i) // 2, i, *Y, nk=4)

            for i in range(8):
                product(l, T_WO + i, (T_WO + i) // 2, i, *M,
                        wait_k=(lambda k: pe.wait_ge(m_ready, l * 8 + k + 1)) if i == 0 else None)

            def norm_stats(x):
                first = [0, 128, 256, 384, 448]
                pe.wait_ge(sum_ready, l * 2 + x + 1)
                take(l, 0, ("sum", x))
                for t in range(5):
                    last = f32(qb[:, 0, t:t + 1], racc[:, first[t]:first[t] + P], ones)
                last.then_inc(side_full[0], 1)

                def spread(tag, col):
                    take(l, 1, tag)
                    for t in range(4):
                        last = f32(qb[:, 1, t * P:(t + 1) * P], st[:, col, t:t + 1].to_broadcast([P, P]), ident)
                    last.then_inc(side_full[1], 1)
                    take(l, 2, tag)
                    f32(qb[:, 2, 0:NS], st[:, col, 4:5].to_broadcast([P, P]),
                        ident[:, P - NS:P]).then_inc(side_full[2], 1)

                drained(pe, l, 0, ("sum", x))
                spread(("mean", x), 0)
                take(l, 3, ("sq", x))
                for k in range(KT):
                    pe.wait_ge(sq_ready, l * 16 + 8 * x + k + 1)
                    for t in range(5):
                        last = f32(qb[:, 3, t:t + 1], sq[:, k, first[t]:first[t] + P], ones,
                                   start=(k == 0 and t == 0), stop=(k == KT - 1 and t == 4), shared=True)
                last.then_inc(side_full[3], 1)
                pe.wait_ge(lrs_ready, l * 2 + x + 1)
                spread(("rstd", x), 3)

            norm_stats(0)

            with pe.Fori(0, 4) as g:
                for i in range(8):
                    product(l, g * 16 + T_FF + i, g * 8 + (T_FF + i) // 2, i, *X,
                            wait_k=(lambda k: pe.wait_ge(x_ready, l * 16 + 8 + k + 1)) if i == 0 else None)
                for i in range(8):
                    product(l, g * 16 + T_FF + 8 + i, g * 8 + (T_FF + 8 + i) // 2, i, *B,
                            wait_k=(lambda k: pe.wait_ge(hid_ready, l * 32 + g * 8 + k + 1 + 2)) if i == 0 else None)
            norm_stats(1)

    @block.scalar
    def _(act):
        act_fn = nc.scalar.activation
        act.dma_start(table_sb[:, :], table).then_inc(table_in, 16)
        act.dma_start(r[:, :, :], xT.rearrange("(k p) n -> p k n", p=P)).then_inc(x_in, 16)

        def free_pair(ins, i):
            ins.then_inc(pair_free[i % 2], 1)

        def gate_tile(l, t, i, br, tile):
            tile_is_done(act, l, t)
            ins = act_fn(halves(gate[:, i, :]), pair(i % 2), ACT.Sigmoid, bias=vcol(V_BG + br * KT + tile))
            free_pair(ins, i)

        act.wait_ge(table_in, 16)
        with act.Fori(0, DEPTH) as l:
            act.wait_ge(x_ready, l * 16 + 8)
            act.dma_start(vec[:, :], vectors[bass.ds(l, 1), :, :].rearrange("l p c -> (l p) c")).then_inc(vec_in, 16)
            act.dma_start(hist[:, :, :, :].rearrange("p a b c -> p (a b c)"),
                          conv_state[bass.ds(l, 1), :, :].rearrange("l p c -> (l p) c")).then_inc(hist_in, 16)
            for i in range(8):
                tile_is_done(act, l, T_RQK + i)
                act.wait_ge(rot_done, l * 8 + i + 1)
                act_fn(halves(rot[:, i % 2, 0, :]), pair(i % 2), ACT.Copy)
                act_fn(halves(rot[0:64, i % 2, 1, :]), gp[64:128, 2 * (i % 2):2 * (i % 2) + 2, 0:HALF], ACT.Copy)
                act_fn(halves(rot[64:128, i % 2, 1, :]), gp[0:64, 2 * (i % 2):2 * (i % 2) + 2, 0:HALF],
                       ACT.Copy).then_inc(rot_in, 1)
                act.wait_ge(rot_in, l * 8 + i + 1)
                act.sem_inc(pair_free[i % 2], 1)
            def state_in(b):
                act.dma_start(s_in(b), ret_state[bass.ds(l, 1), b, :, :, :].rearrange("l h d e -> d (l h) e")
                              ).then_inc(s_in_full[b % 3], 16)

            for b in range(3):
                state_in(b)
            for i in range(4):
                cols = slice(i * 2 * P, (i + 1) * 2 * P)
                act.wait_ge(values_done, l * 4 + i + 1)
                act_fn(v[:, 1:5, cols], gp[:, 0:2, :].rearrange("p a (b c) -> p (a b) c", b=2), ACT.Copy).then_inc(v_ready, 1)
                act.wait_ge(v_ready, l * 8 + 2 * i + 1)
                act.sem_inc(pair_free[0], 1)
                tile_is_done(act, l, T_RV + 2 * i + 1)
                act_fn(v[:, 0, cols], gp[:, 2, 0:2 * P], ACT.Copy).then_inc(v_ready, 1)
                act.wait_ge(v_ready, l * 8 + 2 * i + 2)
                act.sem_inc(pair_free[1], 1)

            def sigmoid(i):
                tile_is_done(act, l, T_RG + i)
                if i >= 2:
                    act.wait_ge(pair_free[i % 2], l * (TILES // 2) + (T_RG + i - 2) // 2 + 2)
                act_fn(halves(tmp[:, i % 2, :]), pair(i % 2), ACT.Sigmoid).then_inc(sig_in, 1)

            def root(c, p):
                act.wait_ge(var_in, l * 5 + c + 1)
                act_fn(sd[0:p, :], ve[0:p, :], ACT.Sqrt).then_inc(std_in, 1)

            act.wait_ge(vec_in, l * 16 + 16)
            act.wait_ge(rot_done, l * 8 + 8 + 2)
            for c in range(NCH):
                sigmoid(2 * c)
                root(c, P)
                sigmoid(2 * c + 1)
                for bank in (2, 3):
                    filled(act, l, bank, ("ot", c))
                    act_fn(oT[:, 4 * (bank - 2):4 * (bank - 1), NS + c * P:NS + (c + 1) * P],
                           qb[:, bank, :].rearrange("p (a b) -> p a b", a=4), ACT.Copy).then_inc(oT_ready, 1)
                    act.wait_ge(oT_ready, l * 8 + 2 * c + bank - 1)
                    act.sem_inc(side_free[bank], 1)
            drained(act, l, 0, ("kv", NCH - 1))
            drained(act, l, 1, ("kv", NCH - 1))
            act.dma_start(ret_prompt[bass.ds(l, 1), :, :, :].rearrange("l h d e -> d (l h) e"),
                          S[:, :, :]).then_inc(st_out, 16)
            gate_tile(l, T_RO, 0, 1, 0)
            for b in range(NB):
                if b == 4:
                    gate_tile(l, T_RO + 1, 1, 1, 1)
                drained(act, l, 0, ("kvs", b))
                drained(act, l, 1, ("kvs", b))
                act.dma_start(ret_sample[bass.ds(l, 1), b, :, :, :].rearrange("l h d e -> d (l h) e"),
                              s_in(b)).then_inc(s_out_done[b % 3], 16)
                if b >= 1 and b + 2 < NB:
                    act.wait_ge(s_out_done[(b - 1) % 3], l * 16 * state_loads((b - 1) % 3) + ((b - 1) // 3) * 16 + 16)
                    state_in(b + 2)
            root(NCH, NS)
            gate_tile(l, T_RO + 2, 2, 1, 2)
            gate_tile(l, T_RO + 3, 3, 1, 3)
            drained(act, l, 1, ("kvs", NB - 1))
            drained(act, l, 2, ("oT", "s"))
            act.wait_ge(st_out, l * 16 + 16)
            act.dma_start(mt_raw[:, :, :], memT.rearrange("(k p) m -> p k m", p=P)).then_inc(mem_in, 16)
            for i in range(3):
                act.wait_ge(s_out_done[i], (l + 1) * 16 * state_loads(i))
            for i in range(4):
                if i == 0:
                    act.wait_ge(pair_free[1], l * (TILES // 2) + (T_RO + 7) // 2 + 2)
                gate_tile(l, T_RO + 8 + i, i, 1, 4 + i)
            for i in range(4):
                tile_is_done(act, l, T_KV + i)
                act_fn(km[:, i, :], gp[:, 2 * (i % 2), 0:ML], ACT.Copy).then_inc(km_ready, 1)
                act.wait_ge(km_ready, l * 8 + i + 1)
                act.sem_inc(pair_free[i % 2], 1)
            for i in (0, 2):
                tile_is_done(act, l, T_KV + 5 + i)
                for m in range(2):
                    act_fn(vm[:, m, i * P:(i + 2) * P], gp[:, 2 * m, 0:2 * P], ACT.Copy).then_inc(km_ready, 1)
                    act.wait_ge(km_ready, l * 8 + 4 + i + m + 1)
                    act.sem_inc(pair_free[m], 1)
            act.dma_start(kT_new[bass.ds(l, 1), :, :, :].rearrange("l p h m -> (l p) h m"), km[:, :, :]).then_inc(km_out, 16)
            act.dma_start(v_new[bass.ds(l, 1), :, :].rearrange("l (m p) c -> p (l m) c", p=P), vm[:, :, :]).then_inc(km_out, 16)
            for t0, buf, s in ((T_MQ, mq, mq_ready), (T_CC, cc, cc_in)):
                for i in range(4):
                    tile_is_done(act, l, t0 + i)
                    act_fn(halves(buf[:, i, :]), pair(i % 2), ACT.Copy).then_inc(s, 1)
                    act.wait_ge(s, l * 4 + i + 1)
                    act.sem_inc(pair_free[i % 2], 1)
            act.wait_ge(z_ready, l * 4 + 4)
            act.dma_start(conv_new[bass.ds(l, 1), :, :].rearrange("l p c -> (l p) c"),
                          tail[:, :, :].rearrange("p a b -> p (a b)")).then_inc(tail_out, 16)

            def cache_in(i):
                src = (kT_cache[bass.ds(l, 1), i, :, :].rearrange("l p c -> (l p) c") if i < NB else
                       v_cache[bass.ds(l, 1), i - NB, :, :].rearrange("l (m p) c -> p (l m) c", p=P))
                dst = kv_slot(i) if i < NB else kv_slot(i).rearrange("p (m c) -> p m c", m=2)
                act.dma_start(dst, src).then_inc(kv_full[i % KV_RING], 16)

            def cache_next(i):
                old = i - KV_RING
                if old == NB - 1:
                    filled(act, l, 0, ("qk", "s"))
                else:
                    act.wait_ge(kv_used, l * 14 + old + 1 - (old >= NB))
                cache_in(i)

            for i in range(KV_RING):
                cache_in(i)

            def conv_gate(n):
                gate_tile(l, T_AM + n, n % 4, 0, n // 8 * 4 + n % 4)

            def exps(n, banks, width, p, out):
                act.wait_ge(nb_ready, l * 5 + n + 1)
                for t in range(4):
                    ins = act_fn(out[0:p, t, :], qb[0:p, banks[t // 2], (t % 2) * ML:(t % 2 + 1) * ML], ACT.Exp,
                                 bias=nb[0:p, n % 2, t:t + 1], scale=ATT_SCALE, accum_out=rs[0:p, n % 2, t:t + 1])
                    if t % 2:
                        ins.then_inc(side_free[banks[t // 2]], 1)

            def head_exps(h):
                b0 = 2 * (h % 2)
                exps(h, (b0, b0 + 1), ML, P, pr[:, h % 2, :, :])

            def transposed(h):
                b0 = 2 * (h % 2)
                for m in range(2):
                    filled(act, l, b0 + m, ("pt", h))
                    if m == 0 and h > 0:
                        filled(act, l, 2 - b0, ("pv", h - 1))
                    act_fn(pT[:, m, :], qb[:, b0 + m, :], ACT.Copy).then_inc(side_free[b0 + m], 1)

            head_exps(0)
            head_exps(1)
            conv_gate(0)
            conv_gate(1)
            transposed(0)
            conv_gate(2)
            transposed(1)
            conv_gate(3)
            head_exps(2)
            transposed(2)
            head_exps(3)
            transposed(3)
            act.wait_ge(pair_free[1], l * (TILES // 2) + (T_AM + 7) // 2 + 2)
            conv_gate(8)
            for i in range(KV_RING, KV_RING + 3):
                cache_next(i)
            conv_gate(9)
            for i in range(KV_RING + 3, 2 * KV_RING + 3):
                cache_next(i)
            conv_gate(10)
            exps(4, (2, 3), ML, NS, pr_s)
            conv_gate(11)
            filled(act, l, 0, ("pt", "s"))
            act_fn(pT_s[:, :, :, :].rearrange("p a b c -> p (a b c)"), qb[:, 0, :], ACT.Copy).then_inc(side_free[0], 1)
            for i in range(2 * KV_RING + 3, 2 * NB):
                cache_next(i)
            act.wait_ge(km_out, l * 32 + 32)
            act.wait_ge(tail_out, l * 16 + 16)
            for j in range(2):
                for i in range(4):
                    if i == 0:
                        act.wait_ge(pair_free[1], l * (TILES // 2) + (T_AM + 8 + 8 * j + 7) // 2 + 2)
                    gate_tile(l, T_AM + 16 + 8 * j + i, i, 2, 4 * j + i)

            def norm(x):
                def spread(tag):
                    filled(act, l, 1, tag)
                    act_fn(row[:, 0:SEQ], qb[:, 1, :], ACT.Copy).then_inc(side_free[1], 1)
                    filled(act, l, 2, tag)
                    act_fn(row[:, SEQ:N], qb[:, 2, 0:NS], ACT.Copy).then_inc(side_free[2], 1)

                spread(("mean", x))
                for k in range(KT):
                    act.wait_ge(d_ready, l * 16 + 8 * x + k + 1)
                    act_fn(sq[:, k, :], r[:, k, :], ACT.Square).then_inc(sq_ready, 1)
                act.wait_ge(lvar_in, l * 2 + x + 1)
                act_fn(st[:, 2, :], st[:, 1, :], ACT.Sqrt).then_inc(lstd_in, 1)
                spread(("rstd", x))
                b = (V_LB1, V_LB2)[x]
                for k in range(KT):
                    act.wait_ge(y1_ready, l * 16 + 8 * x + k + 1)
                    act_fn(x_hi[:, k, :], r[:, k, :], ACT.Identity, bias=vcol(b + k)).then_inc(xh_in, 1)
                for k in range(KT):
                    act.wait_ge(x_ready, l * 16 + 8 * x + 8 + k + 1)
                    ins = act_fn(r[:, k, :], r[:, k, :], ACT.Identity, bias=vcol(b + k))
                    if x == 0:
                        ins.then_inc(act_step, 1)
                        act.wait_ge(act_step, k + 1)
                        ins = act_fn(r[:, k, :], r[:, k, :], ACT.Copy, scale=ALPHA)
                    ins.then_inc(r_ready, 1)

            act.sem_clear(act_step)
            norm(0)
            with act.Fori(0, 4) as g:
                for i in range(8):
                    tile_is_done(act, l, g * 16 + T_FF + i)
                    act.wait_ge(hid_ready, l * 32 + g * 8 + i + 1)
                    act_fn(halves(relu[:, i % 2, :]), pair(i % 2), ACT.Relu).then_inc(relu_in, 1)
                    act.wait_ge(relu_in, l * 32 + g * 8 + i + 1)
                    act.sem_inc(pair_free[i % 2], 1)
            norm(1)
            act.wait_ge(r_ready, l * 16 + 16)

    @block.vector
    def _(dve):
        vec_ = nc.vector
        steps = [0]

        def link(ins):
            steps[0] += 1
            ins.then_inc(dve_step, 1)
            dve.wait_ge(dve_step, steps[0])

        def split(hi, lo, x):
            link(vec_.tensor_copy(hi, x))
            return vec_.tensor_tensor(lo, x, hi.bitcast(F32), ALU.subtract)

        for i in range(2):
            dve.sem_inc(pair_free[i], 1)
        for i in range(4):
            dve.sem_inc(side_free[i], 1)
        dve.sem_inc(rot_done, 2)
        dve.sem_inc(hid_ready, 2)
        dve.wait_ge(x_in, 16)
        for k in range(KT):
            split(x_hi[:, k, :], x_lo[:, k, :], r[:, k, :]).then_inc(x_ready, 1)
        dve.wait_ge(table_in, 16)
        dve.wait_ge(x_ready, 8)
        with dve.Fori(0, DEPTH) as l:
            dve.sem_clear(dve_step)
            steps[0] = 0
            for i in range(8):
                dst = (qT if i < 4 else kT)[:, i % 4, :]
                dve.wait_ge(rot_in, l * 8 + i + 1)
                link(vec_.tensor_tensor(rot[:, i % 2, 0, :], rot[:, i % 2, 0, :], table_sb[:, K_COS:K_COS + N], ALU.mult))
                link(vec_.tensor_tensor(rot[:, i % 2, 1, :], rot[:, i % 2, 1, :], table_sb[:, K_SIN:K_SIN + N], ALU.mult))
                vec_.tensor_tensor(dst, rot[:, i % 2, 0, :], rot[:, i % 2, 1, :], ALU.add).then_inc(rot_done, 1)
            def swish(i):
                dve.wait_ge(sig_in, l * 8 + i + 1)
                vec_.scalar_tensor_tensor(halves(sil[:, i, :]), pair(i % 2), vcol(V_GN + i), halves(tmp[:, i % 2, :]),
                                          ALU.mult, ALU.mult).then_inc(pair_free[i % 2], 1)

            dve.wait_ge(vec_in, l * 16 + 16)

            def group_norm(c, p, between=lambda: None):
                for h in range(H):
                    if h % 2 == 0:
                        filled(dve, l, 2 + h // 2, ("o", c))
                    ins = vec_.bn_stats(bst[0:p, h, :], qb[0:p, 2 + h // 2, (h % 2) * DV:(h % 2 + 1) * DV])
                link(ins)
                for h in range(H):
                    ins = vec_.bn_aggr(mv[0:p, h, :], bst[0:p, h, :])
                link(ins)
                vec_.tensor_scalar(ve[0:p, :], mv[0:p, :, 1], GN_EPS, None, ALU.add).then_inc(var_in, 1)
                between()
                n = c if c != "s" else NCH
                dve.wait_ge(std_in, l * 5 + n + 1)
                link(vec_.reciprocal(rstd[0:p, :], sd[0:p, :]))
                for h in range(H):
                    ins = vec_.tensor_scalar(on[0:p, h, :], qb[0:p, 2 + h // 2, (h % 2) * DV:(h % 2 + 1) * DV],
                                             mv[0:p, h, 0:1], rstd[0:p, h:h + 1], ALU.subtract, ALU.mult)
                    if h % 2:
                        ins.then_inc(side_free[2 + h // 2], 1)

            link(vec_.memset(S[:, :, :], 0.0))
            for c in range(NCH):
                cols = slice(NS + c * P, NS + (c + 1) * P)
                dve.wait_ge(rot_done, l * 8 + 8 + 2)
                link(vec_.tensor_tensor(qd[:, :, :], qT[:, :, cols], const3(K_QDP, H, P), ALU.mult))
                filled(dve, l, 0, ("sc", c))
                vec_.tensor_tensor(sc[:, :, :], qb[:, 0, :].rearrange("p (a b) -> p a b", a=H),
                                   const3(K_DMP, H, P), ALU.mult).then_inc(side_free[0], 1)
                filled(dve, l, 1, ("kt", c))
                vec_.tensor_tensor(kn[:, :].rearrange("p (a b) -> p a b", a=H), qb[:, 1, :].rearrange("p (a b) -> p a b", a=H),
                                   const3(K_KDP, H, 1).to_broadcast([P, H, P]), ALU.mult).then_inc(side_free[1], 1)
                swish(2 * c)

                def state():
                    for bank in (0, 1):
                        filled(dve, l, bank, ("kv", c))
                        for h in (2 * bank, 2 * bank + 1):
                            ins = vec_.scalar_tensor_tensor(S[:, h, :], S[:, h, :], G_CHUNK[h],
                                                            qb[:, bank, (h % 2) * DV:(h % 2 + 1) * DV], ALU.mult, ALU.add)
                        ins.then_inc(side_free[bank], 1)

                group_norm(c, P, between=state)
                swish(2 * c + 1)
                drained(dve, l, 1, ("kv", c))

            def gated(k):
                if k == 0:
                    dve.wait_ge(oT_ready, l * 8 + 8)
                    dve.wait_ge(pair_free[1], l * (TILES // 2) + (T_RG + 7) // 2 + 2)
                t = tmp[:, k % 2, 0:SEQ]
                link(vec_.tensor_tensor(t, oT[:, k, NS:N], sil[:, k, NS:N], ALU.mult))
                split(b_hi[:, k, NS:N], b_lo[:, k, NS:N], t).then_inc(b_ready, 1)

            link(vec_.tensor_tensor(qd[:, :, 0:NS], qT[:, :, 0:NS], const3(K_QDS, H, NS), ALU.mult))
            filled(dve, l, 0, ("sc", "s"))
            vec_.tensor_tensor(sc[0:NS, :, 0:NS], qb[0:NS, 0, 0:H * NS].rearrange("p (a b) -> p a b", a=H),
                               const3(K_DMS, H, NS, NS), ALU.mult).then_inc(side_free[0], 1)
            filled(dve, l, 1, ("kt", "s"))
            keys = prod[0:NS, :]
            vec_.tensor_copy(keys, qb[0:NS, 1, :]).then_inc(side_free[1], 1)
            drained(dve, l, 1, ("kt", "s"))
            for b in range(NB):
                dst = (kn, kb1)[b % 2]
                if b >= 2:
                    filled(dve, l, 1, ("kvs", b - 2))
                vec_.tensor_tensor(dst[0:NS, :].rearrange("p (a b) -> p a b", a=H), keys.rearrange("p (a b) -> p a b", a=H),
                                   const3(K_KDS + b * H, H, 1, NS).to_broadcast([NS, H, P]), ALU.mult).then_inc(knb_ready, 1)
                if b >= 1:
                    state_of = b - 1
                    for bank in (0, 1):
                        filled(dve, l, bank, ("kvs", state_of))
                        for h in (2 * bank, 2 * bank + 1):
                            s = s_in(state_of)[:, h, :]
                            ins = vec_.scalar_tensor_tensor(s, s, G_TS[h], qb[:, bank, (h % 2) * DV:(h % 2 + 1) * DV],
                                                            ALU.mult, ALU.add)
                        ins.then_inc(side_free[bank], 1)
                gated(b)
            for bank in (0, 1):
                filled(dve, l, bank, ("kvs", NB - 1))
                for h in (2 * bank, 2 * bank + 1):
                    s = s_in(NB - 1)[:, h, :]
                    ins = vec_.scalar_tensor_tensor(s, s, G_TS[h], qb[:, bank, (h % 2) * DV:(h % 2 + 1) * DV],
                                                    ALU.mult, ALU.add)
                ins.then_inc(side_free[bank], 1)
            filled(dve, l, 2, ("oT", "s"))
            vec_.tensor_copy(sc[:, :, :].rearrange("p a b -> p (a b)"), qb[:, 2, :]).then_inc(side_free[2], 1)
            group_norm("s", NS)
            filled(dve, l, 2, ("ot", "s"))
            p8 = prod[:, :].rearrange("p (a b) -> p a b", a=KT)
            vec_.tensor_tensor(p8, qb[:, 2, :].rearrange("p (a b) -> p a b", a=KT), sil[:, :, 0:NS],
                               ALU.mult).then_inc(side_free[2], 1)
            drained(dve, l, 2, ("ot", "s"))
            split(b_hi[:, :, 0:NS], b_lo[:, :, 0:NS], p8).then_inc(b_ready, 1)

            dve.wait_ge(mem_in, l * 16 + 16)
            split(mt_hi[:, :, :], mt_lo[:, :, :], mt_raw[:, :, :]).then_inc(mem_split, 1)
            dve.wait_ge(st_out, l * 16 + 16)
            dve.wait_ge(b_ready, l * 9 + 9)
            for j in range(2):
                for i in range(4):
                    tile_is_done(dve, l, T_RO + 8 * j + 4 + i)
                    vec_.tensor_tensor(halves(r[:, 4 * j + i, :]), pair(i % 2), halves(gate[:, i, :]),
                                       ALU.mult).then_inc(pair_free[i % 2], 1)

            dve.wait_ge(hist_in, l * 16 + 16)
            for i in range(4):
                u = up[:, i % 2, :]
                us = u[:, 0:NB * (TS + 2)].rearrange("p (b t) -> p b t", b=NB)
                upr = u[:, NB * (TS + 2):PAD]
                tile_is_done(dve, l, T_CH + i)
                dve.wait_ge(cc_in, l * 4 + i + 1)
                link(vec_.tensor_copy(us[:, :, 0:2], hist[:, i, :, :]))
                link(vec_.memset(upr[:, 0:2], 0.0))
                b0 = 2 * (i % 2)
                c3 = cc[:, i, :]
                link(vec_.tensor_tensor(us[:, :, 2:TS + 2], gp[:, b0, 0:NS].rearrange("p (b t) -> p b t", b=NB),
                                        c3[:, 0:NS].rearrange("p (b t) -> p b t", b=NB), ALU.mult))
                link(vec_.tensor_tensor(upr[:, 2:2 + HALF - NS], gp[:, b0, NS:HALF], c3[:, NS:HALF], ALU.mult))
                vec_.tensor_tensor(upr[:, 2 + HALF - NS:2 + SEQ], gp[:, b0 + 1, 0:HALF], c3[:, HALF:N],
                                   ALU.mult).then_inc(pair_free[i % 2], 1)
                dve.wait_ge(pair_free[i % 2], l * (TILES // 2) + (T_CH + i) // 2 + 2)
                link(vec_.tensor_copy(tail[:, i, 0:2 * NB].rearrange("p (b t) -> p b t", b=NB), us[:, :, TS:TS + 2]))
                link(vec_.tensor_copy(tail[:, i, 2 * NB:2 * NB + 2], upr[:, SEQ:SEQ + 2]))
                for w in range(3):
                    wc = vcol(V_CONV + 4 * w + i)
                    for dst, src in ((c3[:, 0:NS].rearrange("p (b t) -> p b t", b=NB), us[:, :, w:w + TS]),
                                     (c3[:, NS:N], upr[:, w:w + SEQ])):
                        if w == 0:
                            ins = vec_.tensor_scalar(dst, src, wc, None, ALU.mult)
                        else:
                            ins = vec_.scalar_tensor_tensor(dst, src, wc, dst, ALU.mult, ALU.add)
                    link(ins)
            for i in range(4):
                tile_is_done(dve, l, T_CB + i)
                vec_.tensor_tensor(halves(cc[:, i, :]), pair(i % 2), halves(cc[:, i, :]), ALU.mult).then_inc(pair_free[i % 2], 1)
                dve.wait_ge(pair_free[i % 2], l * (TILES // 2) + (T_CB + i) // 2 + 2)
                split(b_hi[:, i, :], b_lo[:, i, :], cc[:, i, :]).then_inc(z_ready, 1)

            def maxima(n, view, p):
                link(vec_.reduce_max(mx[0:p, n % 2, :], view, axis=AX.X))
                vec_.tensor_scalar(nb[0:p, n % 2, :], mx[0:p, n % 2, :], -ATT_SCALE, None, ALU.mult).then_inc(nb_ready, 1)

            def scores(b0, p):
                return qb[0:p, b0:b0 + 2, :].rearrange("p a (b c) -> p (a b) c", b=2)

            def normalise(n, buf, p):
                link(vec_.reciprocal(ri[0:p, n % 2, :], rs[0:p, n % 2, :]))
                for t in range(4):
                    ins = vec_.tensor_scalar(buf[0:p, t, :], buf[0:p, t, :], ri[0:p, n % 2, t:t + 1], None, ALU.mult)
                ins.then_inc(p_ready, 1)

            def head_max(h):
                for bank in (0, 1):
                    filled(dve, l, 2 * (h % 2) + bank, ("qk", h))
                maxima(h, scores(2 * (h % 2), P), P)

            def head_norm(h):
                for bank in (0, 1):
                    drained(dve, l, 2 * (h % 2) + bank, ("qk", h))
                normalise(h, pr[:, h % 2, :, :], P)

            def head_out(h):
                b0 = 2 * (h % 2)
                filled(dve, l, b0, ("pv", h))
                link(vec_.tensor_copy(b_hi[:, 4 + h, NS:N], qb[:, b0, :]))
                vec_.tensor_tensor(b_lo[:, 4 + h, NS:N], qb[:, b0, :], b_hi[:, 4 + h, NS:N].bitcast(F32),
                                   ALU.subtract).then_inc(side_free[b0], 1)

            def branch_out(br, n):
                t, m, i = T_AM + 16 * br + 4 + n // 4 * 8 + n % 4, n, n % 4
                tile_is_done(dve, l, t)
                vec_.tensor_tensor(halves(tmp[:, i % 2, :]), pair(i % 2), halves(gate[:, i, :]),
                                   ALU.mult).then_inc(pair_free[i % 2], 1)
                dve.wait_ge(pair_free[i % 2], l * (TILES // 2) + t // 2 + 2)
                link(vec_.tensor_tensor(r[:, m, :], r[:, m, :], tmp[:, i % 2, :], ALU.add))
                if br == 1:
                    split(m_hi[:, m, :], m_lo[:, m, :], r[:, m, :]).then_inc(m_ready, 1)

            head_max(0)
            head_max(1)
            head_norm(0)
            head_norm(1)
            head_out(0)
            head_max(2)
            head_out(1)
            branch_out(0, 0)
            head_norm(2)
            branch_out(0, 1)
            head_max(3)
            branch_out(0, 2)
            head_norm(3)
            head_out(2)
            branch_out(0, 3)
            head_out(3)
            filled(dve, l, 0, ("qk", "s"))
            vec_.tensor_copy(sT[:, :, :, :].rearrange("p a b c -> p (a b c)"), qb[:, 0, :]).then_inc(side_free[0], 1)
            filled(dve, l, 2, ("sn", "s"))
            filled(dve, l, 3, ("sn", "s"))
            maxima(4, scores(2, NS), NS)
            drained(dve, l, 2, ("sn", "s"))
            drained(dve, l, 3, ("sn", "s"))
            normalise(4, pr_s, NS)
            branch_out(0, 4)
            branch_out(0, 5)
            filled(dve, l, 1, ("pv", "s"))
            o4 = qb[:, 1, 0:H * NS].rearrange("p (a b) -> p a b", a=H)
            link(vec_.tensor_copy(b_hi[:, 4:8, 0:NS], o4))
            vec_.tensor_tensor(b_lo[:, 4:8, 0:NS], o4, b_hi[:, 4:8, 0:NS].bitcast(F32), ALU.subtract).then_inc(side_free[1], 1)
            branch_out(0, 6)
            branch_out(0, 7)
            for n in range(KT):
                branch_out(1, n)
            dve.wait_ge(km_out, l * 32 + 32)
            dve.wait_ge(m_ready, l * 8 + 8)
            for m in range(KT):
                t = T_WO + m
                tile_is_done(dve, l, t)
                vec_.scalar_tensor_tensor(halves(r[:, m, :]), halves(x_hi[:, m, :].bitcast(F32)), ALPHA, pair(m % 2),
                                          ALU.mult, ALU.add).then_inc(pair_free[m % 2], 1)
                dve.wait_ge(pair_free[m % 2], l * (TILES // 2) + t // 2 + 2)
                link(vec_.scalar_tensor_tensor(r[:, m, :], x_lo[:, m, :].bitcast(F32), ALPHA, r[:, m, :], ALU.mult, ALU.add))
                if m == 0:
                    link(vec_.tensor_copy(racc[:, :], r[:, 0, :]))
                elif m < KT - 1:
                    link(vec_.tensor_tensor(racc[:, :], racc[:, :], r[:, m, :], ALU.add))
                else:
                    vec_.tensor_tensor(racc[:, :], racc[:, :], r[:, m, :], ALU.add).then_inc(sum_ready, 1)

            def norm(x):
                filled(dve, l, 0, ("sum", x))
                vec_.tensor_scalar(st[:, 0, :], qb[:, 0, 0:5], -1.0 / D, None, ALU.mult).then_inc(side_free[0], 1)
                drained(dve, l, 1, ("mean", x))
                drained(dve, l, 2, ("mean", x))
                for k in range(KT):
                    vec_.tensor_tensor(r[:, k, :], r[:, k, :], row[:, :], ALU.add).then_inc(d_ready, 1)
                filled(dve, l, 3, ("sq", x))
                link(vec_.tensor_scalar(st[:, 1, :], qb[:, 3, 0:5], 1.0 / D, LN_EPS, ALU.mult, ALU.add))
                dve.sem_inc(side_free[3], 1)
                dve.sem_inc(lvar_in, 1)
                dve.wait_ge(lstd_in, l * 2 + x + 1)
                vec_.reciprocal(st[:, 3, :], st[:, 2, :]).then_inc(lrs_ready, 1)
                drained(dve, l, 1, ("rstd", x))
                drained(dve, l, 2, ("rstd", x))
                g, b = ((V_LG1, V_LB1), (V_LG2, V_LB2))[x]

                def low(k):
                    dve.wait_ge(xh_in, l * 16 + 8 * x + k + 1)
                    vec_.scalar_tensor_tensor(x_lo[:, k, :], r[:, k, :], vcol(b + k), x_hi[:, k, :].bitcast(F32),
                                              ALU.add, ALU.subtract).then_inc(x_ready, 1)

                for k in range(KT):
                    vec_.scalar_tensor_tensor(r[:, k, :], r[:, k, :], vcol(g + k), row[:, :], ALU.mult,
                                              ALU.mult).then_inc(y1_ready, 1)
                    if k:
                        low(k - 1)
                low(KT - 1)

            norm(0)

            base = steps[0]

            def group(g, first_step, last):
                n = [0]

                def glink(ins):
                    n[0] += 1
                    ins.then_inc(dve_step, 1)
                    dve.wait_ge(dve_step, first_step + n[0])

                for i in range(8):
                    dve.wait_ge(relu_in, l * 32 + g * 8 + i + 1)
                    t = relu[:, i % 2, :]
                    glink(vec_.tensor_tensor(t, t, t, ALU.mult))
                    glink(vec_.tensor_copy(b_hi[:, i, :], t))
                    vec_.tensor_tensor(b_lo[:, i, :], t, b_hi[:, i, :].bitcast(F32), ALU.subtract).then_inc(hid_ready, 1)
                dve.wait_ge(r_ready, l * 16 + 8)
                for m in range(KT):
                    tile_is_done(dve, l, g * 16 + T_FF + 8 + m)
                    vec_.tensor_tensor(halves(r[:, m, :]), halves(r[:, m, :]), pair(m % 2), ALU.add).then_inc(pair_free[m % 2], 1)
                    if last:
                        dve.wait_ge(pair_free[m % 2], l * (TILES // 2) + g * 8 + (T_FF + 8 + m) // 2 + 2)
                        if m == 0:
                            glink(vec_.tensor_copy(racc[:, :], r[:, 0, :]))
                        elif m < KT - 1:
                            glink(vec_.tensor_tensor(racc[:, :], racc[:, :], r[:, m, :], ALU.add))
                        else:
                            vec_.tensor_tensor(racc[:, :], racc[:, :], r[:, m, :], ALU.add).then_inc(sum_ready, 1)
                return n[0]

            with dve.Fori(0, 3) as g:
                per = group(g, g * 16 + base, False)
                assert per == 16
            group(3, base + 3 * per, True)
            steps[0] = base + 3 * per + per + KT - 1
            norm(1)
            dve.wait_ge(x_ready, l * 16 + 24)

    block_cm.__exit__(None, None, None)


def state_loads(slot):
    return len(range(slot, NB, 3))


def kv_loads(slot):
    return len(range(slot, 2 * NB, KV_RING))


def shape_table():
    t = np.zeros((P, K_ALL), np.float32)
    pos = np.concatenate([np.tile(4096 + np.arange(TS), NB), np.arange(SEQ)]).astype(np.float32)
    inv = (10000.0 ** (-np.arange(64, dtype=np.float64) / 64)).astype(np.float32)
    ang = (pos[None, :] * inv[:, None]).astype(np.float32).astype(np.float64)
    t[:, K_COS:K_COS + N] = np.concatenate([np.cos(ang)] * 2)
    t[:, K_SIN:K_SIN + N] = np.concatenate([-np.sin(ang), np.sin(ang)])
    g = np.array(LOG_G)
    j, i = np.arange(P)[:, None, None], np.arange(P)[None, None, :]
    keep = np.where(i >= j, np.exp(np.maximum(i - j, 0) * g[None, :, None]), 0.0) * RET_SCALE
    t[:, K_DMP:K_DMP + H * P] = keep.reshape(P, -1)
    js, is_ = j[:NS], i[:, :, :NS]
    same = (js // TS == is_ // TS)
    t[:NS, K_DMS:K_DMS + H * NS] = (keep[:NS, :, :NS] * same).reshape(NS, -1)
    t[:, K_QDP:K_QDP + H * P] = np.exp((np.arange(P)[None] + 1.0) * g[:, None]).reshape(1, -1)
    t[:, K_QDS:K_QDS + H * NS] = np.exp((np.arange(NS)[None] % TS + 1.0) * g[:, None]).reshape(1, -1)
    t[:, K_KDP:K_KDP + H] = np.exp((CHUNK - 1.0 - np.arange(P))[:, None] * g[None]) * RET_SCALE
    kd = np.exp((TS - 1.0 - np.arange(NS) % TS)[:, None, None] * g[None, None]) * RET_SCALE
    own = (np.arange(NS)[:, None] // TS == np.arange(NB)[None])[:, :, None]
    t[:NS, K_KDS:K_KDS + H * NB] = (kd * own).reshape(NS, -1)
    t[:, K_ID:K_ID + P] = np.eye(P)
    t[:, K_ONE] = 1.0
    return t


def kernel(**inputs):
    import concourse.bacc as bacc
    from concourse.bass_utils import run_bass_kernel_spmd

    a = {k: np.asarray(x) for k, x in inputs.items()}
    c = np.ascontiguousarray

    def columns(x):
        return x.reshape(DEPTH, -1, P).transpose(0, 2, 1)

    ins = {
        "xT": c(np.concatenate([a["x_sample"].reshape(NS, D), a["x_prompt"].reshape(SEQ, D)]).T),
        "memT": c(a["mem_prompt"].reshape(ML, D).T),
        "kT_cache": c(a["cache_mem_k"].transpose(0, 1, 4, 3, 2).reshape(DEPTH, NB, P, H * ML)),
        "v_cache": c(a["cache_mem_v"].reshape(DEPTH, NB, ML, CW)),
        "conv_state": c(a["state_conv"].reshape(DEPTH, NB, 2, 4, P).transpose(0, 4, 3, 1, 2).reshape(DEPTH, P, 64)),
        "ret_state": c(a["state_ret"]),
    }
    for w in ("w_in", "w_conv_out", "w_ret_out", "w_mem_out", "w_out", "w_mem_kv", "w_up", "w_down"):
        ins[w] = c(a[w])
    ins["vectors"] = c(np.concatenate(
        [columns(a["b_gate"]), columns(a["ret_gn_g"]), columns(a["conv_w"].reshape(DEPTH, -1)), columns(a["ln1_g"]),
         columns(a["ln1_b"]), columns(a["ln2_g"]), columns(a["ln2_b"])], axis=2))
    ins["table"] = shape_table()
    outs = {"yT": (D, N), "kT_new": (DEPTH, P, H, ML), "v_new": (DEPTH, ML, CW), "conv_new": (DEPTH, P, 72),
            "ret_prompt": (DEPTH, H, DK, DV), "ret_sample": (DEPTH, NB, H, DK, DV)}

    nc = bacc.Bacc("TRN2", target_bir_lowering=False, num_devices=1, dynamic_dma_scratch_size=1024)
    args = [nc.dram_tensor(f"in_{n}", x.shape, F32, kind="ExternalInput").ap() for n, x in ins.items()]
    args += [nc.dram_tensor(f"out_{n}", s, F32, kind="ExternalOutput").ap() for n, s in outs.items()]
    layers(nc, *args)
    res = run_bass_kernel_spmd(nc, [{f"in_{n}": x for n, x in ins.items()}], core_ids=[0]).results[0]
    o = {n: res[f"out_{n}"] for n in outs}
    y = o["yT"].T
    conv = o["conv_new"].reshape(DEPTH, P, 4, NB + 1, 2).transpose(0, 3, 4, 2, 1).reshape(DEPTH, NB + 1, 2, CW)
    return (c(y[NS:]).reshape(1, SEQ, D), c(y[:NS]).reshape(NB, TS, D),
            c(o["kT_new"].transpose(0, 3, 2, 1)).reshape(DEPTH, 1, ML, H, P),
            o["v_new"].reshape(DEPTH, 1, ML, H, P),
            c(conv[:, NB:]), o["ret_prompt"].reshape(DEPTH, 1, H, DK, DV),
            c(conv[:, :NB]), o["ret_sample"])
```

```python
import numpy as np
import concourse.bass as bass
from concourse import mybir

F32 = mybir.dt.float32
F32R = mybir.dt.float32r
ALU = mybir.AluOpType
ACT = mybir.ActivationFunctionType
AX = mybir.AxisListType

DEPTH = 2
D = 1024
SEQ, NB, TS = 512, 8, 8
NS = NB * TS
N = NS + SEQ
HALF = N // 2
P = 128
KT = D // P
CW, H, DK, DV, ML = 512, 4, 128, 256, 256
CHUNK = 128
NCH = SEQ // CHUNK
ALPHA = (2 * DEPTH) ** 0.25
LN_EPS, GN_EPS = 1e-5, 1e-6
ATT_SCALE = P ** -0.5
RET_SCALE = DK ** -0.5
LOG_G = [float(np.log1p(-np.exp2(-5.0 - h))) for h in range(H)]
G_CHUNK = [float(np.exp(CHUNK * g)) for g in LOG_G]
G_TS = [float(np.exp(TS * g)) for g in LOG_G]
PAD = NB * (TS + 2) + SEQ + 2

C_CB, C_CC, C_CH, C_RQ, C_MQ, C_GATE = 0, 512, 1024, 1536, 4608, 5120

T_RQK, T_RV, T_RG, T_RO, T_KV, T_MQ, T_CC, T_CH, T_CB = 0, 8, 16, 24, 40, 48, 52, 56, 60
T_AM, T_WO, T_FF, TILES = 64, 96, 104, 168
STATE_RING = 5
KV_RING = 5
SHIFT_TILES = 3
RING = 4
PIECE = KT * P

K_COS = 0
K_SIN = K_COS + N
K_DMP = K_SIN + N
K_DMS = K_DMP + H * P
K_QDP = K_DMS + H * NS
K_QDS = K_QDP + H * P
K_KDP = K_QDS + H * NS
K_KDS = K_KDP + H
K_ID = K_KDS + H * NB
K_MEAN = K_ID + P
K_ALL = K_MEAN + P

V_BG, V_GN, V_CONV, V_LG1, V_LB1, V_LG2, V_LB2 = 0, 24, 32, 44, 52, 60, 68
V_ALL = 76

SIDE = [[], [], [], []]
for _c in range(NCH):
    SIDE[0] += [("sc", _c), ("kv", _c)]
    SIDE[1] += [("kt", _c), ("kv", _c)]
    SIDE[2] += [("o", _c), ("ot", _c)]
    SIDE[3] += [("o", _c), ("ot", _c)]
SIDE[0] += [("sc", "s")] + [("kvs", _b) for _b in range(NB)]
SIDE[1] += [("kt", "s")] + [("kvs", _b) for _b in range(NB)]
SIDE[2] += [("o", "s"), ("ot", "s")]
SIDE[3] += [("o", "s")]
for _h in range(H):
    for _b in (0, 1):
        SIDE[2 * (_h % 2) + _b] += [("qk", _h), ("pt", _h)] + [("pv", _h)] * (_b == 0)
SIDE[0] += [("pt", "s"), ("vt", "s")]
SIDE[1] += [("pv", "s")]
SIDE[2] += [("qk", "s")]
SIDE[3] += [("qk", "s")]
for _x in range(2):
    SIDE[0] += [("shift", _x), ("mean", _x)]
    SIDE[1] += [("shift", _x), ("mean", _x)]
    SIDE[2] += [("sq", _x)]
    SIDE[3] += [("sq", _x)]


def use(l, bank, tag):
    return l * len(SIDE[bank]) + SIDE[bank].index(tag) + 1


def layers(nc, xT, memT, kT_cache, v_cache, conv_state, ret_state, w_in, w_conv_out, w_ret_out,
           w_mem_out, w_out, w_mem_kv, w_up, w_down, vectors, table,
           yT, kT_new, v_new, conv_new, ret_prompt, ret_sample):
    at = [(nc.sbuf_base + 31) // 32 * 32]

    def place(name, shape, dt, offset=None):
        size = 4 * int(np.prod(shape[1:]))
        if offset is None:
            offset, at[0] = at[0], at[0] + (size + 31) // 32 * 32
        return nc.alloc_sbuf_tensor_at(name, shape, dt, offset=offset)

    def here():
        return at[0]

    stage = place("stage", [P, 2, KT, 2 * P], F32)
    w_hi = place("w_hi", [P, RING, PIECE], F32R)
    w_lo = place("w_lo", [P, RING, PIECE], F32R)
    x_hi = place("x_hi", [P, KT, N], F32R)
    x_lo = place("x_lo", [P, KT, N], F32R)
    a_bhi = here()
    b_hi = place("b_hi", [P, KT, N], F32R)
    a_blo = here()
    b_lo = place("b_lo", [P, KT, N], F32R)
    rot = place("rot", [P, 2, 2, N], F32, a_bhi)
    oT = place("oT", [P, KT, N], F32, a_bhi)
    sil = place("sil", [P, KT, N], F32, a_blo)
    a_r = here()
    r = place("r", [P, KT, N], F32)
    kn = place("kn", [P, H * P], F32, a_r)
    qd = place("qd", [P, H, P], F32, a_r + 2048)
    sc = place("sc", [P, H, P], F32, a_r + 4096)
    kb1 = place("kb1", [P, H * P], F32, a_r + 6144)
    S = place("S", [P, H, DV], F32, a_r + 8192)
    on = place("on", [P, H, DV], F32, a_r + 12288)
    prod = place("prod", [P, 512], F32, a_r + 16384)
    a_g = here()
    gate = place("gate", [P, 4, N], F32)
    place("gate_rest", [P, 4096 - 4 * N], F32)
    s_in_g = place("s_in_g", [P, H, DV], F32, a_g + 16 * N)
    up = place("up", [P, 2, PAD], F32, a_g)
    a_c = here()
    place("C", [P, 11776], F32)

    def c_at(name, shape, dt, first):
        return place(name, shape, dt, a_c + 4 * first)

    qT = c_at("qT", [P, H, N], F32, 0)
    kT = c_at("kT", [P, H, N], F32, 2304)
    v = c_at("v", [P, 5, H * DV], F32, 4608)
    km = c_at("km", [P, H, ML], F32, 9728)
    vm = c_at("vm", [P, 2, CW], F32, 10752)
    s_in_c = c_at("s_in_c", [P, 2, H, DV], F32, 9728)
    s_in_v = c_at("s_in_v", [P, 2, H, DV], F32, 7680)
    q_of = c_at("q_of", [P, NB, H, NS], F32, 5632)
    mt_hi = c_at("mt_hi", [P, KT, ML], F32R, 0)
    mt_lo = c_at("mt_lo", [P, KT, ML], F32R, 2304)
    mt_raw = c_at("mt_raw", [P, KT, ML], F32, 4608)
    mq = c_at("mq", [P, H, N], F32, 0)
    cc = c_at("cc", [P, H, N], F32, 2304)
    pr = c_at("pr", [P, 2, 4, ML], F32, 4608)
    mq_of = c_at("mq_of", [P, NB, H, NS], F32, 4608)
    p_of = [c_at("p_of0", [P, 4, 2, H, NS], F32, 0), c_at("p_of1", [P, 4, 2, H, NS], F32, 4608)]
    pr_s = c_at("pr_s", [P, H, ML], F32, 5632)
    pT = c_at("pT", [P, 2, SEQ], F32, 6656)
    ov = c_at("ov", [P, CW], F32, 6656)
    kv_c = c_at("kv_c", [P, 2, 1024], F32, 7680)
    kv_z = c_at("kv_z", [P, 2, 1024], F32, 2304)
    kv_g = place("kv_g", [P, 1024], F32, a_g + 16 * N)
    m_hi = c_at("m_hi", [P, KT, N], F32R, 0)
    m_lo = c_at("m_lo", [P, KT, N], F32R, 4608)
    relu = c_at("relu", [P, 2, N], F32, 0)
    y = c_at("y", [P, KT, N], F32, 2 * N)
    shift = c_at("shift", [P, N], F32, 9728)
    racc, dacc, sqacc, var, inv = (place(n, [P, N], F32, a_g + 4 * N * i)
                                   for i, n in enumerate(("racc", "dacc", "sqacc", "var", "inv")))
    sq = place("sq", [P, 2, N], F32, a_g + 20 * N)
    table_sb = place("table_sb", [P, K_ALL], F32)
    vec = place("vec", [P, V_ALL], F32)
    tmp = place("tmp", [P, 2, N], F32)
    hist = place("hist", [P, H, NB, 2], F32)
    tail = place("tail", [P, H, 2 * (NB + 1)], F32)
    mx = place("mx", [P, 2, H], F32)
    nb = place("nb", [P, 2, H], F32)
    rs = place("rs", [P, 2, H], F32)
    ri = place("ri", [P, 2, H], F32)
    bst = place("bst", [P, H, 6], F32)
    mv = place("mv", [P, H, 2], F32)
    ve = place("ve", [P, H], F32)
    sd = place("sd", [P, H], F32)
    rstd = place("rstd", [P, H], F32)
    warm = place("warm", [P, 1], F32)
    assert at[0] <= nc.sbuf_usable_end, (at[0], nc.sbuf_usable_end)

    ident = table_sb[:, K_ID:K_ID + P]
    per_d = table_sb[:, K_MEAN:K_MEAN + P]

    def const3(first, a, b, p=P):
        return table_sb[0:p, first:first + a * b].rearrange("p (a b) -> p a b", a=a)

    def vcol(i):
        return vec[:, i:i + 1]

    def s_in(b):
        b %= STATE_RING
        return s_in_c[:, b, :, :] if b < 2 else s_in_g[:, :, :] if b == 2 else s_in_v[:, b - 3, :, :]

    def kv_slot(i):
        i %= KV_RING
        return kv_c[:, i, :] if i < 2 else kv_z[:, i - 2, :] if i < 4 else kv_g[:, :]

    gp = nc.alloc_psum_tensor("gp", [P, 4, 512], F32)
    qb = nc.alloc_psum_tensor("qb", [P, 4, 512], F32)

    def pair(par):
        return gp[:, 2 * par:2 * par + 2, 0:HALF]

    def halves(ap):
        return ap.rearrange("p (a b) -> p a b", a=2)

    sem = nc.alloc_semaphore
    split_done = sem("split_done")
    tile_done = sem("tile_done")
    pair_free = [sem(f"pair_free{i}") for i in range(2)]
    stage_full = [sem(f"stage_full{i}") for i in range(2)]
    hi_done = sem("hi_done")
    split_begun = sem("split_begun")
    side_full = [sem(f"side_full{i}") for i in range(4)]
    side_free = [sem(f"side_free{i}") for i in range(4)]
    dve_step = sem("dve_step")
    act_step = sem("act_step")
    table_in, vec_in, hist_in, mem_in = (sem(n) for n in ("table_in", "vec_in", "hist_in", "mem_in"))
    x_in = [sem(f"x_in{k}") for k in range(KT)]
    s_in_full = [sem(f"s_in_full{i}") for i in range(STATE_RING)]
    s_out_done = [sem(f"s_out_done{i}") for i in range(STATE_RING)]
    values_done = sem("values_done")
    oT_ready = sem("oT_ready")
    kv_full = [sem(f"kv_full{i}") for i in range(KV_RING)]
    kv_used = sem("kv_used")
    x_ready = sem("x_ready")
    mem_split = sem("mem_split")
    km_ready = sem("km_ready")
    rot_in = sem("rot_in")
    rot_done = sem("rot_done")
    v_ready = sem("v_ready")
    sig_in = sem("sig_in")
    mq_ready = sem("mq_ready")
    cc_in = sem("cc_in")
    z_ready = sem("z_ready")
    knb_ready = sem("knb_ready")
    var_in = sem("var_in")
    std_in = sem("std_in")
    b_ready = sem("b_ready")
    mq_masked = sem("mq_masked")
    p_masked = sem("p_masked")
    nb_ready = sem("nb_ready")
    p_ready = sem("p_ready")
    m_ready = sem("m_ready")
    sum_ready = sem("sum_ready")
    shift_in = sem("shift_in")
    d_ready = sem("d_ready")
    sq_ready = sem("sq_ready")
    sq_added = sem("sq_added")
    rest_in = sem("rest_in")
    lvar_in, lstd_in = sem("lvar_in"), sem("lstd_in")
    centred = sem("centred")
    y1_ready = sem("y1_ready")
    xh_in = sem("xh_in")
    r_ready = sem("r_ready")
    y_ready = sem("y_ready")
    relu_in = sem("relu_in")
    hid_ready = sem("hid_ready")
    km_out, st_out, tail_out, y_out = sem("km_out"), sem("st_out"), sem("tail_out"), sem("y_out")

    def filled(eng, l, bank, tag):
        eng.wait_ge(side_full[bank], use(l, bank, tag))

    def drained(eng, l, bank, tag):
        eng.wait_ge(side_free[bank], use(l, bank, tag) + 1)

    def tile_is_done(eng, l, t):
        eng.wait_ge(tile_done, l * TILES + t + 1 + RING)

    block_cm = nc.Block()
    block = block_cm.__enter__()

    @block.sync
    def _(sp):
        def load(l, t, half, src):
            sp.wait_ge(split_done, l * TILES + t + 2)
            rows = src.shape[0] * src.shape[1] // P
            sp.dma_start(stage[:, half, 0:rows, :], src.rearrange("l (k p) c -> p (l k) c", p=P)).then_inc(stage_full[half], 16)

        def four(l, t, w, col, rows=slice(0, D)):
            for i in range(2):
                load(l, t + 2 * i, i, w[bass.ds(l, 1), rows, bass.ds(col + i * 2 * P, 2 * P)])

        with sp.Fori(0, DEPTH) as l:
            with sp.Fori(0, 6) as j:
                four(l, j * 4 + T_RQK, w_in, j * 512 + C_RQ)
            with sp.Fori(0, 2) as j:
                four(l, j * 8 + T_RO, w_in, j * 512 + C_GATE + D)
                four(l, j * 8 + T_RO + 4, w_ret_out, j * 512)
            with sp.Fori(0, 2) as j:
                four(l, j * 4 + T_KV, w_mem_kv, j * 512)
            four(l, T_MQ, w_in, C_MQ)
            four(l, T_CC, w_in, C_CC)
            with sp.Fori(0, 2) as j:
                four(l, j * 4 + T_CH, w_in, j * (C_CB - C_CH) + C_CH)
            for br, w in ((0, w_conv_out), (1, w_mem_out)):
                with sp.Fori(0, 2) as j:
                    four(l, j * 8 + T_AM + 16 * br, w_in, j * 512 + C_GATE + 2 * D * br)
                    four(l, j * 8 + T_AM + 16 * br + 4, w, j * 512, slice(0, CW))
            with sp.Fori(0, 2) as j:
                four(l, j * 4 + T_WO, w_out, j * 512)
            with sp.Fori(0, 4) as g:
                with sp.Fori(0, 2) as j:
                    four(l, g * 16 + j * 4 + T_FF, w_up, g * D + j * 512)
                with sp.Fori(0, 2) as j:
                    four(l, g * 16 + j * 4 + T_FF + 8, w_down, j * 512, bass.ds(g * D, D))
        for k in range(KT):
            sp.wait_ge(y_ready, (DEPTH - 1) * KT + k + 1)
            sp.dma_start(yT[k * P:(k + 1) * P, :], y[:, k, :]).then_inc(y_out, 16)
        sp.wait_ge(y_out, 16 * KT)
        sp.wait_ge(km_out, 32 * DEPTH)
        sp.wait_ge(st_out, 16 * DEPTH)
        sp.wait_ge(tail_out, 16 * DEPTH)
        for i in range(STATE_RING):
            sp.wait_ge(s_out_done[i], 16 * state_loads(i) * DEPTH)

    @block.gpsimd
    def _(pool):
        pool.sem_inc(split_done, RING)

        def split_four(l, first):
            n = l * TILES + first
            for s in range(RING):
                pool.wait_ge(tile_done, n + s + 1)
                if s % 2 == 0:
                    pool.wait_ge(stage_full[s // 2], l * (TILES * 4) + first * 4 + 16)
                pool.sem_inc(split_begun, 1)
                raw = stage[:, s // 2, :, (s % 2) * P:(s % 2 + 1) * P]
                hi, lo = (w[:, s, :].rearrange("p (k c) -> p k c", k=KT) for w in (w_hi, w_lo))
                nc.gpsimd.tensor_scalar(hi, raw, 1.0, 1.0, ALU.mult, ALU.mult).then_inc(hi_done, 1)
                pool.wait_ge(hi_done, n + s + 1)
                nc.gpsimd.tensor_tensor(lo, raw, hi.bitcast(F32), ALU.subtract).then_inc(split_done, 1)

        def centre(l, x):
            pool.wait_ge(rest_in, l * 6 + 3 * x + 3)
            for k in range(KT):
                nc.gpsimd.tensor_tensor(r[:, k, :], r[:, k, :], racc[:, :], ALU.subtract).then_inc(centred, 1)

        def layer(l, last):
            with pool.Fori(0, T_FF // RING) as it:
                split_four(l, it * RING + RING)
            centre(l, 0)
            with pool.Fori(0, (TILES - T_FF) // RING - 1 - last) as it:
                split_four(l, it * RING + T_FF + RING)
            if not last:
                split_four(l, TILES - RING + RING)
            else:
                split_four(l, TILES - RING)
            centre(l, 1)

        split_four(0, 0)
        with pool.Fori(0, DEPTH - 1) as l:
            layer(l, False)
        layer(DEPTH - 1, True)

    @block.tensor
    def _(pe):
        mm = nc.tensor.matmul
        pe.sem_inc(tile_done, RING)

        def product(l, t, half_t, i, hi, lo, nk=KT, wait_k=None):
            pe.wait_ge(split_done, l * TILES + t + 1 + RING)
            pe.wait_ge(pair_free[i % 2], l * (TILES // 2) + half_t + 1)
            n, last = 0, None
            for k in range(nk):
                if wait_k is not None:
                    wait_k(k)
                for w, x in ((w_hi, hi), (w_hi, lo), (w_lo, hi)):
                    for half in range(2):
                        last = mm(gp[:, 2 * (i % 2) + half, 0:HALF], w[:, i % 4, k * P:(k + 1) * P],
                                  x(k, half), start=(n == 0), stop=(n == 3 * nk - 1))
                    n += 1
            last.then_inc(tile_done, 1)

        def two_products(l, t, half_t, hi, lo, wait_k):
            behind = 3
            for step in range(KT + behind):
                for i, k in enumerate((step, step - behind)):
                    if not 0 <= k < KT:
                        continue
                    if k == 0:
                        pe.wait_ge(split_done, l * TILES + t + i + 1 + RING)
                        pe.wait_ge(pair_free[i], l * (TILES // 2) + half_t + 1)
                    if i == 0:
                        wait_k(k)
                    for n, (w, x) in enumerate(((w_hi, hi), (w_hi, lo), (w_lo, hi))):
                        for half in range(2):
                            last = mm(gp[:, 2 * i + half, 0:HALF], w[:, i, k * P:(k + 1) * P], x(k, half),
                                      start=(k == n == 0), stop=(k == KT - 1 and n == 2))
                    if k == KT - 1:
                        last.then_inc(tile_done, 1)

        def tiles_of(buf, first=None):
            def get(k, half):
                if first is None:
                    return buf[:, k, half * HALF:(half + 1) * HALF]
                return buf[:, bass.ds(first + k, 1), half * HALF:(half + 1) * HALF].rearrange("p a b -> p (a b)")
            return get

        X = (tiles_of(x_hi), tiles_of(x_lo))
        B = (tiles_of(b_hi), tiles_of(b_lo))
        M = (tiles_of(m_hi), tiles_of(m_lo))

        def take(l, bank, tag):
            pe.wait_ge(side_free[bank], use(l, bank, tag))

        def f32(out, lhsT, rhs, start=True, stop=True, shared=False):
            return mm(out, lhsT, rhs, start=start, stop=stop, **({"skip_group_check": True} if shared else {}))

        def transpose(out, in_, p=P):
            return nc.tensor.transpose(out, in_, ident[0:p, 0:p])

        def flip(out, in_, p=P):
            return f32(out, in_, ident[0:p, 0:p])

        with pe.Fori(0, DEPTH) as l:
            two_products(l, T_RQK, T_RQK // 2, *X, wait_k=lambda k: pe.wait_ge(x_ready, l * 16 + k + 1))
            for i in range(2, 8):
                product(l, T_RQK + i, (T_RQK + i) // 2, i, *X)
            with pe.Fori(0, 2) as j:
                for i in (0, 2):
                    pe.wait_ge(split_done, l * TILES + j * 4 + T_RV + i + 2 + RING)
                    for t in (1, 2, 3, 4, 0):
                        first = 0 if t == 0 else NS + (t - 1) * P
                        if t == 1:
                            pe.wait_ge(pair_free[0], l * (TILES // 2) + j * 2 + (T_RV + i) // 2 + 1)
                        elif t == 0:
                            pe.wait_ge(pair_free[1], l * (TILES // 2) + j * 2 + (T_RV + i) // 2 + 1)
                        out = gp[:, 2, 0:2 * P] if t == 0 else gp[:, (t - 1) // 2, (t - 1) % 2 * 2 * P:((t - 1) % 2 + 1) * 2 * P]
                        n = 0
                        for k in range(KT):
                            for x, w in ((x_hi, w_hi), (x_hi, w_lo), (x_lo, w_hi)):
                                last = mm(out, x[:, k, first:first + P], w[:, i:i + 2, k * P:(k + 1) * P],
                                          start=(n == 0), stop=(n == 3 * KT - 1))
                                n += 1
                        if t == 4:
                            last.then_inc(values_done, 1)
                    last.then_inc(tile_done, 2)
            def swish(i):
                product(l, T_RG + i, (T_RG + i) // 2, i, *X)

            pe.wait_ge(table_in, 16)
            pe.wait_ge(rot_done, l * 8 + 8 + 2)
            pe.wait_ge(v_ready, l * 8 + 8)
            for c in range(NCH):
                cols = slice(NS + c * P, NS + (c + 1) * P)
                take(l, 0, ("sc", c))
                for h in range(H):
                    last = f32(qb[:, 0, h * P:(h + 1) * P], kT[:, h, cols], qT[:, h, cols])
                last.then_inc(side_full[0], 1)
                take(l, 1, ("kt", c))
                for h in range(H):
                    last = transpose(qb[:, 1, h * P:(h + 1) * P], kT[:, h, cols])
                last.then_inc(side_full[1], 1)
                swish(2 * c)
                drained(pe, l, 0, ("sc", c))
                for bank in (2, 3):
                    take(l, bank, ("o", c))
                    for h in (2 * bank - 4, 2 * bank - 3):
                        out = qb[:, bank, (h % 2) * DV:(h % 2 + 1) * DV]
                        last = f32(out, sc[:, h, :], v[:, c + 1, h * DV:(h + 1) * DV], stop=(c == 0))
                        if c > 0:
                            last = f32(out, qd[:, h, :], S[:, h, :], start=False)
                    last.then_inc(side_full[bank], 1)
                drained(pe, l, 1, ("kt", c))
                for bank in (0, 1):
                    take(l, bank, ("kv", c))
                    for h in (2 * bank, 2 * bank + 1):
                        last = f32(qb[:, bank, (h % 2) * DV:(h % 2 + 1) * DV], kn[:, h * P:(h + 1) * P],
                                   v[:, c + 1, h * DV:(h + 1) * DV])
                    last.then_inc(side_full[bank], 1)
                swish(2 * c + 1)
                for bank in (2, 3):
                    take(l, bank, ("ot", c))
                    for i in range(4):
                        n = 4 * (bank - 2) + i
                        last = transpose(qb[:, bank, i * P:(i + 1) * P], on[:, n // 2, (n % 2) * P:(n % 2 + 1) * P])
                    last.then_inc(side_full[bank], 1)

            def sample_out(h):
                return qb[0:NS, 2 + h // 2, (h % 2) * DV:(h % 2 + 1) * DV]

            def ret_gate(i):
                product(l, T_RO + i, (T_RO + i) // 2, i, *X)

            take(l, 0, ("sc", "s"))
            for h in range(H):
                last = f32(qb[0:NS, 0, h * NS:(h + 1) * NS], kT[:, h, 0:NS], qT[:, h, 0:NS])
            last.then_inc(side_full[0], 1)
            take(l, 1, ("kt", "s"))
            for h in range(H):
                last = flip(qb[0:NS, 1, h * P:(h + 1) * P], kT[:, h, 0:NS])
            last.then_inc(side_full[1], 1)
            ret_gate(0)
            drained(pe, l, 0, ("sc", "s"))
            for bank in (2, 3):
                take(l, bank, ("o", "s"))
            for b in range(NB):
                if b == 4:
                    ret_gate(1)
                pe.wait_ge(s_in_full[b % STATE_RING],
                           l * 16 * state_loads(b % STATE_RING) + (b // STATE_RING) * 16 + 16)
                for h in range(H):
                    last = f32(sample_out(h), q_of[:, b, h, :], s_in(b)[:, h, :], start=(b == 0 and h % 2 == 0),
                               stop=(b == NB - 1 and h % 2 == 1), shared=True)
                    if b == NB - 1 and h % 2:
                        last.then_inc(side_full[2 + h // 2], 1)
                if b == 0:
                    for h in range(H):
                        f32(sample_out(h), sc[0:NS, h, 0:NS], v[0:NS, 0, h * DV:(h + 1) * DV],
                            start=False, stop=False, shared=True)
                pe.wait_ge(knb_ready, l * NB + b + 1)
                keys = (kn, kb1)[b % 2]
                for bank in (0, 1):
                    take(l, bank, ("kvs", b))
                    for h in (2 * bank, 2 * bank + 1):
                        last = f32(qb[:, bank, (h % 2) * DV:(h % 2 + 1) * DV], keys[0:NS, h * P:(h + 1) * P],
                                   v[0:NS, 0, h * DV:(h + 1) * DV])
                    last.then_inc(side_full[bank], 1)
            ret_gate(2)
            drained(pe, l, 3, ("o", "s"))
            take(l, 2, ("ot", "s"))
            for n in range(8):
                last = flip(qb[:, 2, n * NS:(n + 1) * NS], on[0:NS, n // 2, (n % 2) * P:(n % 2 + 1) * P], NS)
            last.then_inc(side_full[2], 1)

            ret_gate(3)

            pe.wait_ge(b_ready, l * 9 + 9)
            for i in range(4):
                product(l, T_RO + 4 + i, (T_RO + 4 + i) // 2, i, *B)
            for i in range(4):
                product(l, T_RO + 8 + i, (T_RO + 8 + i) // 2, i, *X)
            for i in range(4):
                product(l, T_RO + 12 + i, (T_RO + 12 + i) // 2, i, *B)

            pe.wait_ge(mem_split, l + 1)
            for i in range(4):
                t = T_KV + i
                pe.wait_ge(split_done, l * TILES + t + 1 + RING)
                pe.wait_ge(pair_free[i % 2], l * (TILES // 2) + t // 2 + 1)
                n = 0
                for k in range(KT):
                    for w, x in ((w_hi, mt_hi), (w_hi, mt_lo), (w_lo, mt_hi)):
                        last = mm(gp[:, 2 * (i % 2), 0:ML], w[:, i, k * P:(k + 1) * P], x[:, k, :],
                                  start=(n == 0), stop=(n == 3 * KT - 1))
                        n += 1
                last.then_inc(tile_done, 1)
            for i in (0, 2):
                t = T_KV + 4 + i
                pe.wait_ge(split_done, l * TILES + t + 2 + RING)
                for m in range(2):
                    pe.wait_ge(pair_free[m], l * (TILES // 2) + t // 2 + 1)
                    n = 0
                    for k in range(KT):
                        for x, w in ((mt_hi, w_hi), (mt_hi, w_lo), (mt_lo, w_hi)):
                            last = mm(gp[:, 2 * m, 0:2 * P], x[:, k, m * P:(m + 1) * P],
                                      w[:, i:i + 2, k * P:(k + 1) * P], start=(n == 0), stop=(n == 3 * KT - 1))
                            n += 1
                last.then_inc(tile_done, 2)

            with pe.Fori(0, 4) as j:
                for i in range(4):
                    product(l, j * 4 + T_MQ + i, j * 2 + (T_MQ + i) // 2, i, *X)

            Z = (tiles_of(b_hi, 0), tiles_of(b_lo, 0))
            Y = (tiles_of(b_hi, 4), tiles_of(b_lo, 4))

            def conv(*tiles):
                for n in tiles:
                    product(l, T_AM + n, (T_AM + n) // 2, n, *(Z if n // 4 % 2 else X), nk=4 if n // 4 % 2 else KT)

            pe.wait_ge(mq_ready, l * 4 + 4)
            pe.wait_ge(km_ready, l * 8 + 8)

            def qk(h):
                b0 = 2 * (h % 2)
                for bank in (0, 1):
                    take(l, b0 + bank, ("qk", h))
                    for t in (2 * bank, 2 * bank + 1):
                        last = f32(qb[:, b0 + bank, (t % 2) * ML:(t % 2 + 1) * ML],
                                   mq[:, h, NS + t * P:NS + (t + 1) * P], km[:, h, :])
                    last.then_inc(side_full[b0 + bank], 1)

            def pt(h):
                b0 = 2 * (h % 2)
                pe.wait_ge(p_ready, l * 5 + h + 1)
                for m in (0, 1):
                    take(l, b0 + m, ("pt", h))
                    for t in range(4):
                        last = transpose(qb[:, b0 + m, t * P:(t + 1) * P], pr[:, h % 2, t, m * P:(m + 1) * P])
                    last.then_inc(side_full[b0 + m], 1)

            def pv(h):
                b0 = 2 * (h % 2)
                drained(pe, l, b0, ("pt", h))
                drained(pe, l, b0 + 1, ("pt", h))
                for m in (0, 1):
                    last = f32(qb[:, b0, :], vm[:, m, h * P:(h + 1) * P], pT[:, m, :], start=(m == 0), stop=(m == 1))
                last.then_inc(side_full[b0], 1)

            qk(0)
            qk(1)
            conv(0, 1)
            pt(0)
            conv(2)
            pv(0)
            pt(1)
            conv(3)
            qk(2)
            pv(1)
            pe.wait_ge(z_ready, l * 4 + 4)
            conv(4, 5)
            qk(3)
            pt(2)
            conv(6)
            pv(2)
            conv(7)
            pt(3)
            conv(8)
            pv(3)

            conv(9)
            for bank in (2, 3):
                take(l, bank, ("qk", "s"))
            pe.wait_ge(mq_masked, l + 1)
            for b in range(NB):
                pe.wait_ge(kv_full[b % KV_RING], l * 16 * kv_loads(b % KV_RING) + (b // KV_RING) * 16 + 16)
                for h in range(H):
                    last = f32(qb[0:NS, 2 + h // 2, (h % 2) * ML:(h % 2 + 1) * ML], mq_of[:, b, h, :],
                               kv_slot(b)[:, h * ML:(h + 1) * ML], start=(b == 0 and h % 2 == 0),
                               stop=(b == NB - 1 and h % 2 == 1), shared=True)
                    if b == NB - 1 and h % 2:
                        last.then_inc(side_full[2 + h // 2], 1)
                if b < NB - 1:
                    last.then_inc(kv_used, 1)
            conv(10)
            conv(11)
            pe.wait_ge(p_ready, l * 5 + 5)
            take(l, 0, ("pt", "s"))
            for n in range(2 * H):
                m, h = n // H, n % H
                last = flip(qb[:, 0, n * NS:(n + 1) * NS], pr_s[0:NS, h, m * P:(m + 1) * P], NS)
            last.then_inc(side_full[0], 1)
            conv(12)
            take(l, 1, ("pv", "s"))
            for b in range(NB):
                i = NB + b
                if b == 0:
                    pe.wait_ge(p_masked, l + 1)
                if b == 4:
                    conv(13)
                    drained(pe, l, 0, ("pt", "s"))
                pe.wait_ge(kv_full[i % KV_RING], l * 16 * kv_loads(i % KV_RING) + (i // KV_RING) * 16 + 16)
                for m in range(2):
                    for h in range(H):
                        last = f32(qb[0:NS, 1, h * P:(h + 1) * P], p_of[b // 4][:, b % 4, m, h, :],
                                   kv_slot(i)[:, m * CW + h * P:m * CW + (h + 1) * P],
                                   start=(b == m == h == 0), stop=(b == NB - 1 and m == 1 and h == H - 1), shared=True)
                last.then_inc(side_full[1] if b == NB - 1 else kv_used, 1)
            conv(14)
            drained(pe, l, 1, ("pv", "s"))
            take(l, 0, ("vt", "s"))
            for h in range(H):
                last = flip(qb[:, 0, h * NS:(h + 1) * NS], ov[0:NS, h * P:(h + 1) * P], NS)
            last.then_inc(side_full[0], 1)
            conv(15)

            with pe.Fori(0, 2) as j:
                for i in range(4):
                    product(l, j * 8 + T_AM + 16 + i, j * 4 + (T_AM + 16 + i) // 2, i, *X)
                drained(pe, l, 0, ("vt", "s"))
                for i in range(4):
                    product(l, j * 8 + T_AM + 20 + i, j * 4 + (T_AM + 20 + i) // 2, i, *Y, nk=4)

            def average(banks, rows, start=True, stop=True):
                for half, bank in enumerate(banks):
                    last = f32(qb[:, bank, 0:HALF], per_d, rows[:, half * HALF:(half + 1) * HALF], start=start, stop=stop)
                    if stop:
                        last.then_inc(side_full[bank], 1)

            def norm_shift(x):
                pe.wait_ge(sum_ready, l * 4 + 2 * x + 1)
                for bank in (0, 1):
                    take(l, bank, ("shift", x))
                average((0, 1), racc)

            def norm_stats(x):
                pe.wait_ge(sum_ready, l * 4 + 2 * x + 2)
                for bank in (0, 1):
                    take(l, bank, ("mean", x))
                average((0, 1), dacc, stop=False)
                pe.wait_ge(sq_added, l * 12 + 6 * x + 6)
                for bank in (2, 3):
                    take(l, bank, ("sq", x))
                average((2, 3), sqacc, stop=False)
                pe.wait_ge(d_ready, l * 16 + 8 * x + 8)
                average((0, 1), r[:, KT - 1, :], start=False)
                pe.wait_ge(sq_ready, l * 16 + 8 * x + 8)
                average((2, 3), sq[:, (KT - 1) % 2, :], start=False)

            for i in range(8):
                if i == SHIFT_TILES + 1:
                    norm_shift(0)
                product(l, T_WO + i, (T_WO + i) // 2, i, *M,
                        wait_k=(lambda k: pe.wait_ge(m_ready, l * 8 + k + 1)) if i == 0 else None)
            norm_stats(0)

            def mlp(g, first=False, last=False):
                if first:
                    two_products(l, T_FF, T_FF // 2, *X, wait_k=lambda k: pe.wait_ge(x_ready, l * 16 + 8 + k + 1))
                for i in range(2 * first, 8):
                    product(l, g * 16 + T_FF + i, g * 8 + (T_FF + i) // 2, i, *X)
                for i in range(8):
                    if last and i == SHIFT_TILES + 1:
                        norm_shift(1)
                    product(l, g * 16 + T_FF + 8 + i, g * 8 + (T_FF + 8 + i) // 2, i, *B,
                            wait_k=(lambda k: pe.wait_ge(hid_ready, l * 32 + g * 8 + k + 1 + 2)) if i == 0 else None)

            mlp(0, first=True)
            with pe.Fori(1, 3) as g:
                mlp(g)
            mlp(3, last=True)
            norm_stats(1)

    @block.scalar
    def _(act):
        act_fn = nc.scalar.activation
        for k in range(KT):
            act.dma_start(r[:, k, :], xT[k * P:(k + 1) * P, :]).then_inc(x_in[k], 16)
        act.dma_start(table_sb[:, :], table).then_inc(table_in, 16)

        def free_pair(ins, i):
            ins.then_inc(pair_free[i % 2], 1)

        def gate_tile(l, t, i, br, tile):
            tile_is_done(act, l, t)
            ins = act_fn(halves(gate[:, i, :]), pair(i % 2), ACT.Sigmoid, bias=vcol(V_BG + br * KT + tile))
            free_pair(ins, i)

        with act.Fori(0, DEPTH) as l:
            act.wait_ge(x_ready, l * 16 + 8)
            act.dma_start(vec[:, :], vectors[bass.ds(l, 1), :, :].rearrange("l p c -> (l p) c")).then_inc(vec_in, 16)
            act.dma_start(hist[:, :, :, :].rearrange("p a b c -> p (a b c)"),
                          conv_state[bass.ds(l, 1), :, :].rearrange("l p c -> (l p) c")).then_inc(hist_in, 16)
            for i in range(8):
                tile_is_done(act, l, T_RQK + i)
                act.wait_ge(rot_done, l * 8 + i + 1)
                act_fn(halves(rot[:, i % 2, 0, :]), pair(i % 2), ACT.Copy)
                act_fn(halves(rot[0:64, i % 2, 1, :]), gp[64:128, 2 * (i % 2):2 * (i % 2) + 2, 0:HALF], ACT.Copy)
                act_fn(halves(rot[64:128, i % 2, 1, :]), gp[0:64, 2 * (i % 2):2 * (i % 2) + 2, 0:HALF],
                       ACT.Copy).then_inc(rot_in, 1)
                act.wait_ge(rot_in, l * 8 + i + 1)
                act.sem_inc(pair_free[i % 2], 1)
            def state_in(b):
                act.dma_start(s_in(b), ret_state[bass.ds(l, 1), b, :, :, :].rearrange("l h d e -> d (l h) e")
                              ).then_inc(s_in_full[b % STATE_RING], 16)

            for b in range(3):
                state_in(b)
            for i in range(4):
                cols = slice(i * 2 * P, (i + 1) * 2 * P)
                act.wait_ge(values_done, l * 4 + i + 1)
                act_fn(v[:, 1:5, cols], gp[:, 0:2, :].rearrange("p a (b c) -> p (a b) c", b=2), ACT.Copy).then_inc(v_ready, 1)
                act.wait_ge(v_ready, l * 8 + 2 * i + 1)
                act.sem_inc(pair_free[0], 1)
                tile_is_done(act, l, T_RV + 2 * i + 1)
                act_fn(v[:, 0, cols], gp[:, 2, 0:2 * P], ACT.Copy).then_inc(v_ready, 1)
                act.wait_ge(v_ready, l * 8 + 2 * i + 2)
                act.sem_inc(pair_free[1], 1)

            def sigmoid(i):
                tile_is_done(act, l, T_RG + i)
                if i >= 2:
                    act.wait_ge(pair_free[i % 2], l * (TILES // 2) + (T_RG + i - 2) // 2 + 2)
                act_fn(halves(tmp[:, i % 2, :]), pair(i % 2), ACT.Sigmoid).then_inc(sig_in, 1)

            def root(c, p):
                act.wait_ge(var_in, l * 5 + c + 1)
                act_fn(sd[0:p, :], ve[0:p, :], ACT.Sqrt).then_inc(std_in, 1)

            act.wait_ge(vec_in, l * 16 + 16)
            act.wait_ge(rot_done, l * 8 + 8 + 2)
            for c in range(NCH):
                sigmoid(2 * c)
                root(c, P)
                sigmoid(2 * c + 1)
                for bank in (2, 3):
                    filled(act, l, bank, ("ot", c))
                    act_fn(oT[:, 4 * (bank - 2):4 * (bank - 1), NS + c * P:NS + (c + 1) * P],
                           qb[:, bank, :].rearrange("p (a b) -> p a b", a=4), ACT.Copy).then_inc(oT_ready, 1)
                    act.wait_ge(oT_ready, l * 8 + 2 * c + bank - 1)
                    act.sem_inc(side_free[bank], 1)
            drained(act, l, 0, ("kv", NCH - 1))
            drained(act, l, 1, ("kv", NCH - 1))
            act.dma_start(ret_prompt[bass.ds(l, 1), :, :, :].rearrange("l h d e -> d (l h) e"),
                          S[:, :, :]).then_inc(st_out, 16)
            for b in (3, 4):
                state_in(b)
            gate_tile(l, T_RO, 0, 1, 0)
            for b in range(NB):
                if b == 4:
                    gate_tile(l, T_RO + 1, 1, 1, 1)
                drained(act, l, 0, ("kvs", b))
                drained(act, l, 1, ("kvs", b))
                act.dma_start(ret_sample[bass.ds(l, 1), b, :, :, :].rearrange("l h d e -> d (l h) e"),
                              s_in(b)).then_inc(s_out_done[b % STATE_RING], 16)
                if b >= 1 and b - 1 + STATE_RING < NB:
                    act.wait_ge(s_out_done[b - 1], l * 16 * state_loads(b - 1) + 16)
                    state_in(b - 1 + STATE_RING)
            root(NCH, NS)
            gate_tile(l, T_RO + 2, 2, 1, 2)
            gate_tile(l, T_RO + 3, 3, 1, 3)
            drained(act, l, 1, ("kvs", NB - 1))
            act.wait_ge(st_out, l * 16 + 16)
            act.dma_start(mt_raw[:, :, :], memT.rearrange("(k p) m -> p k m", p=P)).then_inc(mem_in, 16)
            for i in range(STATE_RING):
                act.wait_ge(s_out_done[i], (l + 1) * 16 * state_loads(i))
            for i in range(4):
                if i == 0:
                    act.wait_ge(pair_free[1], l * (TILES // 2) + (T_RO + 7) // 2 + 2)
                gate_tile(l, T_RO + 8 + i, i, 1, 4 + i)
            for i in range(4):
                tile_is_done(act, l, T_KV + i)
                act_fn(km[:, i, :], gp[:, 2 * (i % 2), 0:ML], ACT.Copy).then_inc(km_ready, 1)
                act.wait_ge(km_ready, l * 8 + i + 1)
                act.sem_inc(pair_free[i % 2], 1)
            for i in (0, 2):
                tile_is_done(act, l, T_KV + 5 + i)
                for m in range(2):
                    act_fn(vm[:, m, i * P:(i + 2) * P], gp[:, 2 * m, 0:2 * P], ACT.Copy).then_inc(km_ready, 1)
                    act.wait_ge(km_ready, l * 8 + 4 + i + m + 1)
                    act.sem_inc(pair_free[m], 1)
            act.dma_start(kT_new[bass.ds(l, 1), :, :, :].rearrange("l p h m -> (l p) h m"), km[:, :, :]).then_inc(km_out, 16)
            act.dma_start(v_new[bass.ds(l, 1), :, :].rearrange("l (m p) c -> p (l m) c", p=P), vm[:, :, :]).then_inc(km_out, 16)
            for t0, buf, s in ((T_MQ, mq, mq_ready), (T_CC, cc, cc_in)):
                for i in range(4):
                    tile_is_done(act, l, t0 + i)
                    act_fn(halves(buf[:, i, :]), pair(i % 2), ACT.Copy).then_inc(s, 1)
                    act.wait_ge(s, l * 4 + i + 1)
                    act.sem_inc(pair_free[i % 2], 1)
            act.wait_ge(z_ready, l * 4 + 4)
            act.dma_start(conv_new[bass.ds(l, 1), :, :].rearrange("l p c -> (l p) c"),
                          tail[:, :, :].rearrange("p a b -> p (a b)")).then_inc(tail_out, 16)

            def cache_in(i):
                src = (kT_cache[bass.ds(l, 1), i, :, :].rearrange("l p c -> (l p) c") if i < NB else
                       v_cache[bass.ds(l, 1), i - NB, :, :].rearrange("l (m p) c -> p (l m) c", p=P))
                dst = kv_slot(i) if i < NB else kv_slot(i).rearrange("p (m c) -> p m c", m=2)
                act.dma_start(dst, src).then_inc(kv_full[i % KV_RING], 16)

            def cache_next(i):
                old = i - KV_RING
                if old == NB - 1:
                    filled(act, l, 3, ("qk", "s"))
                else:
                    act.wait_ge(kv_used, l * 14 + old + 1 - (old >= NB))
                cache_in(i)

            for i in range(KV_RING):
                cache_in(i)

            def conv_gate(n):
                gate_tile(l, T_AM + n, n % 4, 0, n // 8 * 4 + n % 4)

            def exps(n, banks, width, p, out):
                act.wait_ge(nb_ready, l * 5 + n + 1)
                for t in range(4):
                    ins = act_fn(out[0:p, t, :], qb[0:p, banks[t // 2], (t % 2) * ML:(t % 2 + 1) * ML], ACT.Exp,
                                 bias=nb[0:p, n % 2, t:t + 1], scale=ATT_SCALE, accum_out=rs[0:p, n % 2, t:t + 1])
                    if t % 2:
                        ins.then_inc(side_free[banks[t // 2]], 1)

            def head_exps(h):
                b0 = 2 * (h % 2)
                exps(h, (b0, b0 + 1), ML, P, pr[:, h % 2, :, :])

            def transposed(h):
                b0 = 2 * (h % 2)
                for m in range(2):
                    filled(act, l, b0 + m, ("pt", h))
                    if m == 0 and h > 0:
                        filled(act, l, 2 - b0, ("pv", h - 1))
                    act_fn(pT[:, m, :], qb[:, b0 + m, :], ACT.Copy).then_inc(side_free[b0 + m], 1)

            head_exps(0)
            head_exps(1)
            conv_gate(0)
            conv_gate(1)
            transposed(0)
            conv_gate(2)
            transposed(1)
            conv_gate(3)
            head_exps(2)
            transposed(2)
            head_exps(3)
            transposed(3)
            act.wait_ge(pair_free[1], l * (TILES // 2) + (T_AM + 7) // 2 + 2)
            conv_gate(8)
            conv_gate(9)
            for i in range(KV_RING, 2 * KV_RING + 3):
                cache_next(i)
            conv_gate(10)
            exps(4, (2, 3), ML, NS, pr_s)
            conv_gate(11)
            for i in range(2 * KV_RING + 3, 2 * NB):
                cache_next(i)
            filled(act, l, 1, ("pv", "s"))
            act_fn(ov[0:NS, :], qb[0:NS, 1, :], ACT.Copy).then_inc(side_free[1], 1)
            act.wait_ge(km_out, l * 32 + 32)
            act.wait_ge(tail_out, l * 16 + 16)
            for j in range(2):
                for i in range(4):
                    if i == 0:
                        act.wait_ge(pair_free[1], l * (TILES // 2) + (T_AM + 8 + 8 * j + 7) // 2 + 2)
                    gate_tile(l, T_AM + 16 + 8 * j + i, i, 2, 4 * j + i)

            def residual(k):
                act.wait_ge(x_ready, l * 16 + 8 + k + 1)
                act_fn(r[:, k, :], r[:, k, :], ACT.Identity, bias=vcol(V_LB1 + k)).then_inc(act_step, 1)
                act.wait_ge(act_step, k + 1)
                act_fn(r[:, k, :], r[:, k, :], ACT.Copy, scale=ALPHA).then_inc(r_ready, 1)

            def norm(x):
                for bank in (0, 1):
                    filled(act, l, bank, ("shift", x))
                act_fn(halves(shift[:, :]), qb[:, 0:2, 0:HALF], ACT.Copy, scale=KT / SHIFT_TILES).then_inc(shift_in, 1)
                act.wait_ge(shift_in, l * 2 + x + 1)
                for bank in (0, 1):
                    act.sem_inc(side_free[bank], 1)
                for k in range(KT):
                    act.wait_ge(d_ready, l * 16 + 8 * x + k + 1)
                    if k >= 2:
                        act.wait_ge(sq_added, l * 12 + 6 * x + max(1, k - 2))
                    act_fn(sq[:, k % 2, :], r[:, k, :], ACT.Square).then_inc(sq_ready, 1)
                    if k == KT - 2:
                        act_fn(warm[:, :], per_d[:, 0:1], ACT.Sqrt)
                for half in range(2):
                    cols = slice(half * HALF, (half + 1) * HALF)
                    filled(act, l, half, ("mean", x))
                    act_fn(shift[:, cols], qb[:, half, 0:HALF], ACT.Square).then_inc(rest_in, 1)
                for half in range(2):
                    cols = slice(half * HALF, (half + 1) * HALF)
                    act.wait_ge(lvar_in, l * 4 + 2 * x + half + 1)
                    act_fn(var[:, cols], var[:, cols], ACT.Sqrt).then_inc(lstd_in, 1)
                act.wait_ge(sum_ready, l * 4 + 2 * x + 2)
                act_fn(halves(racc[:, :]), qb[:, 0:2, 0:HALF], ACT.Copy).then_inc(rest_in, 1)
                act.wait_ge(rest_in, l * 6 + 3 * x + 3)
                for bank in (0, 1):
                    act.sem_inc(side_free[bank], 1)
                b = (V_LB1, V_LB2)[x]
                for k in range(KT):
                    act.wait_ge(y1_ready, l * 16 + 8 * x + k + 1)
                    act_fn(x_hi[:, k, :], r[:, k, :], ACT.Identity, bias=vcol(b + k)).then_inc(xh_in, 1)
                    if x == 1:
                        act_fn(y[:, k, :], r[:, k, :], ACT.Identity, bias=vcol(b + k)).then_inc(y_ready, 1)

            act.sem_clear(act_step)
            norm(0)

            def relu_tile(g, i):
                tile_is_done(act, l, g * 16 + T_FF + i)
                act.wait_ge(hid_ready, l * 32 + g * 8 + i + 1)
                act_fn(halves(relu[:, i % 2, :]), pair(i % 2), ACT.Relu).then_inc(relu_in, 1)
                act.wait_ge(relu_in, l * 32 + g * 8 + i + 1)
                act.sem_inc(pair_free[i % 2], 1)

            for i in range(8):
                relu_tile(0, i)
                residual(i)
            with act.Fori(1, 4) as g:
                for i in range(8):
                    relu_tile(g, i)
            norm(1)
            act.wait_ge(y_ready, l * 8 + 8)

    @block.vector
    def _(dve):
        vec_ = nc.vector
        steps = [0]

        def link(ins):
            steps[0] += 1
            ins.then_inc(dve_step, 1)
            dve.wait_ge(dve_step, steps[0])

        def split(hi, lo, x):
            link(vec_.tensor_copy(hi, x))
            return vec_.tensor_tensor(lo, x, hi.bitcast(F32), ALU.subtract)

        for i in range(2):
            dve.sem_inc(pair_free[i], 1)
        for i in range(4):
            dve.sem_inc(side_free[i], 1)
        dve.sem_inc(rot_done, 2)
        dve.sem_inc(hid_ready, 2)
        for k in range(KT):
            dve.wait_ge(x_in[k], 16)
            split(x_hi[:, k, :], x_lo[:, k, :], r[:, k, :]).then_inc(x_ready, 1)
        dve.wait_ge(table_in, 16)
        dve.wait_ge(x_ready, 8)
        with dve.Fori(0, DEPTH) as l:
            dve.sem_clear(dve_step)
            steps[0] = 0
            for i in range(8):
                dst = (qT if i < 4 else kT)[:, i % 4, :]
                dve.wait_ge(rot_in, l * 8 + i + 1)
                link(vec_.tensor_tensor(rot[:, i % 2, 0, :], rot[:, i % 2, 0, :], table_sb[:, K_COS:K_COS + N], ALU.mult))
                link(vec_.tensor_tensor(rot[:, i % 2, 1, :], rot[:, i % 2, 1, :], table_sb[:, K_SIN:K_SIN + N], ALU.mult))
                vec_.tensor_tensor(dst, rot[:, i % 2, 0, :], rot[:, i % 2, 1, :], ALU.add).then_inc(rot_done, 1)
            def swish(i):
                dve.wait_ge(sig_in, l * 8 + i + 1)
                vec_.scalar_tensor_tensor(halves(sil[:, i, :]), pair(i % 2), vcol(V_GN + i), halves(tmp[:, i % 2, :]),
                                          ALU.mult, ALU.mult).then_inc(pair_free[i % 2], 1)

            dve.wait_ge(vec_in, l * 16 + 16)

            def group_norm(c, p, between=lambda: None):
                for h in range(H):
                    if h % 2 == 0:
                        filled(dve, l, 2 + h // 2, ("o", c))
                    ins = vec_.bn_stats(bst[0:p, h, :], qb[0:p, 2 + h // 2, (h % 2) * DV:(h % 2 + 1) * DV])
                link(ins)
                for h in range(H):
                    ins = vec_.bn_aggr(mv[0:p, h, :], bst[0:p, h, :])
                link(ins)
                vec_.tensor_scalar(ve[0:p, :], mv[0:p, :, 1], GN_EPS, None, ALU.add).then_inc(var_in, 1)
                between()
                n = c if c != "s" else NCH
                dve.wait_ge(std_in, l * 5 + n + 1)
                link(vec_.reciprocal(rstd[0:p, :], sd[0:p, :]))
                for h in range(H):
                    ins = vec_.tensor_scalar(on[0:p, h, :], qb[0:p, 2 + h // 2, (h % 2) * DV:(h % 2 + 1) * DV],
                                             mv[0:p, h, 0:1], rstd[0:p, h:h + 1], ALU.subtract, ALU.mult)
                    if h % 2:
                        ins.then_inc(side_free[2 + h // 2], 1)

            link(vec_.memset(S[:, :, :], 0.0))
            for c in range(NCH):
                cols = slice(NS + c * P, NS + (c + 1) * P)
                dve.wait_ge(rot_done, l * 8 + 8 + 2)
                link(vec_.tensor_tensor(qd[:, :, :], qT[:, :, cols], const3(K_QDP, H, P), ALU.mult))
                filled(dve, l, 0, ("sc", c))
                vec_.tensor_tensor(sc[:, :, :], qb[:, 0, :].rearrange("p (a b) -> p a b", a=H),
                                   const3(K_DMP, H, P), ALU.mult).then_inc(side_free[0], 1)
                filled(dve, l, 1, ("kt", c))
                vec_.tensor_tensor(kn[:, :].rearrange("p (a b) -> p a b", a=H), qb[:, 1, :].rearrange("p (a b) -> p a b", a=H),
                                   const3(K_KDP, H, 1).to_broadcast([P, H, P]), ALU.mult).then_inc(side_free[1], 1)
                swish(2 * c)

                def state():
                    for bank in (0, 1):
                        filled(dve, l, bank, ("kv", c))
                        for h in (2 * bank, 2 * bank + 1):
                            ins = vec_.scalar_tensor_tensor(S[:, h, :], S[:, h, :], G_CHUNK[h],
                                                            qb[:, bank, (h % 2) * DV:(h % 2 + 1) * DV], ALU.mult, ALU.add)
                        ins.then_inc(side_free[bank], 1)

                group_norm(c, P, between=state)
                swish(2 * c + 1)
                drained(dve, l, 1, ("kv", c))

            def gated(k):
                if k == 0:
                    dve.wait_ge(oT_ready, l * 8 + 8)
                    dve.wait_ge(pair_free[1], l * (TILES // 2) + (T_RG + 7) // 2 + 2)
                t = tmp[:, k % 2, 0:SEQ]
                link(vec_.tensor_tensor(t, oT[:, k, NS:N], sil[:, k, NS:N], ALU.mult))
                split(b_hi[:, k, NS:N], b_lo[:, k, NS:N], t).then_inc(b_ready, 1)

            link(vec_.memset(q_of[:, :, :, :], 0.0))
            for b in range(NB):
                cols = slice(b * TS, (b + 1) * TS)
                ins = vec_.tensor_tensor(q_of[:, b, :, cols], qT[:, :, cols], const3(K_QDS, H, NS)[:, :, cols], ALU.mult)
            link(ins)
            filled(dve, l, 0, ("sc", "s"))
            vec_.tensor_tensor(sc[0:NS, :, 0:NS], qb[0:NS, 0, 0:H * NS].rearrange("p (a b) -> p a b", a=H),
                               const3(K_DMS, H, NS, NS), ALU.mult).then_inc(side_free[0], 1)
            filled(dve, l, 1, ("kt", "s"))
            keys = prod[0:NS, :]
            vec_.tensor_copy(keys, qb[0:NS, 1, :]).then_inc(side_free[1], 1)
            drained(dve, l, 1, ("kt", "s"))
            for b in range(NB):
                dst = (kn, kb1)[b % 2]
                if b >= 2:
                    filled(dve, l, 1, ("kvs", b - 2))
                vec_.tensor_tensor(dst[0:NS, :].rearrange("p (a b) -> p a b", a=H), keys.rearrange("p (a b) -> p a b", a=H),
                                   const3(K_KDS + b * H, H, 1, NS).to_broadcast([NS, H, P]), ALU.mult).then_inc(knb_ready, 1)
                if b >= 1:
                    state_of = b - 1
                    for bank in (0, 1):
                        filled(dve, l, bank, ("kvs", state_of))
                        for h in (2 * bank, 2 * bank + 1):
                            s = s_in(state_of)[:, h, :]
                            ins = vec_.scalar_tensor_tensor(s, s, G_TS[h], qb[:, bank, (h % 2) * DV:(h % 2 + 1) * DV],
                                                            ALU.mult, ALU.add)
                        ins.then_inc(side_free[bank], 1)
                gated(b)
            for bank in (0, 1):
                filled(dve, l, bank, ("kvs", NB - 1))
                for h in (2 * bank, 2 * bank + 1):
                    s = s_in(NB - 1)[:, h, :]
                    ins = vec_.scalar_tensor_tensor(s, s, G_TS[h], qb[:, bank, (h % 2) * DV:(h % 2 + 1) * DV],
                                                    ALU.mult, ALU.add)
                ins.then_inc(side_free[bank], 1)
            group_norm("s", NS)
            filled(dve, l, 2, ("ot", "s"))
            p8 = prod[:, :].rearrange("p (a b) -> p a b", a=KT)
            vec_.tensor_tensor(p8, qb[:, 2, :].rearrange("p (a b) -> p a b", a=KT), sil[:, :, 0:NS],
                               ALU.mult).then_inc(side_free[2], 1)
            drained(dve, l, 2, ("ot", "s"))
            split(b_hi[:, :, 0:NS], b_lo[:, :, 0:NS], p8).then_inc(b_ready, 1)

            dve.wait_ge(mem_in, l * 16 + 16)
            split(mt_hi[:, :, :], mt_lo[:, :, :], mt_raw[:, :, :]).then_inc(mem_split, 1)
            dve.wait_ge(st_out, l * 16 + 16)
            dve.wait_ge(b_ready, l * 9 + 9)
            for j in range(2):
                for i in range(4):
                    tile_is_done(dve, l, T_RO + 8 * j + 4 + i)
                    vec_.tensor_tensor(halves(r[:, 4 * j + i, :]), pair(i % 2), halves(gate[:, i, :]),
                                       ALU.mult).then_inc(pair_free[i % 2], 1)

            dve.wait_ge(hist_in, l * 16 + 16)
            for i in range(4):
                u = up[:, i % 2, :]
                us = u[:, 0:NB * (TS + 2)].rearrange("p (b t) -> p b t", b=NB)
                upr = u[:, NB * (TS + 2):PAD]
                tile_is_done(dve, l, T_CH + i)
                dve.wait_ge(cc_in, l * 4 + i + 1)
                link(vec_.tensor_copy(us[:, :, 0:2], hist[:, i, :, :]))
                link(vec_.memset(upr[:, 0:2], 0.0))
                b0 = 2 * (i % 2)
                c3 = cc[:, i, :]
                link(vec_.tensor_tensor(us[:, :, 2:TS + 2], gp[:, b0, 0:NS].rearrange("p (b t) -> p b t", b=NB),
                                        c3[:, 0:NS].rearrange("p (b t) -> p b t", b=NB), ALU.mult))
                link(vec_.tensor_tensor(upr[:, 2:2 + HALF - NS], gp[:, b0, NS:HALF], c3[:, NS:HALF], ALU.mult))
                vec_.tensor_tensor(upr[:, 2 + HALF - NS:2 + SEQ], gp[:, b0 + 1, 0:HALF], c3[:, HALF:N],
                                   ALU.mult).then_inc(pair_free[i % 2], 1)
                dve.wait_ge(pair_free[i % 2], l * (TILES // 2) + (T_CH + i) // 2 + 2)
                link(vec_.tensor_copy(tail[:, i, 0:2 * NB].rearrange("p (b t) -> p b t", b=NB), us[:, :, TS:TS + 2]))
                link(vec_.tensor_copy(tail[:, i, 2 * NB:2 * NB + 2], upr[:, SEQ:SEQ + 2]))
                for w in range(3):
                    wc = vcol(V_CONV + 4 * w + i)
                    for dst, src in ((c3[:, 0:NS].rearrange("p (b t) -> p b t", b=NB), us[:, :, w:w + TS]),
                                     (c3[:, NS:N], upr[:, w:w + SEQ])):
                        if w == 0:
                            ins = vec_.tensor_scalar(dst, src, wc, None, ALU.mult)
                        else:
                            ins = vec_.scalar_tensor_tensor(dst, src, wc, dst, ALU.mult, ALU.add)
                    link(ins)
            for i in range(4):
                tile_is_done(dve, l, T_CB + i)
                vec_.tensor_tensor(halves(cc[:, i, :]), pair(i % 2), halves(cc[:, i, :]), ALU.mult).then_inc(pair_free[i % 2], 1)
                dve.wait_ge(pair_free[i % 2], l * (TILES // 2) + (T_CB + i) // 2 + 2)
                split(b_hi[:, i, :], b_lo[:, i, :], cc[:, i, :]).then_inc(z_ready, 1)

            def maxima(n, view, p):
                link(vec_.reduce_max(mx[0:p, n % 2, :], view, axis=AX.X))
                vec_.tensor_scalar(nb[0:p, n % 2, :], mx[0:p, n % 2, :], -ATT_SCALE, None, ALU.mult).then_inc(nb_ready, 1)

            def scores(b0, p):
                return qb[0:p, b0:b0 + 2, :].rearrange("p a (b c) -> p (a b) c", b=2)

            def normalise(n, buf, p):
                link(vec_.reciprocal(ri[0:p, n % 2, :], rs[0:p, n % 2, :]))
                for t in range(4):
                    ins = vec_.tensor_scalar(buf[0:p, t, :], buf[0:p, t, :], ri[0:p, n % 2, t:t + 1], None, ALU.mult)
                ins.then_inc(p_ready, 1)

            def head_max(h):
                for bank in (0, 1):
                    filled(dve, l, 2 * (h % 2) + bank, ("qk", h))
                maxima(h, scores(2 * (h % 2), P), P)

            def head_norm(h):
                for bank in (0, 1):
                    drained(dve, l, 2 * (h % 2) + bank, ("qk", h))
                normalise(h, pr[:, h % 2, :, :], P)

            def head_out(h):
                b0 = 2 * (h % 2)
                filled(dve, l, b0, ("pv", h))
                link(vec_.tensor_copy(b_hi[:, 4 + h, NS:N], qb[:, b0, :]))
                vec_.tensor_tensor(b_lo[:, 4 + h, NS:N], qb[:, b0, :], b_hi[:, 4 + h, NS:N].bitcast(F32),
                                   ALU.subtract).then_inc(side_free[b0], 1)

            def branch_out(br, n):
                t, m, i = T_AM + 16 * br + 4 + n // 4 * 8 + n % 4, n, n % 4
                tile_is_done(dve, l, t)
                vec_.tensor_tensor(halves(tmp[:, i % 2, :]), pair(i % 2), halves(gate[:, i, :]),
                                   ALU.mult).then_inc(pair_free[i % 2], 1)
                dve.wait_ge(pair_free[i % 2], l * (TILES // 2) + t // 2 + 2)
                link(vec_.tensor_tensor(r[:, m, :], r[:, m, :], tmp[:, i % 2, :], ALU.add))
                if br == 1:
                    split(m_hi[:, m, :], m_lo[:, m, :], r[:, m, :]).then_inc(m_ready, 1)

            head_max(0)
            head_max(1)
            head_norm(0)
            head_norm(1)
            head_out(0)
            head_max(2)
            head_out(1)
            branch_out(0, 0)
            head_norm(2)
            branch_out(0, 1)
            head_max(3)
            branch_out(0, 2)
            head_norm(3)
            head_out(2)
            branch_out(0, 3)
            for bank in (2, 3):
                filled(dve, l, bank, ("pt", 3))
            link(vec_.memset(mq_of[:, :, :, :], 0.0))
            for b in range(NB):
                cols = slice(b * TS, (b + 1) * TS)
                ins = vec_.tensor_copy(mq_of[:, b, :, cols], mq[:, :, cols])
            ins.then_inc(mq_masked, 1)
            head_out(3)
            filled(dve, l, 2, ("qk", "s"))
            filled(dve, l, 3, ("qk", "s"))
            maxima(4, scores(2, NS), NS)
            vec_.memset(p_of[0][:, :, :, :, :], 0.0)
            drained(dve, l, 2, ("qk", "s"))
            drained(dve, l, 3, ("qk", "s"))
            normalise(4, pr_s, NS)

            def own_probabilities(half):
                src = qb[:, 0, :].rearrange("p (m h c) -> p m h c", m=2, h=H)
                for b in range(4):
                    cols = slice((4 * half + b) * TS, (4 * half + b + 1) * TS)
                    ins = vec_.tensor_copy(p_of[half][:, b, :, :, cols], src[:, :, :, cols])
                return ins

            filled(dve, l, 0, ("pt", "s"))
            own_probabilities(0).then_inc(p_masked, 1)
            link(vec_.memset(p_of[1][:, :, :, :, :], 0.0))
            own_probabilities(1).then_inc(side_free[0], 1)
            branch_out(0, 4)
            branch_out(0, 5)
            branch_out(0, 6)
            filled(dve, l, 0, ("vt", "s"))
            o4 = qb[:, 0, 0:H * NS].rearrange("p (a b) -> p a b", a=H)
            link(vec_.tensor_copy(b_hi[:, 4:8, 0:NS], o4))
            vec_.tensor_tensor(b_lo[:, 4:8, 0:NS], o4, b_hi[:, 4:8, 0:NS].bitcast(F32), ALU.subtract).then_inc(side_free[0], 1)
            branch_out(0, 7)
            for n in range(KT):
                branch_out(1, n)
            dve.wait_ge(m_ready, l * 8 + 8)

            def statistics(x, m, link):
                d0, s0, q0 = l * 16 + 8 * x, l * 4 + 2 * x, l * 12 + 6 * x

                def centre(k):
                    vec_.tensor_tensor(r[:, k, :], r[:, k, :], shift[:, :], ALU.subtract).then_inc(d_ready, 1)

                def shifted(k):
                    dve.wait_ge(d_ready, d0 + k)
                    dve.sem_inc(d_ready, 1)

                def add(k):
                    dve.wait_ge(d_ready, d0 + k + 1)
                    ins = vec_.tensor_tensor(dacc[:, :], dacc[:, :], r[:, k, :], ALU.add)
                    if k == KT - 2:
                        ins.then_inc(sum_ready, 1)
                    else:
                        link(ins)

                def add_square(k):
                    dve.wait_ge(sq_ready, d0 + k + 1)
                    if k > 1:
                        dve.wait_ge(sq_added, q0 + k - 1)
                    vec_.tensor_tensor(sqacc[:, :], sq[:, 0, :] if k == 1 else sqacc[:, :], sq[:, k % 2, :],
                                       ALU.add).then_inc(sq_added, 1)

                if m == 1:
                    link(vec_.tensor_tensor(racc[:, :], r[:, 0, :], r[:, 1, :], ALU.add))
                elif m == 2:
                    vec_.tensor_tensor(racc[:, :], racc[:, :], r[:, 2, :], ALU.add).then_inc(sum_ready, 1)
                elif m == 3:
                    dve.wait_ge(shift_in, l * 2 + x + 1)
                    dve.wait_ge(sum_ready, s0 + 1)
                    for k in range(SHIFT_TILES + 1):
                        centre(k)
                    link(vec_.scalar_tensor_tensor(dacc[:, :], shift[:, :], -float(SHIFT_TILES), racc[:, :],
                                                   ALU.mult, ALU.add))
                elif m == 4:
                    shifted(4)
                    add(3)
                    add(4)
                    add_square(1)
                elif m == 5:
                    shifted(5)
                    add_square(2)
                    add(5)
                    add_square(3)
                    add_square(4)
                elif m == 6:
                    shifted(6)
                    add_square(5)
                    add(6)
                    add_square(6)
                elif m == 7:
                    shifted(7)

            def less_shift(m, link):
                if m > SHIFT_TILES:
                    link(vec_.tensor_tensor(r[:, m, :], r[:, m, :], shift[:, :], ALU.subtract))

            for m in range(KT):
                t = T_WO + m
                link(vec_.tensor_scalar(r[:, m, :], x_hi[:, m, :].bitcast(F32), ALPHA, None, ALU.mult))
                link(vec_.scalar_tensor_tensor(r[:, m, :], x_lo[:, m, :].bitcast(F32), ALPHA, r[:, m, :], ALU.mult, ALU.add))
                less_shift(m, link)
                tile_is_done(dve, l, t)
                vec_.tensor_tensor(halves(r[:, m, :]), halves(r[:, m, :]), pair(m % 2), ALU.add).then_inc(pair_free[m % 2], 1)
                dve.wait_ge(pair_free[m % 2], l * (TILES // 2) + t // 2 + 2)
                statistics(0, m, link)

            def norm(x):
                for half in range(2):
                    cols = slice(half * HALF, (half + 1) * HALF)
                    dve.wait_ge(rest_in, l * 6 + 3 * x + half + 1)
                    filled(dve, l, 2 + half, ("sq", x))
                    vec_.scalar_tensor_tensor(var[:, cols], qb[:, 2 + half, 0:HALF], LN_EPS, shift[:, cols],
                                              ALU.add, ALU.subtract).then_inc(lvar_in, 1)
                for half in range(2):
                    cols = slice(half * HALF, (half + 1) * HALF)
                    dve.wait_ge(lstd_in, l * 4 + 2 * x + half + 1)
                    ins = vec_.reciprocal(inv[:, cols], var[:, cols])
                link(ins)
                for bank in (2, 3):
                    dve.sem_inc(side_free[bank], 1)
                g, b = ((V_LG1, V_LB1), (V_LG2, V_LB2))[x]

                def low(k):
                    dve.wait_ge(xh_in, l * 16 + 8 * x + k + 1)
                    vec_.scalar_tensor_tensor(x_lo[:, k, :], r[:, k, :], vcol(b + k), x_hi[:, k, :].bitcast(F32),
                                              ALU.add, ALU.subtract).then_inc(x_ready, 1)

                for k in range(KT):
                    dve.wait_ge(centred, l * 16 + 8 * x + k + 1)
                    vec_.scalar_tensor_tensor(r[:, k, :], r[:, k, :], vcol(g + k), inv[:, :], ALU.mult,
                                              ALU.mult).then_inc(y1_ready, 1)
                    if k:
                        low(k - 1)
                low(KT - 1)

            norm(0)

            base = steps[0]

            def group(g, first_step, last):
                n = [0]

                def glink(ins):
                    n[0] += 1
                    ins.then_inc(dve_step, 1)
                    dve.wait_ge(dve_step, first_step + n[0])

                for i in range(8):
                    dve.wait_ge(relu_in, l * 32 + g * 8 + i + 1)
                    t = relu[:, i % 2, :]
                    glink(vec_.tensor_tensor(t, t, t, ALU.mult))
                    glink(vec_.tensor_copy(b_hi[:, i, :], t))
                    vec_.tensor_tensor(b_lo[:, i, :], t, b_hi[:, i, :].bitcast(F32), ALU.subtract).then_inc(hid_ready, 1)
                dve.wait_ge(r_ready, l * 8 + 8)
                for m in range(KT):
                    if last:
                        less_shift(m, glink)
                    tile_is_done(dve, l, g * 16 + T_FF + 8 + m)
                    vec_.tensor_tensor(halves(r[:, m, :]), halves(r[:, m, :]), pair(m % 2), ALU.add).then_inc(pair_free[m % 2], 1)
                    if last:
                        dve.wait_ge(pair_free[m % 2], l * (TILES // 2) + g * 8 + (T_FF + 8 + m) // 2 + 2)
                        statistics(1, m, glink)
                return n[0]

            with dve.Fori(0, 3) as g:
                per = group(g, g * 16 + base, False)
                assert per == 16
            n_last = group(3, base + 3 * per, True)
            steps[0] = base + 3 * per + n_last
            norm(1)
            dve.wait_ge(x_ready, l * 16 + 24)

    block_cm.__exit__(None, None, None)


def state_loads(slot):
    return len(range(slot, NB, STATE_RING))


def kv_loads(slot):
    return len(range(slot, 2 * NB, KV_RING))


def shape_table():
    t = np.zeros((P, K_ALL), np.float32)
    pos = np.concatenate([np.tile(4096 + np.arange(TS), NB), np.arange(SEQ)]).astype(np.float32)
    inv = (10000.0 ** (-np.arange(64, dtype=np.float64) / 64)).astype(np.float32)
    ang = (pos[None, :] * inv[:, None]).astype(np.float32).astype(np.float64)
    t[:, K_COS:K_COS + N] = np.concatenate([np.cos(ang)] * 2)
    t[:, K_SIN:K_SIN + N] = np.concatenate([-np.sin(ang), np.sin(ang)])
    g = np.array(LOG_G)
    j, i = np.arange(P)[:, None, None], np.arange(P)[None, None, :]
    keep = np.where(i >= j, np.exp(np.maximum(i - j, 0) * g[None, :, None]), 0.0) * RET_SCALE
    t[:, K_DMP:K_DMP + H * P] = keep.reshape(P, -1)
    js, is_ = j[:NS], i[:, :, :NS]
    same = (js // TS == is_ // TS)
    t[:NS, K_DMS:K_DMS + H * NS] = (keep[:NS, :, :NS] * same).reshape(NS, -1)
    t[:, K_QDP:K_QDP + H * P] = np.exp((np.arange(P)[None] + 1.0) * g[:, None]).reshape(1, -1)
    t[:, K_QDS:K_QDS + H * NS] = np.exp((np.arange(NS)[None] % TS + 1.0) * g[:, None]).reshape(1, -1)
    t[:, K_KDP:K_KDP + H] = np.exp((CHUNK - 1.0 - np.arange(P))[:, None] * g[None]) * RET_SCALE
    kd = np.exp((TS - 1.0 - np.arange(NS) % TS)[:, None, None] * g[None, None]) * RET_SCALE
    own = (np.arange(NS)[:, None] // TS == np.arange(NB)[None])[:, :, None]
    t[:NS, K_KDS:K_KDS + H * NB] = (kd * own).reshape(NS, -1)
    t[:, K_ID:K_ID + P] = np.eye(P)
    t[:, K_MEAN:K_MEAN + P] = 1.0 / D
    return t


def kernel(**inputs):
    import concourse.bacc as bacc
    from concourse.bass_utils import run_bass_kernel_spmd

    a = {k: np.asarray(x) for k, x in inputs.items()}
    c = np.ascontiguousarray

    def columns(x):
        return x.reshape(DEPTH, -1, P).transpose(0, 2, 1)

    ins = {
        "xT": c(np.concatenate([a["x_sample"].reshape(NS, D), a["x_prompt"].reshape(SEQ, D)]).T),
        "memT": c(a["mem_prompt"].reshape(ML, D).T),
        "kT_cache": c(a["cache_mem_k"].transpose(0, 1, 4, 3, 2).reshape(DEPTH, NB, P, H * ML)),
        "v_cache": c(a["cache_mem_v"].reshape(DEPTH, NB, ML, CW)),
        "conv_state": c(a["state_conv"].reshape(DEPTH, NB, 2, 4, P).transpose(0, 4, 3, 1, 2).reshape(DEPTH, P, 64)),
        "ret_state": c(a["state_ret"]),
    }
    for w in ("w_in", "w_conv_out", "w_ret_out", "w_mem_out", "w_out", "w_mem_kv", "w_up", "w_down"):
        ins[w] = c(a[w])
    ins["vectors"] = c(np.concatenate(
        [columns(a["b_gate"]), columns(a["ret_gn_g"]), columns(a["conv_w"].reshape(DEPTH, -1)), columns(a["ln1_g"]),
         columns(a["ln1_b"]), columns(a["ln2_g"]), columns(a["ln2_b"])], axis=2))
    ins["table"] = shape_table()
    outs = {"yT": (D, N), "kT_new": (DEPTH, P, H, ML), "v_new": (DEPTH, ML, CW), "conv_new": (DEPTH, P, 72),
            "ret_prompt": (DEPTH, H, DK, DV), "ret_sample": (DEPTH, NB, H, DK, DV)}

    nc = bacc.Bacc("TRN2", target_bir_lowering=False, num_devices=1, dynamic_dma_scratch_size=1024)
    args = [nc.dram_tensor(f"in_{n}", x.shape, F32, kind="ExternalInput").ap() for n, x in ins.items()]
    args += [nc.dram_tensor(f"out_{n}", s, F32, kind="ExternalOutput").ap() for n, s in outs.items()]
    layers(nc, *args)
    res = run_bass_kernel_spmd(nc, [{f"in_{n}": x for n, x in ins.items()}], core_ids=[0]).results[0]
    o = {n: res[f"out_{n}"] for n in outs}
    y = o["yT"].T
    conv = o["conv_new"].reshape(DEPTH, P, 4, NB + 1, 2).transpose(0, 3, 4, 2, 1).reshape(DEPTH, NB + 1, 2, CW)
    return (c(y[NS:]).reshape(1, SEQ, D), c(y[:NS]).reshape(NB, TS, D),
            c(o["kT_new"].transpose(0, 3, 2, 1)).reshape(DEPTH, 1, ML, H, P),
            o["v_new"].reshape(DEPTH, 1, ML, H, P),
            c(conv[:, NB:]), o["ret_prompt"].reshape(DEPTH, 1, H, DK, DV),
            c(conv[:, :NB]), o["ret_sample"])
```
